# Optimizing a Trainium2 kernel written in Bass

```python
import jax, jax.numpy as jnp
from jax import lax
import numpy as np

D_MODEL = 1024
BATCH = 1
SEQ = 512
DEPTH = 2
DEC_BATCH = 8
DEC_SEQ = 8
PAST_LEN = 4096
PAGE_SIZE = 128

D_MIX = D_MODEL
D_LRU = D_MIX // 2
N_LRU_BLOCKS = 8
LRU_BLOCK = D_LRU // N_LRU_BLOCKS
CONV_W = 4
LRU_C = 8.0
D_GLA = D_MIX - D_LRU
GLA_HEADS = 4
GLA_DV = D_GLA // GLA_HEADS
GLA_DK = GLA_DV // 2
GLA_RANK = 16
GLA_NORMALIZER = 16.0
GLA_CHUNK = 64
D_FF = 2816
EPS = 1e-6
IN_WIDTHS = (D_LRU, D_LRU, GLA_HEADS * GLA_DK, GLA_HEADS * GLA_DK, D_GLA, D_GLA, GLA_RANK)
IN_SPLITS = tuple(int(s) for s in np.cumsum(IN_WIDTHS)[:-1])
D_IN = int(sum(IN_WIDTHS))

kernel_name = "hymba_rglru_gla_macaron_decode_step"

def rmsnorm(x, g):
    xf = x.astype(jnp.float32)
    y = xf * lax.rsqrt(jnp.mean(xf * xf, axis=-1, keepdims=True) + EPS)
    return (y * g.astype(jnp.float32)).astype(x.dtype)

def swiglu(h, w_gate, w_up, w_down):
    return (jax.nn.silu(h @ w_gate) * (h @ w_up)) @ w_down

def causal_conv(x, buf, w, b):
    T = x.shape[1]
    xp = jnp.concatenate([buf.astype(x.dtype), x], axis=1)
    out = sum(xp[:, j:j + T] * w[j] for j in range(CONV_W)) + b
    return out, xp[:, xp.shape[1] - (CONV_W - 1):]

def rg_lru(xc, h0, reset_first, wa, ba, wx, bx, lam):
    B, T, _ = xc.shape
    xf = xc.astype(jnp.float32)
    xb = xf.reshape(B, T, N_LRU_BLOCKS, LRU_BLOCK)
    r = jax.nn.sigmoid(jnp.einsum('btnd,nde->btne', xb, wa.astype(jnp.float32)).reshape(B, T, D_LRU) + ba)
    i = jax.nn.sigmoid(jnp.einsum('btnd,nde->btne', xb, wx.astype(jnp.float32)).reshape(B, T, D_LRU) + bx)
    log_a = -LRU_C * r * jax.nn.softplus(-lam.astype(jnp.float32))
    a = jnp.exp(log_a)
    mult = jnp.sqrt(-jnp.expm1(2.0 * log_a))
    if reset_first:
        mult = mult.at[:, 0].set(1.0)
    bterm = mult * i * xf
    bterm = bterm.at[:, 0].add(a[:, 0] * h0.astype(jnp.float32))

    def combine(left, right):
        a_l, b_l = left
        a_r, b_r = right
        return a_l * a_r, a_r * b_l + b_r

    _, h = lax.associative_scan(combine, (a, bterm), axis=1)
    return h, h[:, -1]

def gla_chunked(q, k, v, gk, S0):
    B, T = q.shape[0], q.shape[1]
    C = GLA_CHUNK if T % GLA_CHUNK == 0 else T
    n = T // C

    def to_chunks(z):
        return z.reshape(B, n, C, GLA_HEADS, z.shape[-1]).transpose(1, 0, 3, 2, 4)

    mask = jnp.tril(jnp.ones((C, C), dtype=bool))[:, :, None]

    def step(S, inp):
        qc, kc, vc, gc = inp
        bcum = jnp.cumsum(gc, axis=2)
        diff = bcum[:, :, :, None, :] - bcum[:, :, None, :, :]
        decay = jnp.exp(jnp.where(mask, diff, -jnp.inf))
        scores = jnp.einsum('bhtd,bhsd,bhtsd->bhts', qc, kc, decay)
        o = jnp.einsum('bhts,bhsv->bhtv', scores, vc) + jnp.einsum('bhtd,bhdv->bhtv', qc * jnp.exp(bcum), S)
        blast = bcum[:, :, -1:]
        S_new = jnp.exp(blast[:, :, 0])[..., None] * S + jnp.einsum('bhsd,bhsv->bhdv', kc * jnp.exp(blast - bcum), vc)
        return S_new, o

    S_fin, o = lax.scan(step, S0.astype(jnp.float32), (to_chunks(q), to_chunks(k), to_chunks(v), to_chunks(gk)))
    o = o.transpose(1, 0, 3, 2, 4).reshape(B, T, GLA_HEADS, GLA_DV)
    return o, S_fin

def mixer(h, st_h, st_conv, st_gla, reset_first, p):
    B, T, _ = h.shape
    proj = h @ p['w_in']
    xl, yl, q, k, v, g, gd = jnp.split(proj, IN_SPLITS, axis=-1)
    xc, new_conv = causal_conv(xl, st_conv, p['conv_w'], p['conv_b'])
    hl, h_last = rg_lru(xc, st_h, reset_first, p['lru_wa'], p['lru_ba'], p['lru_wx'], p['lru_bx'], p['lru_lambda'])
    lru_out = rmsnorm((hl * jax.nn.gelu(yl.astype(jnp.float32))).astype(h.dtype), p['lru_norm'])
    gk = jax.nn.log_sigmoid((gd @ p['gla_w_gate'] + p['gla_b_gate']).astype(jnp.float32)) / GLA_NORMALIZER
    qh = q.astype(jnp.float32).reshape(B, T, GLA_HEADS, GLA_DK) * (GLA_DK ** -0.5)
    kh = k.astype(jnp.float32).reshape(B, T, GLA_HEADS, GLA_DK)
    vh = v.astype(jnp.float32).reshape(B, T, GLA_HEADS, GLA_DV)
    o, S_fin = gla_chunked(qh, kh, vh, gk.reshape(B, T, GLA_HEADS, GLA_DK), st_gla)
    o = rmsnorm(o, p['gla_norm']).reshape(B, T, D_GLA)
    gla_out = (o * jax.nn.silu(g.astype(jnp.float32))).astype(h.dtype)
    out = jnp.concatenate([lru_out, gla_out], axis=-1) @ p['w_out']
    return out, h_last, new_conv, S_fin

def layer(x, st_h, st_conv, st_gla, reset_first, p):
    h = rmsnorm(x, p['norm_pre'][0])
    x = x + 0.5 * rmsnorm(swiglu(h, p['w_ffn_gate'][0], p['w_ffn_up'][0], p['w_ffn_down'][0]), p['norm_post'][0])
    h = rmsnorm(x, p['norm_pre'][1])
    m, h_last, new_conv, S_fin = mixer(h, st_h, st_conv, st_gla, reset_first, p)
    x = x + rmsnorm(m, p['norm_post'][1])
    h = rmsnorm(x, p['norm_pre'][2])
    x = x + 0.5 * rmsnorm(swiglu(h, p['w_ffn_gate'][1], p['w_ffn_up'][1], p['w_ffn_down'][1]), p['norm_post'][2])
    return x, h_last, new_conv, S_fin

def setup_inputs(seed: int = 0) -> dict:
    key = jax.random.key(seed)
    ks = jax.random.split(key, 24)
    f32 = jnp.float32
    nrm = lambda k, shape, s: (jax.random.normal(k, shape, f32) * s)
    a0 = jax.random.uniform(ks[15], (DEPTH, D_LRU), f32, 0.9, 0.999)
    return {
        'x_prompt': nrm(ks[0], (BATCH, SEQ, D_MODEL), 1.0),
        'x_sample': nrm(ks[1], (DEC_BATCH, DEC_SEQ, D_MODEL), 1.0),
        'state_lru_h': nrm(ks[2], (DEPTH, DEC_BATCH, D_LRU), 0.5),
        'state_lru_conv': nrm(ks[3], (DEPTH, DEC_BATCH, CONV_W - 1, D_LRU), 1.0),
        'state_gla': nrm(ks[4], (DEPTH, DEC_BATCH, GLA_HEADS, GLA_DK, GLA_DV), 0.5),
        'norm_pre': 1.0 + nrm(ks[5], (DEPTH, 3, D_MODEL), 0.05),
        'norm_post': 1.0 + nrm(ks[6], (DEPTH, 3, D_MODEL), 0.05),
        'w_ffn_gate': nrm(ks[7], (DEPTH, 2, D_MODEL, D_FF), D_MODEL ** -0.5),
        'w_ffn_up': nrm(ks[8], (DEPTH, 2, D_MODEL, D_FF), D_MODEL ** -0.5),
        'w_ffn_down': nrm(ks[9], (DEPTH, 2, D_FF, D_MODEL), D_FF ** -0.5),
        'w_in': nrm(ks[10], (DEPTH, D_MODEL, D_IN), D_MODEL ** -0.5),
        'conv_w': nrm(ks[11], (DEPTH, CONV_W, D_LRU), CONV_W ** -0.5),
        'conv_b': nrm(ks[12], (DEPTH, D_LRU), 0.01),
        'lru_wa': nrm(ks[13], (DEPTH, N_LRU_BLOCKS, LRU_BLOCK, LRU_BLOCK), LRU_BLOCK ** -0.5),
        'lru_ba': nrm(ks[14], (DEPTH, D_LRU), 0.01),
        'lru_wx': nrm(ks[16], (DEPTH, N_LRU_BLOCKS, LRU_BLOCK, LRU_BLOCK), LRU_BLOCK ** -0.5),
        'lru_bx': nrm(ks[17], (DEPTH, D_LRU), 0.01),
        'lru_lambda': jnp.log(a0) - jnp.log1p(-a0),
        'lru_norm': 1.0 + nrm(ks[18], (DEPTH, D_LRU), 0.05),
        'gla_w_gate': nrm(ks[19], (DEPTH, GLA_RANK, GLA_HEADS * GLA_DK), GLA_RANK ** -0.5),
        'gla_b_gate': nrm(ks[20], (DEPTH, GLA_HEADS * GLA_DK), 0.01),
        'gla_norm': 1.0 + nrm(ks[21], (DEPTH, GLA_DV), 0.05),
        'w_out': nrm(ks[22], (DEPTH, D_MIX, D_MODEL), D_MIX ** -0.5),
    }

def reference(x_prompt, x_sample, state_lru_h, state_lru_conv, state_gla,
              norm_pre, norm_post, w_ffn_gate, w_ffn_up, w_ffn_down, w_in,
              conv_w, conv_b, lru_wa, lru_ba, lru_wx, lru_bx, lru_lambda, lru_norm,
              gla_w_gate, gla_b_gate, gla_norm, w_out):
    B = x_prompt.shape[0]
    yp, ys = x_prompt, x_sample
    hp_list, cp_list, sp_list = [], [], []
    hs_list, cs_list, ss_list = [], [], []
    for l in range(DEPTH):
        p = {
            'norm_pre': norm_pre[l], 'norm_post': norm_post[l],
            'w_ffn_gate': w_ffn_gate[l], 'w_ffn_up': w_ffn_up[l], 'w_ffn_down': w_ffn_down[l],
            'w_in': w_in[l], 'conv_w': conv_w[l], 'conv_b': conv_b[l],
            'lru_wa': lru_wa[l], 'lru_ba': lru_ba[l], 'lru_wx': lru_wx[l], 'lru_bx': lru_bx[l],
            'lru_lambda': lru_lambda[l], 'lru_norm': lru_norm[l],
            'gla_w_gate': gla_w_gate[l], 'gla_b_gate': gla_b_gate[l], 'gla_norm': gla_norm[l],
            'w_out': w_out[l],
        }
        zero_h = jnp.zeros((B, D_LRU), jnp.float32)
        zero_conv = jnp.zeros((B, CONV_W - 1, D_LRU), x_prompt.dtype)
        zero_gla = jnp.zeros((B, GLA_HEADS, GLA_DK, GLA_DV), jnp.float32)
        yp, hp, cp, sp = layer(yp, zero_h, zero_conv, zero_gla, True, p)
        ys, hs, cs, ss = layer(ys, state_lru_h[l], state_lru_conv[l], state_gla[l], False, p)
        hp_list.append(hp); cp_list.append(cp); sp_list.append(sp)
        hs_list.append(hs); cs_list.append(cs); ss_list.append(ss)
    new_lru_h_prompt = jnp.stack(hp_list, axis=0)
    new_lru_conv_prompt = jnp.stack(cp_list, axis=0)
    new_gla_prompt = jnp.stack(sp_list, axis=0)
    new_lru_h_sample = jnp.stack(hs_list, axis=0)
    new_lru_conv_sample = jnp.stack(cs_list, axis=0)
    new_gla_sample = jnp.stack(ss_list, axis=0)
    return (yp, ys, new_lru_h_prompt, new_lru_conv_prompt, new_gla_prompt,
            new_lru_h_sample, new_lru_conv_sample, new_gla_sample)


_drawn_inputs = setup_inputs


def setup_inputs(seed=0):
    import zlib

    import numpy as np

    out = dict(_drawn_inputs(seed))
    spreads = {}
    factors = {'lru_ba': 21.501, 'lru_bx': 8.0, 'gla_b_gate': 8.0}
    for name, (base, spread) in spreads.items():
        noise = np.random.default_rng([zlib.crc32(name.encode()), seed]).standard_normal(out[name].shape)
        drawn = base * np.exp(spread * noise) if base else spread * noise
        out[name] = __import__('jax').numpy.asarray(drawn.astype(out[name].dtype))
    for name, factor in factors.items():
        out[name] = (out[name] * factor).astype(out[name].dtype)
    return out
```

```python
from contextlib import ExitStack, contextmanager

import concourse.bass as bass
from concourse import mybir

F32 = mybir.dt.float32
F32R = mybir.dt.float32r
U8 = mybir.dt.uint8
ALU = mybir.AluOpType
ACT = mybir.ActivationFunctionType

P = 128
D = 1024
DT = D // P
L = 2
SEQ = 512
NB, NS = 8, 8
NT = SEQ + NB * NS
H = NT // 2
FF = 2816
FT = FF // P
CH = 2
FC = FT // CH
DL = 512
LT = DL // P
CW = 4
XP = SEQ + CW - 1
XS = NS + CW - 1
XA = XP + NB * XS
HEADS = 4
DK, DV = 64, 128
PR = 2
RANK = 16
C = 128
NC_ = SEQ // C
LEVELS = [4, 8, 16, 32, 64]
EPS = 1e-6
TC = 96
NTC = NT // TC
NSL = 4 + len(LEVELS)
LRU_C, NORMALIZER = 8.0, 16.0
GK_MIN = -40.0
TINY = 1e-18

PRE, POST, CONVW, CONVB, BA, BX, LAM, LNORM, GB, GNORM, NPAR = 0, 24, 48, 64, 68, 72, 76, 80, 84, 86, 87
O_CP, O_CS, O_HP, O_HS, NST = 0, 3, 27, 28, 36
V_XC, V_D, V_ONE, V_B, V_AH, V_BS, V_A0, V_H, V_O = 4, 5, 6, 7, 8, 9, 10, 11, 12
A_R, A_I, A_TAU, A_AA, A_L1, A_L2, A_M, A_GE = range(1, 9)
P_HEAD, P_IX, P_ST = 1, 2, 3
G_D, G_SG, G_KF, G_SC, G_S, G_KEM, G_S1, G_S2 = 1, 2, 3, 4, 5, 5, 6, 7
A_VC, A_VT, A_N, A_E, A_KET, A_O = range(1, 7)
P_QF = 1
T_VT, T_KE, T_SA, T_SB, T_O, T_SU = range(1, 7)


class Tally:

    def __init__(self, small_step=None):
        self.small_step, self.count, self.open, self.pauses = small_step, {}, [], 0

    def pause(self):
        if self.small_step:
            self.small_step(self.pauses)
            self.pauses += 1

    def now(self, sem, more=0):
        v = self.count.get(sem.name, 0) + more
        for reg, rises in self.open:
            if rises.get(sem.name, 0):
                v = reg * rises[sem.name] + v
        return v

    def up(self, sem, k=1):
        self.count[sem.name] = self.count.get(sem.name, 0) + k
        return self.now(sem)

    @contextmanager
    def loop(self, eng, times, rises):
        if self.open:
            self.pause()
        before = dict(self.count)
        with eng.Fori(0, times) as i:
            self.open.append((i, rises))
            yield i
            self.open.pop()
        rise = {k: v - before.get(k, 0) for k, v in self.count.items() if v != before.get(k, 0)}
        assert all(rises.get(k) == v for k, v in rise.items()), f"a loop raises {rise}, said {rises}"
        for k, v in rise.items():
            self.count[k] = before.get(k, 0) + v * times


PAIR = {f"{k}{s}": 1 for k in ("lo_ready", "hi_ready", "unit_done", "out_taken") for s in (0, 1)}
PAIR |= {"raw_landed0": 16, "raw_landed1": 16}
HIDDEN = PAIR | {"silu_ready": 1, "silur_ready": 1, "hidh_ready": 1, "hidl_ready": 1}
SQUARED = PAIR | {"sq_ready": 2, "sq_used": 2}
TILES = {"x_ready": 2, "xpart": 2, "hh_ready": 2, "hl_ready": 2, "sq_ready": 2, "sq_used": 2}
LRU_TILE = PAIR | {"gates_landed": 16, "lru_v": 12, "lru_a": 8, "lru_p": 3, "lru_t": 1, "sq_ready": 1, "sq_used": 1}
CHUNK = {"gla_v": 5, "gla_a": 6, "gla_p": 1, "gla_t": 6, "placed": 5}
SAMPLE = {"gla_v": 7, "gla_a": 6, "gla_p": 1, "gla_t": 6, "placed": 1}
UNITS = 2 * (FT * 2 + CH * DT) + 20 + DT
LAYER = {f"{k}{s}": UNITS // 2 for k in ("lo_ready", "hi_ready", "unit_done") for s in (0, 1)}
LAYER |= {"out_taken0": UNITS // 2, "out_taken1": UNITS // 2 + 1, "raw_landed0": 8 * UNITS, "raw_landed1": 8 * UNITS}
LAYER |= {k: LT * LRU_TILE[k] for k in ("gates_landed", "lru_v", "lru_a", "lru_p", "lru_t")}
LAYER |= {k: NC_ * CHUNK[k] + SAMPLE[k] for k in CHUNK}
LAYER |= {"x_ready": 3 * DT, "xpart": 3 * DT, "hh_ready": 4 * DT, "hl_ready": 4 * DT}
LAYER |= {"sq_ready": 6 * DT + LT, "sq_used": 6 * DT + LT, "ssum_zero": 4, "small_landed": 32}
LAYER |= {"cols_ready": 3, "std_ready": 7, "inv_ready": 7, "diag_ready": 6, "bcast_ready": 6, "rstd_ready": 3}
LAYER |= {"silu_ready": 2 * FT, "silur_ready": 2 * FT, "hidh_ready": 2 * FT, "hidl_ready": 2 * FT}
LAYER |= {"gdh_ready": 1, "gdl_ready": 1, "gdp_ready": 1, "logit_ready": 1, "gk_v": 4, "gk_a": 3}
LAYER |= {"s_zero": 1, "odd_out": 1, "s0_landed": 16, "s_stored": 32, "head_sq": 1, "mix_cols": 1, "mix_t": 5, "mix_d": 5, "mix_v": 16}
SQ_BEFORE_S0 = 3 * DT + LT


def halves(ap):
    return ap.rearrange("p (a n) -> p a n", a=2)


def build(nc, a):
    ctx = ExitStack()
    with ctx:
        program(nc, a, ctx)


def program(nc, a, ctx):
    cursor = [(nc.sbuf_base + 31) // 32 * 32]

    def sb(name, shape, dt=F32):
        size = 1 if dt == U8 else 4
        for n in shape[1:]:
            size *= n
        t = nc.alloc_sbuf_tensor_at(name, shape, dt, offset=cursor[0])
        cursor[0] += (size + 31) // 32 * 32
        assert cursor[0] <= nc.sbuf_usable_end, (name, cursor[0])
        return t

    xT = sb("xT", [P, DT, NT])
    operand_at = cursor[0]
    hh = sb("hh", [P, DT, NT], F32R)
    hl = sb("hl", [P, DT, NT], F32R)
    raw = [sb(f"raw{s}", [P, FC * P]) for s in (0, 1)]
    wh = [sb(f"wh{s}", [P, FC * P], F32R) for s in (0, 1)]
    wl = [sb(f"wl{s}", [P, FC * P], F32R) for s in (0, 1)]
    par = sb("par", [P, L * NPAR])
    ph = sb("ph", [P, L * 24])
    sp8 = sb("sp8", [P, L * LT])
    nsp8 = sb("nsp8", [P, L * LT])
    spt = sb("spt", [P, 6, L * LT])
    ones = sb("ones", [P, P])
    means = sb("means", [P, 3])
    spare = sb("spare", [P, 64])
    epsc = sb("epsc", [P, 1])
    tinyc = sb("tinyc", [P, 1])
    rstd = sb("rstd", [P, NT])
    ident = sb("ident", [P, P])
    dcol = sb("dcol", [P, 5 * NTC])
    dinv = sb("dinv", [P, 5 * NTC])
    diag = [sb(f"diag{s}", [P, NTC, TC]) for s in (0, 1)]
    ssum = sb("ssum", [P, NT])
    sq = [sb(f"sq{s}", [P, NT]) for s in (0, 1)]
    tmp = [sb(f"tmp{s}", [P, NT]) for s in (0, 1)]
    state_out = sb("state_out", [P, L * LT, NST])
    sth = sb("sth", [P, L * LT, NB])
    stc = sb("stc", [P, L * LT, NB, CW - 1])
    wgd = sb("wgd", [P, DT * RANK])
    wgdh = sb("wgdh", [P, DT * RANK], F32R)
    wgdl = sb("wgdl", [P, DT * RANK], F32R)
    wg2 = sb("wg2", [RANK, PR * P])
    gates = sb("gates", [P, 2 * P])
    masks = sb("masks", [P, 6, C], U8)
    sign = sb("sign", [P, len(LEVELS), C])
    seqmask = sb("seqmask", [NB * NS, NB])
    cont = sb("cont", [P, NT])
    sc = sb("sc", [P, HEADS, C])
    scs = sb("scs", [NB * NS, HEADS, NB * NS])
    S = sb("S", [P, PR, DV])
    result_at = cursor[0]
    yT = sb("yT", [P, DT, NT])
    shared_at = cursor[0]
    hidh = sb("hidh", [P, FC, NT], F32R)
    hidl = sb("hidl", [P, FC, NT], F32R)
    gate = sb("gate", [P, NT])
    act = sb("act", [P, NT])
    actr = sb("actr", [P, NT])
    hid = sb("hid", [P, NT])
    cursor[0] = shared_at
    qk = sb("qk", [P, 2 * PR, NT])
    bc = sb("bc", [P, PR, NT])
    vT = sb("vT", [P, HEADS, NT])
    gT = sb("gT", [P, HEADS, NT])
    oT = sb("oT", [P, HEADS, NT])
    lruo = sb("lruo", [P, LT, NT])
    gd = sb("gd", [RANK, NT])
    xlp = sb("xlp", [P, XA])
    l1 = sb("l1", [P, NT])
    l2 = sb("l2", [P, NT])
    cursor[0] = result_at
    cv = [sb(f"cv{s}", [P, XA - CW + 1]) for s in (0, 1)]
    xc = sb("xc", [P, NT])
    rg = sb("rg", [P, NT])
    ig = sb("ig", [P, NT])
    tau = sb("tau", [P, NT])
    aa = sb("aa", [P, NT])
    assert cursor[0] <= shared_at
    cursor[0] = result_at
    S0 = sb("S0", [P, NB, PR, DV])
    kem = sb("kem", [NB * NS, NB, PR * P])
    assert cursor[0] <= shared_at
    cursor[0] = operand_at
    dec = sb("dec", [P, PR, NSL, C])
    qf = sb("qf", [P, PR, NSL - 2, C])
    kf = sb("kf", [P, PR, NSL - 2, C])
    vc = sb("vc", [P, HEADS, C])
    vt = sb("vt", [P, HEADS * DV])
    ket = sb("ket", [P, PR * P])
    assert cursor[0] <= operand_at + 2 * DT * NT * 4
    maskf = qk[:, :, :].rearrange("p a n -> p (a n)")[:, 0:6 * C].rearrange("p (v n) -> p v n", v=6)
    xls = xlp[:, XP:XA].rearrange("p (b t) -> p b t", t=XS)

    psU = ctx.enter_context(nc.psum_tensor("psU", [P, 4, 512], F32))
    psM = ctx.enter_context(nc.psum_tensor("psM", [P, 4, 512], F32))

    def sem(name):
        return ctx.enter_context(nc.semaphore(name))

    x_landed = [sem(f"x_landed{m}") for m in range(DT)]
    const_landed = sem("const_landed")
    raw_landed, hi_ready, lo_ready, unit_done, out_taken = (
        [sem(f"{k}{s}") for s in (0, 1)] for k in ("raw_landed", "hi_ready", "lo_ready", "unit_done", "out_taken"))
    small_landed = sem("small_landed")
    gates_landed = sem("gates_landed")
    setup_v, setup_a, setup_p = sem("setup_v"), sem("setup_a"), sem("setup_p")
    x_ready = sem("x_ready")
    xpart = sem("xpart")
    hh_ready, hl_ready = sem("hh_ready"), sem("hl_ready")
    sq_ready, sq_used = sem("sq_ready"), sem("sq_used")
    ssum_zero = sem("ssum_zero")
    cols_ready, std_ready, inv_ready, diag_ready, bcast_ready, rstd_ready = (
        sem(k) for k in ("cols_ready", "std_ready", "inv_ready", "diag_ready", "bcast_ready", "rstd_ready"))
    silu_ready, silur_ready = sem("silu_ready"), sem("silur_ready")
    hidh_ready, hidl_ready = sem("hidh_ready"), sem("hidl_ready")
    gdh_ready, gdl_ready, gdp_ready, logit_ready = (sem(k) for k in ("gdh_ready", "gdl_ready", "gdp_ready", "logit_ready"))
    lru_v, lru_a, lru_p, lru_t = (sem(f"lru_{k}") for k in "vapt")
    gk_v, gk_a = sem("gk_v"), sem("gk_a")
    gla_v, gla_a, gla_p, gla_t = (sem(f"gla_{k}") for k in "vapt")
    odd_out = sem("odd_out")
    placed = sem("placed")
    s_zero, s0_landed, s_stored = sem("s_zero"), sem("s0_landed"), sem("s_stored")
    head_sq, mix_cols, mix_t, mix_d, mix_v = (sem(k) for k in ("head_sq", "mix_cols", "mix_t", "mix_d", "mix_v"))
    y_stored = sem("y_stored")

    block = ctx.enter_context(nc.Block())

    def tile(t, m):
        return t[:, m, :] if isinstance(m, int) else t[:, bass.ds(m, 1), :].rearrange("p o n -> p (o n)")

    def col(t, k):
        return t[:, bass.ds(k, 1)]

    def dram(t, k):
        return t[bass.ds(k, 1), :, :].rearrange("o p n -> (o p) n")

    @block.sync
    def _(e):
        n = Tally()

        def load(s, width, src):
            e.wait_ge(lo_ready[s], n.now(lo_ready[s]))
            n.up(lo_ready[s])
            e.dma_start(raw[s][:, 0:width], src).then_inc(raw_landed[s], 16)

        def pairs(times, width, src, first):
            with n.loop(e, times, PAIR) as j:
                for s in (0, 1):
                    load(s, width, dram(src, first + j * 2 + s))

        def ffn(l, f):
            for c in range(CH):
                pairs(FC, D, a["w_gu"], (l * 2 + f) * (CH * FC * 2) + c * FC * 2)
                pairs(DT // 2, FC * P, a["w_d"], (l * 2 + f) * (CH * DT) + c * DT)

        for m in range(DT):
            e.dma_start(yT[:, m, :], a["xT"][:, m, :]).then_inc(x_landed[m], 16)
        for t, src in ((par, "par"), (sth, "st_h"), (stc, "st_conv"), (ident, "ident"), (maskf, "masks"), (sign, "sign"),
                       (seqmask, "seqmask"), (cont, "cont")):
            e.dma_start(maskf if t is maskf else t[:], a[src]).then_inc(const_landed, 16)

        with n.loop(e, L, LAYER) as l:
            ffn(l, 0)
            e.wait_ge(logit_ready, n.now(logit_ready))
            n.up(logit_ready)
            e.dma_start(wgd[:, :], dram(a["w_gd"], l)).then_inc(small_landed, 16)
            e.dma_start(wg2[:, :], dram(a["w_g2"], l)).then_inc(small_landed, 16)
            with n.loop(e, LT, LRU_TILE) as i:
                e.wait_ge(lru_t, n.now(lru_t))
                n.up(lru_t)
                e.dma_start(gates[:, :], dram(a["w_ax"], l * LT + i)).then_inc(gates_landed, 16)
                for s in (0, 1):
                    load(s, D, dram(a["w_in"], l * 20 + i * 2 + s))
            pairs(6, D, a["w_in"], l * 20 + 2 * LT)
            e.wait_ge(lru_v, n.up(lru_v, LT * LRU_TILE["lru_v"]))
            e.wait_ge(lru_p, n.up(lru_p, LT * LRU_TILE["lru_p"]))
            e.wait_ge(sq_used, n.up(sq_used, SQ_BEFORE_S0))
            e.dma_start(S0[:, :, :, :], a["st_gla"][bass.ds(l, 1), :, :, :, :].rearrange("o p b r v -> (o p) b r v")).then_inc(s0_landed, 16)
            for s in (0, 1):
                load(s, D, dram(a["w_out"], l * DT + s))
            e.wait_ge(gla_v, n.up(gla_v, NC_ * CHUNK["gla_v"]))
            e.dma_start(a["gla_p"][bass.ds(l, 1), :, :, :].rearrange("o p r v -> (o p) r v"), S[:, :, :]).then_inc(s_stored, 16)
            e.wait_ge(gla_v, n.up(gla_v, SAMPLE["gla_v"]))
            e.dma_start(a["gla_s"][bass.ds(l, 1), :, :, :, :].rearrange("o p b r v -> (o p) b r v"), S0[:, :, :, :]).then_inc(s_stored, 16)
            n.up(sq_used, LAYER["sq_used"] - SQ_BEFORE_S0)
            pairs(DT // 2 - 1, D, a["w_out"], l * DT + 2)
            ffn(l, 1)
        for m in range(DT):
            e.wait_ge(x_ready, DT * 3 * L + m + 1)
            e.dma_start(a["yT"][:, m, :], xT[:, m, :]).then_inc(y_stored, 16)
        e.dma_start(a["states"], state_out[:, :, :]).then_inc(y_stored, 16)
        e.wait_ge(y_stored, 16 * (DT + 1))
        e.wait_ge(s_stored, 32 * L)

    @block.tensor
    def _(e):
        n = Tally(lambda k: e.matmul(psM[:, 3, 511:512], ones[:, :], means[:, 0:1], start=True, stop=True))

        def product(out, KT, w_h, w_l, M, xh, xl, ready=(), after=None):
            for kt in range(KT):
                for r in ready:
                    e.wait_ge(r, n.up(r))
                for part, (w, x) in enumerate([(w_h, xh), (w_h, xl), (w_l, xh)]):
                    for h in (0, 1):
                        mm = e.matmul(out[h], w[:, kt * M:(kt + 1) * M], x[:, kt, h * H:(h + 1) * H],
                                      start=(kt == 0 and part == 0), stop=(kt == KT - 1 and part == 2))
                if after is not None and kt < KT - 1:
                    after(kt)
            return mm

        def unit(s, KT, xh, xl, ready=(), after=None):
            e.wait_ge(lo_ready[s], n.up(lo_ready[s]))
            e.wait_ge(out_taken[s], n.now(out_taken[s]))
            n.up(out_taken[s]), n.up(unit_done[s])
            product([psU[:, 2 * s + h, 0:H] for h in (0, 1)], KT, wh[s], wl[s], P, xh, xl, ready, after)\
                .then_inc(unit_done[s], 1)
            if after is not None:
                after(KT - 1)

        def pair(KT, xh, xl, ready=()):
            unit(0, KT, xh, xl, ready)
            unit(1, KT, xh, xl)

        def columns(src, k, at, first, last):
            for t in range(NTC):
                mm = e.matmul(psM[0:TC, 0, at + t:at + t + 1], src[:, t * TC:(t + 1) * TC], means[:, k:k + 1],
                              start=(first and t == 0), stop=last, skip_group_check=True)
            return mm

        def spread():
            e.wait_ge(diag_ready, n.up(diag_ready))
            for h in (0, 1):
                mm = e.matmul(psM[:, 1 + h, 0:H], ones[0:TC, :], diag[0][0:TC, 3 * h:3 * h + 3, :], start=True, stop=True)
            mm.then_inc(bcast_ready, 1)

        def pre_columns(kt):
            e.wait_ge(sq_ready, n.up(sq_ready))
            n.up(sq_used)
            columns(sq[kt % 2], 0, 0, kt == 0, kt == DT - 1).then_inc(sq_used, 1)

        def post_norm():
            e.wait_ge(sq_used, n.up(sq_used, DT))
            n.up(sq_ready, DT)
            columns(ssum, 0, 0, True, True).then_inc(cols_ready, 1)
            spread()

        def ffn():
            for c in range(CH):
                if c == 0:
                    unit(0, DT, hh, hl, (hh_ready, hl_ready), pre_columns)
                    unit(1, DT, hh, hl, after=lambda kt: spread() if kt == 5 else None)
                with n.loop(e, FC - (c == 0), PAIR):
                    pair(DT, hh, hl)
                pair(FC, hidh, hidl, (hidl_ready,))
                with n.loop(e, DT // 2 - 1, PAIR):
                    pair(FC, hidh, hidl)
            post_norm()

        def chunk(T, nl, sample=False):
            up = CHUNK if not sample else SAMPLE
            e.wait_ge(gla_v, n.now(gla_v))
            e.wait_ge(gla_a, n.now(gla_a, A_VC))
            for h in range(HEADS):
                mm = e.transpose(psM[:, 0, h * DV:(h + 1) * DV], vc[:, h, :], ident[:, :])
            mm.then_inc(gla_t, 1)
            e.wait_ge(gla_v, n.now(gla_v, G_KF))
            for pr in range(PR):
                mm = e.transpose(psM[:, 1, pr * P:(pr + 1) * P], kf[:, pr, nl + 1, :], ident[:, :])
            mm.then_inc(gla_t, 1)
            e.wait_ge(gla_p, n.now(gla_p, P_QF))
            narrow = LEVELS[:min(nl, 4)]
            for odd in (0, 1):
                rows = slice(DK * odd, DK * odd + DK)
                for pr in range(PR):
                    for v, m in enumerate(narrow):
                        q = qf[rows, pr, 2 + v, 0:T].rearrange("p (b m) -> p b m", m=2 * m)[:, :, m:2 * m]
                        mm = e.matmul(psM[:, 2 + odd, pr * 256 + v * (T // 2):pr * 256 + (v + 1) * (T // 2)],
                                      kf[rows, pr, v, :], q, start=(pr == 0 and v == 0), stop=True, skip_group_check=True)
            mm.then_inc(gla_t, 1)
            e.wait_ge(gla_a, n.now(gla_a, A_KET))
            for odd in (0, 1):
                rows = slice(DK * odd, DK * odd + DK)
                for pr in range(PR):
                    mm = e.matmul(psM[:, odd, pr * 256:pr * 256 + T], kf[rows, pr, nl, :], qf[rows, pr, 1, 0:T],
                                  start=(pr == 0), stop=True, skip_group_check=True)
                    if nl == 5:
                        mm = e.matmul(psM[:, odd, pr * 256 + T:pr * 256 + T + T // 2], kf[rows, pr, 4, :],
                                      qf[rows, pr, 6, T // 2:T], start=False, stop=True, skip_group_check=True)
            mm.then_inc(gla_t, 1)
            e.wait_ge(gla_v, n.now(gla_v, G_SC))
            if sample:
                e.wait_ge(s0_landed, n.up(s0_landed, 16))
            for odd in (1, 0):
                for pr in range(PR):
                    h = 2 * pr + odd
                    mm = e.matmul(psM[:, 2 + odd, pr * C:pr * C + T], vt[0:T, h * DV:(h + 1) * DV],
                                  (scs if sample else sc)[0:T, 2 * odd + pr, 0:T], start=(pr == 0), stop=False, skip_group_check=True)
                if odd and sample:
                    mm.then_inc(odd_out, 1)
            for odd in (0, 1):
                rows = slice(DK * odd, DK * odd + DK)
                if odd and sample:
                    e.wait_ge(odd_out, n.up(odd_out))
                for pr in range(PR):
                    if not sample:
                        mm = e.matmul(psM[:, 2 + odd, pr * C:pr * C + T], S[rows, pr, :], qf[rows, pr, 0, 0:T],
                                      start=False, stop=True, skip_group_check=True)
                    else:
                        for b in range(NB):
                            mm = e.matmul(psM[:, 2 + odd, pr * C + b * NS:pr * C + (b + 1) * NS], S0[rows, b, pr, :],
                                          qf[rows, pr, 0, b * NS:(b + 1) * NS], start=False, stop=True, skip_group_check=True)
            mm.then_inc(gla_t, 1)
            if not sample:
                for h in range(HEADS):
                    rows = slice(DK * (h % 2), DK * (h % 2) + DK)
                    mm = e.matmul(psM[rows, 0, (h // 2) * DV:(h // 2 + 1) * DV], ket[0:T, h * DK:(h + 1) * DK],
                                  vt[0:T, h * DV:(h + 1) * DV], start=(h < 2), stop=True, skip_group_check=True)
            else:
                e.wait_ge(gla_a, n.now(gla_a, A_O))
                e.wait_ge(gla_v, n.now(gla_v, G_KEM))
                n.pause()
                for b in range(NB):
                    for h in range(HEADS):
                        rows = slice(DK * (h % 2), DK * (h % 2) + DK)
                        at = (b * PR + h // 2) * DV
                        mm = e.matmul(psM[rows, at // 512, at % 512:at % 512 + DV], kem[:, b, h * DK:(h + 1) * DK],
                                      vt[0:T, h * DV:(h + 1) * DV], start=(at % 512 == 0), stop=True, skip_group_check=True)
            mm.then_inc(gla_t, 1)
            n.up(gla_t, up["gla_t"]), n.up(gla_v, up["gla_v"]), n.up(gla_a, up["gla_a"]), n.up(gla_p, up["gla_p"])

        def mixer():
            e.wait_ge(gdl_ready, n.up(gdl_ready))
            e.wait_ge(out_taken[1], n.now(out_taken[1]))
            n.up(out_taken[1])
            product([psU[0:RANK, 2 + h, 0:H] for h in (0, 1)], DT, wgdh, wgdl, RANK, hh, hl, (hh_ready, hl_ready), pre_columns)\
                .then_inc(gdp_ready, 1)
            pre_columns(DT - 1)
            spread()
            with n.loop(e, LT, LRU_TILE):
                pair(DT, hh, hl)
                e.wait_ge(gates_landed, n.up(gates_landed, 16))
                e.wait_ge(lru_v, n.now(lru_v, V_XC))
                e.wait_ge(lru_a, n.now(lru_a))
                n.up(lru_v, LRU_TILE["lru_v"]), n.up(lru_a, LRU_TILE["lru_a"]), n.up(lru_t)
                for g in (0, 1):
                    for h in (0, 1):
                        mm = e.matmul(psM[:, 2 * g + h, 0:H], gates[:, g * P:(g + 1) * P], xc[:, h * H:(h + 1) * H],
                                      start=True, stop=True)
                mm.then_inc(lru_t, 1)
            e.wait_ge(lru_a, n.now(lru_a))
            for pr in range(PR):
                for h in (0, 1):
                    mm = e.matmul(psM[:, 2 * pr + h, 0:H], wg2[:, pr * P:(pr + 1) * P], gd[:, h * H:(h + 1) * H],
                                  start=True, stop=True)
            mm.then_inc(logit_ready, 1)
            with n.loop(e, 6, PAIR):
                pair(DT, hh, hl)
            e.wait_ge(gk_v, n.up(gk_v, 4))
            with n.loop(e, NC_, CHUNK):
                chunk(C, 5)
            chunk(NB * NS, 1, sample=True)
            e.wait_ge(gla_v, n.now(gla_v))
            e.wait_ge(sq_used, n.up(sq_used, LT))
            n.up(sq_ready, LT)
            columns(ssum, 1, 0, True, True)
            e.wait_ge(head_sq, n.up(head_sq))
            for h in range(HEADS):
                mm = columns(vT[:, h, :], 2, (1 + h) * NTC, False, True)
            mm.then_inc(mix_cols, 1)
            for g in range(5):
                e.wait_ge(mix_d, n.up(mix_d))
                for h in (0, 1):
                    mm = e.matmul(psM[:, 2 * (g % 2) + h, 0:H], ones[0:TC, :], diag[g % 2][0:TC, 3 * h:3 * h + 3, :],
                                  start=True, stop=True)
                mm.then_inc(mix_t, 1)
            pair(DT, hh, hl, (hh_ready, hl_ready))
            with n.loop(e, DT // 2 - 1, PAIR):
                pair(DT, hh, hl)
            post_norm()

        e.wait_ge(setup_p, 1)
        e.wait_ge(const_landed, 16 * 8)
        with n.loop(e, L, LAYER):
            ffn()
            mixer()
            ffn()

    @block.scalar
    def _(e):
        n = Tally(lambda k: e.activation(spare[0:1, k:k + 1], ones[0:1, 0:1], ACT.Copy))

        def split_hi(s, width):
            if width:
                e.wait_ge(raw_landed[s], n.up(raw_landed[s], 16))
                e.wait_ge(unit_done[s], n.now(unit_done[s]))
                e.activation(wh[s][:, 0:width], raw[s][:, 0:width], ACT.Copy).then_inc(hi_ready[s], 1)

        def output(s):
            n.up(unit_done[s])
            e.wait_ge(out_taken[s], n.up(out_taken[s]))

        def root(cols):
            e.activation(dcol[0:TC, 0:cols], psM[0:TC, 0, 0:cols], ACT.Sqrt, bias=epsc[0:TC, :]).then_inc(std_ready, 1)

        def pre(l, stage):
            with n.loop(e, DT // 2, TILES) as i:
                for s in (0, 1):
                    m = i * 2 + s
                    e.wait_ge(x_ready, n.up(x_ready))
                    e.activation(tile(hh, m), tile(xT, m), ACT.Copy, scale=col(par, l * NPAR + (PRE + stage * DT) + m))\
                        .then_inc(hh_ready, 1)
                    if s == 0:
                        e.wait_ge(sq_used, n.now(sq_used))
                        n.pause()
                    e.activation(sq[s][:, :], tile(xT, m), ACT.Square).then_inc(sq_ready, 1)
                n.up(sq_used, 2)
            e.wait_ge(sq_used, n.now(sq_used))
            root(NTC)

        def result(width, after):
            def body(i, after):
                split_hi(1, width)
                output(0)
                e.wait_ge(sq_used, n.now(sq_used))
                n.pause()
                e.activation(sq[0][:, :], tile(yT, i * 2), ACT.Square).then_inc(sq_ready, 1)
                split_hi(0, after)
                output(1)
                e.activation(sq[1][:, :], tile(yT, i * 2 + 1), ACT.Square).then_inc(sq_ready, 1)
                n.up(sq_used, 2)
            with n.loop(e, DT // 2 - 1, SQUARED) as i:
                body(i, width)
            body(DT // 2 - 1, after)
            e.wait_ge(cols_ready, n.up(cols_ready))
            root(NTC)

        def passing(width, after):
            split_hi(1, width)
            output(0)
            split_hi(0, after)
            output(1)

        def ffn(l, stage, after):
            pre(l, stage)
            for c in range(CH):
                def body(j, width):
                    split_hi(1, D)
                    output(0)
                    e.activation(act[:, :], gate[:, :], ACT.Silu).then_inc(silu_ready, 1)
                    split_hi(0, width)
                    output(1)
                    e.activation(tile(hidh, j), hid[:, :], ACT.Copy).then_inc(hidh_ready, 1)
                with n.loop(e, FC - 1, HIDDEN) as j:
                    body(j, D)
                body(FC - 1, FC * P)
                if c < CH - 1:
                    with n.loop(e, DT // 2 - 1, PAIR):
                        passing(FC * P, FC * P)
                    passing(FC * P, D)
                else:
                    result(FC * P, after)

        def chunk(t0, T, nl, up):
            at = bass.ds(t0, T)
            e.activation(vc[:, :, 0:T], vT[:, :, at], ACT.Copy).then_inc(gla_a, 1)
            e.wait_ge(gla_t, n.now(gla_t, T_VT))
            e.activation(vt[0:T, :], psM[0:T, 0, :], ACT.Copy).then_inc(gla_a, 1)
            e.wait_ge(gla_v, n.now(gla_v, G_SG))
            e.activation(dec[:, :, nl + 2, 0:T], dec[:, :, 1, 0:T], ACT.Exp, scale=-1.0).then_inc(gla_a, 1)
            e.activation(dec[:, :, 0, 0:T], bc[:, :, at], ACT.Exp)
            e.activation(dec[:, :, nl + 3, 0:T], dec[:, :, nl + 3, 0:T], ACT.Exp, scale=-1.0)
            e.wait_ge(gla_a, n.now(gla_a, A_N))
            e.activation(dec[:, :, 1:nl + 2, 0:T], dec[:, :, 1:nl + 2, 0:T], ACT.Exp).then_inc(gla_a, 1)
            e.wait_ge(gla_t, n.now(gla_t, T_KE))
            e.activation(ket[0:T, :], psM[0:T, 1, 0:PR * P], ACT.Copy).then_inc(gla_a, 1)
            e.wait_ge(gla_t, n.now(gla_t, T_O))
            for odd in (0, 1):
                ins = e.activation(oT[:, :, :].rearrange("p (r o) t -> p r o t", o=2)[:, :, odd, at],
                                   psM[:, 2 + odd, 0:PR * C].rearrange("p (r t) -> p r t", r=PR)[:, :, 0:T], ACT.Copy)
            ins.then_inc(gla_a, 1)
            n.up(gla_t, up["gla_t"]), n.up(gla_v, up["gla_v"]), n.up(gla_a, up["gla_a"])

        def mixer(l):
            e.wait_ge(small_landed, n.up(small_landed, 32))
            e.activation(wgdh[:, :], wgd[:, :], ACT.Copy).then_inc(gdh_ready, 1)
            pre(l, 1)
            n.up(out_taken[1])
            with n.loop(e, LT, LRU_TILE) as i:
                k = l * LT + i
                pk = l * NPAR + i
                split_hi(1, D)
                output(0)
                split_hi(0, D)
                output(1)
                e.wait_ge(lru_t, n.up(lru_t))
                e.activation(halves(rg[:, :]), psM[:, 0:2, 0:H], ACT.Sigmoid, bias=col(par, pk + BA)).then_inc(lru_a, 1)
                e.activation(halves(ig[:, :]), psM[:, 2:4, 0:H], ACT.Sigmoid, bias=col(par, pk + BX)).then_inc(lru_a, 1)
                e.wait_ge(lru_a, n.now(lru_a, A_R))
                e.activation(tau[:, :], rg[:, :], ACT.Tanh, scale=col(sp8, k)).then_inc(lru_a, 1)
                e.activation(aa[:, :], rg[:, :], ACT.Exp, scale=col(nsp8, k)).then_inc(lru_a, 1)
                e.wait_ge(lru_a, n.now(lru_a, A_TAU))
                e.activation(l1[:, :], tau[:, :], ACT.Ln, scale=2.0, bias=tinyc[:, :]).then_inc(lru_a, 1)
                e.activation(l2[:, :], tau[:, :], ACT.Ln, bias=1.0).then_inc(lru_a, 1)
                e.wait_ge(lru_v, n.now(lru_v, V_D))
                e.activation(l1[:, :], l1[:, :], ACT.Exp, scale=0.5).then_inc(lru_a, 1)
                e.activation(tile(lruo, i), tile(lruo, i), ACT.Gelu_apprx_tanh).then_inc(lru_a, 1)
                n.up(lru_v, LRU_TILE["lru_v"]), n.up(lru_a, LRU_TILE["lru_a"])
                e.wait_ge(lru_v, n.now(lru_v))
                e.wait_ge(sq_used, n.now(sq_used))
                n.pause()
                e.activation(sq[0][:, :], tile(lruo, i), ACT.Square).then_inc(sq_ready, 1)
                n.up(sq_used)
            passing(D, D)
            e.wait_ge(logit_ready, n.up(logit_ready))
            for pr in range(PR):
                ins = e.activation(halves(oT[:, pr, :]), psM[:, 2 * pr:2 * pr + 2, 0:H], ACT.Abs, bias=col(par, l * NPAR + (GB + pr)))
            ins.then_inc(gk_a, 1)
            e.wait_ge(gk_a, n.up(gk_a))
            e.activation(oT[:, 0:PR, :], oT[:, 0:PR, :], ACT.Exp, scale=-1.0).then_inc(gk_a, 1)
            e.wait_ge(gk_a, n.up(gk_a))
            e.activation(oT[:, 0:PR, :], oT[:, 0:PR, :], ACT.Ln, bias=1.0).then_inc(gk_a, 1)
            n.up(gk_a)
            passing(D, D)
            with n.loop(e, 2, PAIR):
                passing(D, D)
            with n.loop(e, 2, PAIR) as i:
                split_hi(1, D)
                output(0)
                e.activation(tile(gT, i * 2), tile(gT, i * 2), ACT.Silu)
                split_hi(0, D)
                output(1)
                e.activation(tile(gT, i * 2 + 1), tile(gT, i * 2 + 1), ACT.Silu)
            with n.loop(e, NC_, CHUNK) as c:
                chunk(c * C, C, 5, CHUNK)
            chunk(SEQ, NB * NS, 1, SAMPLE)
            e.wait_ge(gla_a, n.now(gla_a))
            e.activation(vT[:, :, :], oT[:, :, :], ACT.Square).then_inc(head_sq, 1)
            e.wait_ge(mix_cols, n.up(mix_cols))
            root(5 * NTC)
            for k in range(DT):
                e.wait_ge(mix_v, n.up(mix_v, 2))
                e.activation(hh[:, k, :], (l1, l2)[k % 2][:, :], ACT.Copy).then_inc(hh_ready, 1)
            result(D, D)

        e.wait_ge(const_landed, 16 * 8)
        e.wait_ge(setup_p, 1)
        lam = par[:, :].rearrange("p (l k) -> p l k", l=L)[:, :, LAM:LAM + LT]
        t = [spt[:, k, :].rearrange("p (l k) -> p l k", l=L) for k in range(6)]
        e.activation(t[0], lam, ACT.Abs).then_inc(setup_a, 1)
        e.wait_ge(setup_a, 1)
        e.activation(t[1], t[0], ACT.Exp, scale=-1.0).then_inc(setup_a, 1)
        e.wait_ge(setup_v, 2)
        e.activation(t[3], t[2], ACT.Ln).then_inc(setup_a, 1)
        e.wait_ge(setup_v, 9)
        with n.loop(e, L, LAYER) as l:
            split_hi(0, D)
            ffn(l, 0, D)
            mixer(l)
            ffn(l, 2, 0)

    @block.vector
    def _(e):
        n = Tally(lambda k: e.tensor_copy(spare[32:33, k:k + 1], ones[32:33, 0:1]))

        def split_lo(s, width):
            if width:
                e.wait_ge(hi_ready[s], n.up(hi_ready[s]))
                e.tensor_tensor(wl[s][:, 0:width], raw[s][:, 0:width], wh[s][:, 0:width].bitcast(F32), ALU.subtract)\
                    .then_inc(lo_ready[s], 1)

        def psum(s):
            return psU[:, 2 * s:2 * s + 2, 0:H]

        def product_done(s):
            e.wait_ge(unit_done[s], n.up(unit_done[s]))
            n.up(out_taken[s])

        def inverse(cols):
            e.wait_ge(std_ready, n.up(std_ready))
            e.reciprocal(dinv[0:TC, 0:cols], dcol[0:TC, 0:cols]).then_inc(inv_ready, 1)
            e.wait_ge(inv_ready, n.up(inv_ready))

        def diagonals(out, at):
            return e.tensor_tensor(out[0:TC, :, :], ident[0:TC, 0:TC].unsqueeze(1).broadcast_to([TC, NTC, TC]),
                                   dinv[0:TC, at:at + NTC].unsqueeze(2).broadcast_to([TC, NTC, TC]), ALU.mult)

        def pre_lo(l, stage):
            with n.loop(e, DT // 2, TILES) as i:
                for s in (0, 1):
                    m = i * 2 + s
                    e.wait_ge(hh_ready, n.up(hh_ready))
                    e.scalar_tensor_tensor(tile(hl, m), tile(xT, m), col(par, l * NPAR + (PRE + stage * DT) + m),
                                           tile(hh, m).bitcast(F32), ALU.mult, ALU.subtract).then_inc(hl_ready, 1)
                n.up(hl_ready, 2)

        def pre_rms():
            inverse(NTC)
            diagonals(diag[0], 0).then_inc(diag_ready, 1)
            e.wait_ge(bcast_ready, n.up(bcast_ready))
            e.tensor_copy(halves(rstd[:, :]), psM[:, 1:3, 0:H]).then_inc(rstd_ready, 1)
            e.wait_ge(rstd_ready, n.up(rstd_ready))

        def residual(l, stage):
            inverse(NTC)
            diagonals(diag[0], 0).then_inc(diag_ready, 1)
            e.wait_ge(bcast_ready, n.up(bcast_ready))
            with n.loop(e, DT // 2, TILES) as i:
                e.wait_ge(x_ready, n.now(x_ready))
                n.up(x_ready, 2)
                for s in (0, 1):
                    e.tensor_tensor(halves(tmp[s][:, :]), halves(tile(yT, i * 2 + s)), psM[:, 1:3, 0:H], ALU.mult).then_inc(xpart, 1)
                for s in (0, 1):
                    e.wait_ge(xpart, n.up(xpart))
                    e.scalar_tensor_tensor(tile(xT, i * 2 + s), tmp[s][:, :], col(ph, l * 24 + stage * DT + i * 2 + s),
                                           tile(xT, i * 2 + s), ALU.mult, ALU.add).then_inc(x_ready, 1)

        def take(s, out, scale=None):
            product_done(s)
            if scale is None:
                e.tensor_tensor(halves(out), psum(s), halves(rstd[:, :]), ALU.mult).then_inc(out_taken[s], 1)
            else:
                e.scalar_tensor_tensor(halves(out), psum(s), scale, halves(rstd[:, :]), ALU.mult, ALU.mult).then_inc(out_taken[s], 1)

        def ffn(l, stage, after):
            pre_lo(l, stage)
            for c in range(CH):
                def body(j, width, first=False):
                    split_lo(1, D)
                    if first:
                        pre_rms()
                    take(0, gate[:, :])
                    split_lo(0, width)
                    e.wait_ge(silur_ready, n.up(silur_ready))
                    product_done(1)
                    e.tensor_tensor(halves(hid[:, :]), psum(1), halves(actr[:, :]), ALU.mult).then_inc(out_taken[1], 1)
                if c == 0:
                    body(0, D, first=True)
                with n.loop(e, FC - 1 - (c == 0), HIDDEN) as j:
                    body(j, D)
                body(0, FC * P)

                def down(i, after):
                    for s, width in ((0, FC * P), (1, after)):
                        split_lo(1 - s, width)
                        product_done(s)
                        y = halves(tile(yT, i * 2 + s))
                        if c == 0:
                            e.tensor_copy(y, psum(s)).then_inc(out_taken[s], 1)
                        else:
                            e.tensor_tensor(y, psum(s), y, ALU.add).then_inc(out_taken[s], 1)
                with n.loop(e, DT // 2 - 1, PAIR) as i:
                    down(i, FC * P)
                down(DT // 2 - 1, D if c < CH - 1 else after)
            residual(l, stage)

        def lru_tile(l, i):
            k = l * LT + i
            pk = l * NPAR + i

            def step(ins, more=0):
                ins.then_inc(lru_v, 1)

            split_lo(1, D)
            product_done(0)
            e.wait_ge(lru_p, n.now(lru_p))
            e.tensor_tensor(xlp[:, CW - 1:CW - 1 + H], psU[:, 0, 0:H], rstd[:, 0:H], ALU.mult)
            e.tensor_tensor(xlp[:, CW - 1 + H:XP], psU[:, 1, 0:SEQ - H], rstd[:, H:SEQ], ALU.mult)
            e.tensor_tensor(xls[:, :, CW - 1:XS], psU[:, 1, SEQ - H:H].rearrange("p (b t) -> p b t", t=NS),
                            rstd[:, SEQ:NT].rearrange("p (b t) -> p b t", t=NS), ALU.mult).then_inc(out_taken[0], 1)
            e.wait_ge(out_taken[0], n.now(out_taken[0]))
            e.wait_ge(lru_p, n.now(lru_p, P_HEAD))
            W = XA - CW + 1
            e.tensor_scalar(cv[0][:, :], xlp[:, 0:W], col(par, pk + CONVW), col(par, pk + CONVB), ALU.mult, ALU.add).then_inc(lru_v, 1)
            e.wait_ge(lru_v, n.now(lru_v, 1))
            e.scalar_tensor_tensor(cv[1][:, :], xlp[:, 1:1 + W], col(par, pk + (CONVW + LT)), cv[0][:, :], ALU.mult, ALU.add).then_inc(lru_v, 1)
            e.wait_ge(lru_v, n.now(lru_v, 2))
            e.scalar_tensor_tensor(cv[0][:, :], xlp[:, 2:2 + W], col(par, pk + (CONVW + 2 * LT)), cv[1][:, :], ALU.mult, ALU.add).then_inc(lru_v, 1)
            e.wait_ge(lru_v, n.now(lru_v, 3))
            w3 = col(par, pk + (CONVW + 3 * LT))
            e.scalar_tensor_tensor(xc[:, 0:SEQ], xlp[:, 3:3 + SEQ], w3, cv[0][:, 0:SEQ], ALU.mult, ALU.add)
            e.scalar_tensor_tensor(xc[:, SEQ:NT].rearrange("p (b t) -> p b t", t=NS), xls[:, :, CW - 1:XS], w3,
                                   starts_of(cv[0], XP, XS, NS), ALU.mult, ALU.add).then_inc(lru_v, 1)
            split_lo(0, D)
            take(1, tile(lruo, i))
            e.wait_ge(lru_a, n.now(lru_a, A_L2))
            e.tensor_tensor(l1[:, :], l1[:, :], l2[:, :], ALU.subtract).then_inc(lru_v, 1)
            e.wait_ge(lru_a, n.now(lru_a, A_M))
            e.memset(l1[:, 0:1], 1.0).then_inc(lru_v, 1)
            e.wait_ge(lru_v, n.now(lru_v, V_ONE))
            e.wait_ge(lru_p, n.now(lru_p, P_IX))
            e.tensor_tensor(l2[:, :], l1[:, :], ig[:, :], ALU.mult).then_inc(lru_v, 1)
            first = [t[:, SEQ:NT].rearrange("p (b t) -> p b t", t=NS)[:, :, 0] for t in (aa, l2)]
            e.tensor_tensor(cv[1][:, 0:NB], first[0], tile(sth, k), ALU.mult).then_inc(lru_v, 1)
            e.wait_ge(lru_v, n.now(lru_v, V_AH))
            e.tensor_tensor(first[1], first[1], cv[1][:, 0:NB], ALU.add).then_inc(lru_v, 1)
            e.memset(first[0], 0.0).then_inc(lru_v, 1)
            e.wait_ge(lru_v, n.now(lru_v, V_A0))
            e.tensor_tensor_scan(tau[:, :], aa[:, :], l2[:, :], 0.0, ALU.mult, ALU.add).then_inc(lru_v, 1)
            e.wait_ge(lru_v, n.now(lru_v, V_H))
            e.wait_ge(lru_a, n.now(lru_a, A_GE))
            e.tensor_tensor(tile(lruo, i), tau[:, :], tile(lruo, i), ALU.mult).then_inc(lru_v, 1)
            n.up(lru_v, LRU_TILE["lru_v"]), n.up(lru_a, LRU_TILE["lru_a"]), n.up(lru_p, LRU_TILE["lru_p"])

        def starts_of(t, at, period, width):
            whole = t[:, at:at + (NB - 1) * period + width]
            return bass.AP(whole.tensor, whole.offset, [list(whole.ap[0]), [period, NB], [1, width]])

        def chunk(t0, T, nl, up):
            at = bass.ds(t0, T)
            sample = up is SAMPLE

            def about(slot, width, ref):
                b = bc[:, :, at].rearrange("p r (b m) -> p r b m", m=width)
                return e.tensor_tensor(dec[:, :, slot, 0:T].rearrange("p r (b m) -> p r b m", m=width), b,
                                       b[:, :, :, ref:ref + 1].broadcast_to([P, PR, T // width, width]), ALU.subtract)
            e.wait_ge(gla_p, n.now(gla_p))
            about(1, 4, 1)
            about(nl + 3, NS if sample else T, (NS if sample else T) - 1)
            for v, m in enumerate(LEVELS[:nl]):
                ins = about(2 + v, 2 * m, m - 1)
            ins.then_inc(gla_v, 1)
            e.wait_ge(gla_v, n.now(gla_v, G_D))
            lv = dec[:, :, 2:2 + nl, 0:T]
            e.tensor_tensor(lv, lv, sign[:, 0:nl, 0:T].unsqueeze(1).broadcast_to([P, PR, nl, T]), ALU.mult).then_inc(gla_v, 1)
            e.wait_ge(gla_a, n.now(gla_a, A_E))
            e.tensor_tensor(kf[:, :, 0:nl + 2, 0:T], dec[:, :, 2:nl + 4, 0:T],
                            qk[:, PR:2 * PR, at].unsqueeze(2).broadcast_to([P, PR, nl + 2, T]), ALU.mult).then_inc(gla_v, 1)
            out = scs if sample else sc

            def place(m, data, mask):
                def blocks(t):
                    return t.rearrange("p h (b m) -> p h b m", m=m)
                o = out[0:T, :, 0:T].rearrange("p h (b m) -> p h b m", m=2 * m)[:, :, :, m:2 * m]
                e.copy_predicated(o, blocks(mask.unsqueeze(1).broadcast_to([T, HEADS, T // 2])), blocks(data)).then_inc(placed, 1)
                e.wait_ge(placed, n.up(placed))
                n.pause()
            e.wait_ge(gla_t, n.now(gla_t, T_SA))
            n.pause()
            banks = [psM[0:T, 2 * g:2 * g + 2, :].rearrange("p o (r x) -> p (o r) x", r=PR) for g in (0, 1)]
            for v, m in enumerate(LEVELS[:min(nl, 4)]):
                place(m, banks[1][:, :, v * (T // 2):(v + 1) * (T // 2)], masks[0:T, v, 0:T // 2])
            e.wait_ge(gla_t, n.now(gla_t, T_SB))
            n.pause()
            if nl == 5:
                place(LEVELS[4], banks[0][:, :, T:T + T // 2], masks[0:T, 4, 0:T // 2])
            e.copy_predicated(out[0:T, :, 0:T], masks[0:T, 5, 0:T].unsqueeze(1).broadcast_to([T, HEADS, T]),
                              banks[0][:, :, 0:T]).then_inc(gla_v, 1)
            if not sample:
                e.wait_ge(gla_t, n.now(gla_t, T_SU))
                for pr in range(PR):
                    ins = e.scalar_tensor_tensor(S[:, pr, :], S[:, pr, :], dec[:, pr, 0, T - 1:T], psM[:, 0, pr * DV:(pr + 1) * DV],
                                                 ALU.mult, ALU.add)
                ins.then_inc(gla_v, 1)
            else:
                e.wait_ge(gla_a, n.now(gla_a, A_KET))
                e.tensor_tensor(kem[:, :, :], ket[0:T, :].unsqueeze(1).broadcast_to([T, NB, PR * P]),
                                seqmask[:, :].unsqueeze(2).broadcast_to([T, NB, PR * P]), ALU.mult).then_inc(gla_v, 1)
                e.wait_ge(gla_t, n.now(gla_t, T_O))
                last = dec[:, :, 0, 0:T].rearrange("p r (b t) -> p b r t", t=NS)[:, :, :, NS - 1:NS]
                e.tensor_tensor(S0[:, :, :, :], S0[:, :, :, :], last.broadcast_to([P, NB, PR, DV]), ALU.mult).then_inc(gla_v, 1)
                e.wait_ge(gla_v, n.now(gla_v, G_S1))
                e.wait_ge(gla_t, n.now(gla_t, T_SU))
                s0 = S0[:, :, :, :].rearrange("p b r v -> p (b r v)")
                e.tensor_tensor(s0, s0, psM[:, :, :].rearrange("p o n -> p (o n)"), ALU.add).then_inc(gla_v, 1)
            n.up(gla_v, up["gla_v"]), n.up(gla_a, up["gla_a"]), n.up(gla_p, up["gla_p"]), n.up(gla_t, up["gla_t"])

        def mixer(l):
            e.wait_ge(gdh_ready, n.up(gdh_ready))
            e.tensor_tensor(wgdl[:, :], wgd[:, :], wgdh[:, :].bitcast(F32), ALU.subtract).then_inc(gdl_ready, 1)
            pre_lo(l, 1)
            pre_rms()
            e.wait_ge(gdp_ready, n.up(gdp_ready))
            n.up(out_taken[1])
            e.tensor_tensor(halves(gd[:, :]), psU[0:RANK, 2:4, 0:H], halves(rstd[0:RANK, :]), ALU.mult).then_inc(out_taken[1], 1)
            with n.loop(e, LT, LRU_TILE) as i:
                lru_tile(l, i)
            for t, scale in ((0, DK ** -0.5), (PR, 1.0)):
                split_lo(1, D)
                take(0, qk[:, t, :], scale)
                split_lo(0, D)
                take(1, qk[:, t + 1, :], scale)
                if t == 0:
                    e.wait_ge(logit_ready, n.up(logit_ready))
                    e.wait_ge(gk_a, n.up(gk_a))
                    for pr in range(PR):
                        ins = e.tensor_scalar(halves(oT[:, PR + pr, :]), psM[:, 2 * pr:2 * pr + 2, 0:H],
                                              col(par, l * NPAR + (GB + pr)), 0.0, ALU.add, ALU.min)
                    ins.then_inc(gk_v, 1)
                    e.wait_ge(gk_v, n.up(gk_v))
                    e.wait_ge(gk_a, n.up(gk_a, 2))
                    g = oT[:, PR:2 * PR, :]
                    e.tensor_tensor(g, g, oT[:, 0:PR, :], ALU.subtract).then_inc(gk_v, 1)
                    e.wait_ge(gk_v, n.up(gk_v))
                    e.tensor_scalar(g, g, 1.0 / NORMALIZER, GK_MIN, ALU.mult, ALU.max).then_inc(gk_v, 1)
                    e.wait_ge(gk_v, n.up(gk_v))
                    for pr in range(PR):
                        ins = e.tensor_tensor_scan(bc[:, pr, :], cont[:, :], oT[:, PR + pr, :], 0.0, ALU.mult, ALU.add)
                    ins.then_inc(gk_v, 1)
                    n.up(gk_v)
            for t in (vT, gT):
                with n.loop(e, 2, PAIR) as i:
                    split_lo(1, D)
                    take(0, tile(t, i * 2))
                    split_lo(0, D)
                    take(1, tile(t, i * 2 + 1))
            e.wait_ge(gk_v, n.now(gk_v))
            e.wait_ge(s_zero, n.up(s_zero))
            with n.loop(e, NC_, CHUNK) as c:
                chunk(c * C, C, 5, CHUNK)
            chunk(SEQ, NB * NS, 1, SAMPLE)
            inverse(5 * NTC)
            diagonals(diag[0], 0).then_inc(mix_d, 1)
            diagonals(diag[1], NTC).then_inc(mix_d, 1)
            k = 0
            for g in range(5):
                e.wait_ge(mix_t, n.up(mix_t))
                for src in ([lruo[:, i, :] for i in range(LT)] if g == 0 else [oT[:, g - 1, :]]):
                    val = (l1, l2)[k % 2]
                    e.tensor_tensor(halves(tmp[k % 2][:, :]), halves(src), psM[:, 2 * (g % 2):2 * (g % 2) + 2, 0:H], ALU.mult)\
                        .then_inc(mix_v, 1)
                    e.wait_ge(mix_v, n.up(mix_v))
                    if k >= 2:
                        e.wait_ge(hl_ready, n.now(hl_ready, k - 1))
                    if g == 0:
                        ins = e.tensor_scalar(val[:, :], tmp[k % 2][:, :], col(par, l * NPAR + (LNORM + k)), None, ALU.mult)
                    else:
                        ins = e.scalar_tensor_tensor(val[:, :], tmp[k % 2][:, :], col(par, l * NPAR + GNORM), gT[:, g - 1, :],
                                                     ALU.mult, ALU.mult)
                    ins.then_inc(mix_v, 1)
                    n.up(mix_v)
                    k += 1
                if g < 3:
                    diagonals(diag[g % 2], (g + 2) * NTC).then_inc(mix_d, 1)
            n.up(hh_ready, DT), n.up(hl_ready, DT)
            e.wait_ge(s_stored, n.up(s_stored, 32))

            def out(i, after):
                for s, width in ((0, D), (1, after)):
                    split_lo(1 - s, width)
                    product_done(s)
                    e.tensor_copy(halves(tile(yT, i * 2 + s)), psum(s)).then_inc(out_taken[s], 1)
            with n.loop(e, DT // 2 - 1, PAIR) as i:
                out(i, D)
            out(DT // 2 - 1, D)
            residual(l, 1)

        e.wait_ge(const_landed, 16 * 8)
        e.wait_ge(setup_p, 1)
        e.tensor_copy(masks[:, :, :], maskf)
        for l in range(L):
            for s, f in enumerate((0.5, 1.0, 0.5)):
                at = l * NPAR + POST + s * DT
                ins = e.tensor_scalar(ph[:, l * 24 + s * DT:l * 24 + (s + 1) * DT], par[:, at:at + DT], f, None, ALU.mult)
        ins.then_inc(setup_v, 1)
        lam = par[:, :].rearrange("p (l k) -> p l k", l=L)[:, :, LAM:LAM + LT]
        t = [spt[:, k, :].rearrange("p (l k) -> p l k", l=L) for k in range(6)]
        made = 1

        def then(ins):
            nonlocal made
            made += 1
            ins.then_inc(setup_v, 1)
            e.wait_ge(setup_v, made)
        e.wait_ge(setup_a, 2)
        then(e.tensor_scalar(t[2], t[1], 1.0, None, ALU.add))
        then(e.scalar_tensor_tensor(t[1], t[2], -1.0, t[1], ALU.add, ALU.subtract))
        then(e.reciprocal(t[4], t[2]))
        then(e.tensor_tensor(t[1], t[1], t[4], ALU.mult))
        then(e.tensor_scalar(t[5], lam, -1.0, 0.0, ALU.mult, ALU.max))
        e.wait_ge(setup_a, 3)
        then(e.tensor_tensor(t[3], t[3], t[1], ALU.subtract))
        then(e.tensor_tensor(t[3], t[3], t[5], ALU.add))
        e.tensor_scalar(sp8[:, :], spt[:, 3, :], LRU_C, None, ALU.mult)
        then(e.tensor_scalar(nsp8[:, :], spt[:, 3, :], -LRU_C, None, ALU.mult))
        for m in range(DT):
            e.wait_ge(x_landed[m], 16)
            e.tensor_copy(xT[:, m, :], yT[:, m, :]).then_inc(x_ready, 1)
            n.up(x_ready)
        with n.loop(e, L, LAYER) as l:
            split_lo(0, D)
            ffn(l, 0, D)
            mixer(l)
            ffn(l, 2, 0)

    @block.gpsimd
    def _(e):
        n = Tally(lambda k: e.tensor_tensor(spare[:, 32 + k:33 + k], ones[:, 0:1], ones[:, 1:2], ALU.mult))

        def add_squares(s):
            e.wait_ge(sq_ready, n.up(sq_ready))
            e.wait_ge(sq_used, n.now(sq_used))
            n.up(sq_used)
            e.tensor_tensor(ssum[:, :], ssum[:, :], sq[s][:, :], ALU.add).then_inc(sq_used, 1)

        def clear(ready):
            e.wait_ge(ready, n.up(ready))
            n.pause()
            e.memset(ssum[:, :], 0.0).then_inc(ssum_zero, 1)

        def pre():
            n.up(hh_ready, DT), n.up(sq_ready, DT), n.up(sq_used, DT)

        def result():
            e.wait_ge(ssum_zero, n.up(ssum_zero))
            with n.loop(e, DT // 2, SQUARED):
                add_squares(0)
                add_squares(1)
            clear(cols_ready)

        def ffn():
            pre()
            for c in range(CH):
                with n.loop(e, FC, HIDDEN) as j:
                    e.wait_ge(silu_ready, n.up(silu_ready))
                    e.tensor_tensor(actr[:, :], act[:, :], rstd[:, :], ALU.mult).then_inc(silur_ready, 1)
                    e.wait_ge(hidh_ready, n.up(hidh_ready))
                    e.tensor_tensor(tile(hidl, j), hid[:, :], tile(hidh, j).bitcast(F32), ALU.subtract).then_inc(hidl_ready, 1)
            result()

        def chunk(t0, T, nl, up):
            e.wait_ge(gla_a, n.now(gla_a, A_E))
            e.tensor_tensor(qf[:, :, 0:nl + 2, 0:T], dec[:, :, 0:nl + 2, 0:T],
                            qk[:, 0:PR, bass.ds(t0, T)].unsqueeze(2).broadcast_to([P, PR, nl + 2, T]), ALU.mult).then_inc(gla_p, 1)
            n.up(gla_a, up["gla_a"]), n.up(gla_p, up["gla_p"])
            n.up(gla_t, up["gla_t"])

        def mixer(l):
            pre()
            e.wait_ge(s_stored, n.now(s_stored))
            n.up(s_stored, 32)
            n.pause()
            e.memset(xlp[:, 0:CW - 1], 0.0)
            e.memset(S[:, :, :], 0.0).then_inc(s_zero, 1)
            e.wait_ge(ssum_zero, n.up(ssum_zero))
            with n.loop(e, LT, LRU_TILE) as i:
                k = l * LT + i
                e.wait_ge(lru_v, n.now(lru_v))
                e.tensor_copy(xls[:, :, 0:CW - 1], stc[:, bass.ds(k, 1), :, :].rearrange("p o b t -> p (o b) t")).then_inc(lru_p, 1)
                e.wait_ge(lru_a, n.now(lru_a, A_I))
                e.tensor_tensor(ig[:, :], ig[:, :], xc[:, :], ALU.mult).then_inc(lru_p, 1)
                e.wait_ge(lru_v, n.now(lru_v, V_H))
                out = tile(state_out, k)
                e.tensor_copy(out[:, O_CP:O_CS], xlp[:, SEQ:XP])
                e.tensor_copy(out[:, O_CS:O_HP].rearrange("p (b t) -> p b t", t=CW - 1), xls[:, :, NS:XS])
                e.tensor_copy(out[:, O_HP:O_HS], tau[:, SEQ - 1:SEQ])
                e.tensor_copy(out[:, O_HS:NST], tau[:, SEQ:NT].rearrange("p (b t) -> p b t", t=NS)[:, :, NS - 1])\
                    .then_inc(lru_p, 1)
                add_squares(0)
                n.up(lru_v, LRU_TILE["lru_v"]), n.up(lru_a, LRU_TILE["lru_a"]), n.up(lru_p, LRU_TILE["lru_p"])
            with n.loop(e, NC_, CHUNK) as c:
                chunk(c * C, C, 5, CHUNK)
            chunk(SEQ, NB * NS, 1, SAMPLE)
            clear(mix_cols)
            for k in range(DT):
                e.wait_ge(hh_ready, n.up(hh_ready))
                e.tensor_tensor(hl[:, k, :], (l1, l2)[k % 2][:, :], hh[:, k, :].bitcast(F32), ALU.subtract).then_inc(hl_ready, 1)
            result()

        e.memset(ones[:, :], 1.0)
        for k, width in enumerate((D, DL, DV)):
            e.memset(means[:, k:k + 1], 1.0 / width)
        e.memset(epsc[:, :], EPS)
        e.memset(tinyc[:, :], TINY)
        e.memset(sc[:, :, :], 0.0)
        e.memset(scs[:, :, :], 0.0)
        e.memset(ssum[:, :], 0.0).then_inc(ssum_zero, 1)
        e.memset(dcol[:, :], 1.0).then_inc(setup_p, 1)
        e.wait_ge(setup_p, 1)
        with n.loop(e, L, LAYER) as l:
            ffn()
            mixer(l)
            ffn()



def layouts(x_prompt, x_sample, state_lru_h, state_lru_conv, state_gla, norm_pre, norm_post, w_ffn_gate, w_ffn_up,
            w_ffn_down, w_in, conv_w, conv_b, lru_wa, lru_ba, lru_wx, lru_bx, lru_lambda, lru_norm, gla_w_gate,
            gla_b_gate, gla_norm, w_out):
    import numpy as np
    f = np.float32

    def units(w):
        *lead, K, N = w.shape
        w = w.reshape(*lead, K // P, P, N // P, P)
        k = len(lead)
        return w.transpose(*range(k), k + 2, k + 1, k, k + 3).reshape(*lead, N // P, P, K)

    def vec(v):
        return v.reshape(L, -1, P).transpose(2, 0, 1)

    x = np.concatenate([x_prompt.reshape(SEQ, D), x_sample.reshape(NB * NS, D)])
    gu = np.stack([units(w_ffn_gate), units(w_ffn_up)], axis=3)
    down = units(w_ffn_down.reshape(L, 2, CH, FC * P, D))
    wi = units(w_in[:, :, :20 * P])
    order = [t for i in range(LT) for t in (i, LT + i)] + list(range(2 * LT, 20))
    gates = np.zeros((L, LT, P, 2, P), f)
    for g, w in enumerate((lru_wa, lru_wx)):
        for b in range(8):
            r = slice(64 * (b % 2), 64 * (b % 2) + 64)
            gates[:, b // 2, r, g, r] = w[:, b]
    par = np.concatenate([vec(norm_pre.reshape(L, -1)), vec(norm_post.reshape(L, -1)), vec(conv_w.reshape(L, -1)),
                          vec(conv_b), vec(lru_ba), vec(lru_bx), vec(lru_lambda), vec(lru_norm), vec(gla_b_gate),
                          vec(gla_norm)], axis=2)
    s, t = np.arange(C)[:, None], np.arange(C)[None, :]
    masks = np.zeros((P, 6, C), f)
    sign = np.zeros((P, len(LEVELS), C), f)
    for v, m in enumerate(LEVELS):
        ok = (s // (2 * m) == t // (2 * m)) & (s % (2 * m) < m) & (t % (2 * m) >= m)
        masks[:, v, :C // 2] = ok[:, (np.arange(C) % (2 * m)) >= m]
        sign[:, v, :] = np.where(t % (2 * m) >= m, 1.0, -1.0)
    masks[:, 5, :] = (s // 4 == t // 4) & (s <= t)
    cont = np.ones((P, NT), f)
    cont[:, 0:SEQ:C] = 0
    cont[:, SEQ:NT:NS] = 0
    return {
        "xT": x.reshape(NT, DT, P).transpose(2, 1, 0),
        "w_gu": gu.reshape(-1, P, D),
        "w_d": down.reshape(-1, P, FC * P),
        "w_in": wi[:, order].reshape(-1, P, D),
        "w_gd": w_in[:, :, 20 * P:].reshape(L, DT, P, RANK).transpose(0, 2, 1, 3).reshape(L, P, DT * RANK),
        "w_g2": gla_w_gate,
        "w_ax": gates.reshape(L * LT, P, 2 * P),
        "w_out": units(w_out).reshape(-1, P, D),
        "par": par.reshape(P, L * NPAR),
        "st_h": state_lru_h.reshape(L, NB, LT, P).transpose(3, 0, 2, 1).reshape(P, L * LT, NB),
        "st_conv": state_lru_conv.reshape(L, NB, CW - 1, LT, P).transpose(4, 0, 3, 1, 2).reshape(P, L * LT, NB, CW - 1),
        "st_gla": state_gla.reshape(L, NB, PR, P, DV).transpose(0, 3, 1, 2, 4),
        "ident": np.eye(P, dtype=f), "masks": masks, "sign": sign,
        "seqmask": np.repeat(np.eye(NB, dtype=f), NS, axis=0), "cont": cont,
    }


OUTPUTS = {"yT": (P, DT, NT), "states": (P, L * LT, NST), "gla_p": (L, P, PR, DV), "gla_s": (L, P, NB, PR, DV)}


def kernel(**inputs):
    import numpy as np
    import concourse.bacc as bacc
    from concourse.bass_utils import run_bass_kernel_spmd

    arrays = {f"in_{k}": np.ascontiguousarray(v) for k, v in layouts(**{k: np.asarray(v) for k, v in inputs.items()}).items()}
    nc = bacc.Bacc("TRN2", target_bir_lowering=False, num_devices=1)
    a = {k[3:]: nc.dram_tensor(k, v.shape, mybir.dt.from_np(v.dtype), kind="ExternalInput").ap() for k, v in arrays.items()}
    a["yT_in"] = a["xT"]
    for k, shape in OUTPUTS.items():
        a[k] = nc.dram_tensor(f"out_{k}", shape, F32, kind="ExternalOutput").ap()
    build(nc, a)
    r = run_bass_kernel_spmd(nc, [arrays], core_ids=[0]).results[0]
    y = r["out_yT"].transpose(2, 1, 0).reshape(NT, D)
    st = r["out_states"].reshape(P, L, LT, NST).transpose(1, 3, 2, 0).reshape(L, NST, DL)
    return (y[:SEQ].reshape(1, SEQ, D), y[SEQ:].reshape(NB, NS, D),
            st[:, O_HP:O_HS], st[:, O_CP:O_CS].reshape(L, 1, CW - 1, DL),
            r["out_gla_p"].transpose(0, 2, 1, 3).reshape(L, 1, HEADS, DK, DV),
            st[:, O_HS:], st[:, O_CS:O_HP].reshape(L, NB, CW - 1, DL),
            r["out_gla_s"].transpose(0, 2, 3, 1, 4).reshape(L, NB, HEADS, DK, DV))
```

```python
from contextlib import ExitStack, contextmanager

import concourse.bass as bass
from concourse import mybir

F32 = mybir.dt.float32
F32R = mybir.dt.float32r
U8 = mybir.dt.uint8
ALU = mybir.AluOpType
ACT = mybir.ActivationFunctionType

P = 128
D = 1024
DT = D // P
L = 2
SEQ = 512
NB, NS = 8, 8
NT = SEQ + NB * NS
H = NT // 2
FF = 2816
FT = FF // P
CH = 2
FC = FT // CH
DL = 512
LT = DL // P
CW = 4
XP = SEQ + CW - 1
XS = NS + CW - 1
XA = XP + NB * XS
HEADS = 4
DK, DV = 64, 128
PR = 2
RANK = 16
C = 128
NC_ = SEQ // C
LEVELS = [4, 8, 16, 32, 64]
EPS = 1e-6
TC = 96
NTC = NT // TC
NSL = 3 + len(LEVELS)
LRU_C, NORMALIZER = 8.0, 16.0
GK_MIN = -40.0
TINY = 1e-18

PRE, POST, CONVW, CONVB, BA, BX, LAM, LNORM, GB, GNORM, NPAR = 0, 24, 48, 64, 68, 72, 76, 80, 84, 86, 87
O_CP, O_CS, O_HP, O_HS, NST = 0, 3, 27, 28, 36
V_XC, V_D, V_ONE, V_B, V_AH, V_BS, V_A0, V_H, V_O = 4, 5, 6, 7, 8, 9, 10, 11, 12
A_R, A_I, A_TAU, A_AA, A_L1, A_L2, A_M, A_GE = range(1, 9)
P_HEAD, P_IX, P_ST = 1, 2, 3
G_SC, G_S, G_KEM, G_S1, G_S2 = 1, 2, 2, 3, 4
D_VC, D_N, D_E = 1, 2, 3
A_VT, A_KET, A_O = 1, 2, 3
T_VT, T_KE, T_SA, T_SB, T_O, T_SU = range(1, 7)


class Tally:

    def __init__(self, small_step=None):
        self.small_step, self.count, self.open, self.pauses = small_step, {}, [], 0

    def pause(self):
        if self.small_step:
            self.small_step(self.pauses)
            self.pauses += 1

    def now(self, sem, more=0):
        v = self.count.get(sem.name, 0) + more
        for reg, rises in self.open:
            if rises.get(sem.name, 0):
                v = reg * rises[sem.name] + v
        return v

    def up(self, sem, k=1):
        self.count[sem.name] = self.count.get(sem.name, 0) + k
        return self.now(sem)

    @contextmanager
    def loop(self, eng, times, rises):
        before = dict(self.count)
        with eng.Fori(0, times) as i:
            self.open.append((i, rises))
            yield i
            self.open.pop()
        rise = {k: v - before.get(k, 0) for k, v in self.count.items() if v != before.get(k, 0)}
        assert all(rises.get(k) == v for k, v in rise.items()), f"a loop raises {rise}, said {rises}"
        for k, v in rise.items():
            self.count[k] = before.get(k, 0) + v * times


PAIR = {f"{k}{s}": 1 for k in ("lo_ready", "hi_ready", "unit_done", "out_taken") for s in (0, 1)}
PAIR |= {"raw_landed0": 16, "raw_landed1": 16}
HIDDEN = PAIR | {"silu_ready": 1, "silur_ready": 1, "hidh_ready": 1, "hidl_ready": 1}
SQUARED = PAIR | {"sq_ready": 2, "sq_used": 2}
TILES = {"x_ready": 2, "xpart": 2, "hh_ready": 2, "hl_ready": 2, "sq_ready": 2, "sq_used": 2}
LRU_TILE = {k: 2 * v for k, v in PAIR.items()} | {"gates_landed": 16, "lru_v": 12, "lru_a": 8, "lru_p": 3, "lru_t": 1, "sq_ready": 1, "sq_used": 1}
CHUNK = {"gla_v": 2, "gla_a": 3, "gla_t": 6, "placed": 5, "dec_v": 2, "dec_a": 3, "keys_ready": 1, "queries_ready": 2}
SAMPLE = {"gla_v": 4, "gla_a": 3, "gla_t": 6, "placed": 1, "dec_v": 2, "dec_a": 3, "keys_ready": 1, "queries_ready": 2}
UNITS = 2 * (FT * 2 + CH * DT) + 20 + DT
LAYER = {f"{k}{s}": UNITS // 2 for k in ("lo_ready", "hi_ready", "unit_done") for s in (0, 1)}
LAYER |= {"out_taken0": UNITS // 2, "out_taken1": UNITS // 2 + 1, "raw_landed0": 8 * UNITS, "raw_landed1": 8 * UNITS}
LAYER |= {k: LT * LRU_TILE[k] for k in ("gates_landed", "lru_v", "lru_a", "lru_p", "lru_t")}
LAYER |= {k: NC_ * CHUNK[k] + SAMPLE[k] for k in CHUNK}
LAYER |= {"eb_ready": 1}
LAYER |= {"x_ready": 3 * DT, "xpart": 3 * DT, "hh_ready": 4 * DT, "hl_ready": 4 * DT}
LAYER |= {"sq_ready": 6 * DT + LT, "sq_used": 6 * DT + LT, "ssum_zero": 4, "small_landed": 32}
LAYER |= {"cols_ready": 3, "std_ready": 7, "inv_ready": 7, "diag_ready": 6, "bcast_ready": 6, "rstd_ready": 3}
LAYER |= {"silu_ready": 2 * FT, "silur_ready": 2 * FT, "hidh_ready": 2 * FT, "hidl_ready": 2 * FT}
LAYER |= {"gdh_ready": 1, "gdl_ready": 1, "gdp_ready": 1, "logit_ready": 1, "gk_v": 4, "gk_a": 3}
LAYER |= {"s_zero": 1, "odd_out": 1, "s0_landed": 16, "s_stored": 32, "head_sq": 1, "mix_cols": 1, "mix_t": 5, "mix_d": 5, "mix_v": 16}
SQ_BEFORE_S0 = 3 * DT + LT


def halves(ap):
    return ap.rearrange("p (a n) -> p a n", a=2)


def build(nc, a):
    ctx = ExitStack()
    with ctx:
        program(nc, a, ctx)


def program(nc, a, ctx):
    cursor = [(nc.sbuf_base + 31) // 32 * 32]

    def sb(name, shape, dt=F32):
        size = 1 if dt == U8 else 4
        for n in shape[1:]:
            size *= n
        t = nc.alloc_sbuf_tensor_at(name, shape, dt, offset=cursor[0])
        cursor[0] += (size + 31) // 32 * 32
        assert cursor[0] <= nc.sbuf_usable_end, (name, cursor[0])
        return t

    xT = sb("xT", [P, DT, NT])
    operand_at = cursor[0]
    hh = sb("hh", [P, DT, NT], F32R)
    hl = sb("hl", [P, DT, NT], F32R)
    raw = [sb(f"raw{s}", [P, FC * P]) for s in (0, 1)]
    wh = [sb(f"wh{s}", [P, FC * P], F32R) for s in (0, 1)]
    wl = [sb(f"wl{s}", [P, FC * P], F32R) for s in (0, 1)]
    par = sb("par", [P, L * NPAR])
    ph = sb("ph", [P, L * 24])
    sp8 = sb("sp8", [P, L * LT])
    nsp8 = sb("nsp8", [P, L * LT])
    spt = sb("spt", [P, 6, L * LT])
    ones = sb("ones", [P, P])
    means = sb("means", [P, 3])
    spare = sb("spare", [P, 64])
    qkvs = sb("qkvs", [P, 2 * PR + HEADS])
    epsc = sb("epsc", [P, 1])
    tinyc = sb("tinyc", [P, 1])
    rstd = sb("rstd", [P, NT])
    ident = sb("ident", [P, P])
    dcol = sb("dcol", [P, 5 * NTC])
    dinv = sb("dinv", [P, 5 * NTC])
    diag = [sb(f"diag{s}", [P, NTC, TC]) for s in (0, 1)]
    ssum = sb("ssum", [P, NT])
    sq = [sb(f"sq{s}", [P, NT]) for s in (0, 1)]
    tmp = [sb(f"tmp{s}", [P, NT]) for s in (0, 1)]
    state_out = sb("state_out", [P, L * LT, NST])
    sth = sb("sth", [P, L * LT, NB])
    stc = sb("stc", [P, L * LT, NB, CW - 1])
    wgd = sb("wgd", [P, DT * RANK])
    wgdh = sb("wgdh", [P, DT * RANK], F32R)
    wgdl = sb("wgdl", [P, DT * RANK], F32R)
    wg2 = sb("wg2", [RANK, PR * P])
    gates = sb("gates", [P, 2 * P])
    masks = sb("masks", [P, 6, C], U8)
    sign = sb("sign", [P, len(LEVELS), C])
    seqmask = sb("seqmask", [NB * NS, NB])
    cont = sb("cont", [P, NT])
    sc = sb("sc", [P, HEADS, C])
    scs = sb("scs", [NB * NS, HEADS, NB * NS])
    S = sb("S", [P, PR, DV])
    result_at = cursor[0]
    yT = sb("yT", [P, DT, NT])
    shared_at = cursor[0]
    hidh = sb("hidh", [P, FC, NT], F32R)
    hidl = sb("hidl", [P, FC, NT], F32R)
    gate = sb("gate", [P, NT])
    act = sb("act", [P, NT])
    actr = sb("actr", [P, NT])
    hid = sb("hid", [P, NT])
    cursor[0] = shared_at
    qkv = sb("qkv", [P, 2 * PR + HEADS, NT])
    qk, vT = qkv[:, 0:2 * PR, :], qkv[:, 2 * PR:, :]
    bc = sb("bc", [P, PR, NT])
    gT = sb("gT", [P, HEADS, NT])
    oT = sb("oT", [P, HEADS, NT])
    lruo = sb("lruo", [P, LT, NT])
    gd = sb("gd", [RANK, NT])
    xlp = sb("xlp", [P, XA])
    l1 = sb("l1", [P, NT])
    l2 = sb("l2", [P, NT])
    cursor[0] = result_at
    cv = [sb(f"cv{s}", [P, XA - CW + 1]) for s in (0, 1)]
    xc = sb("xc", [P, NT])
    rg = sb("rg", [P, NT])
    ig = sb("ig", [P, NT])
    tau = sb("tau", [P, NT])
    aa = sb("aa", [P, NT])
    assert cursor[0] <= shared_at
    cursor[0] = result_at
    S0 = sb("S0", [P, NB, PR, DV])
    kem = sb("kem", [NB * NS, NB, PR * P])
    assert cursor[0] <= shared_at
    cursor[0] = operand_at
    eb = sb("eb", [P, PR, NT])
    qe = sb("qe", [P, PR, C])
    dec = sb("dec", [P, PR, NSL, C])
    qf = sb("qf", [P, PR, NSL - 2, C])
    kf = sb("kf", [P, PR, NSL - 1, C])
    vc = sb("vc", [P, HEADS, C])
    vt = sb("vt", [P, HEADS * DV])
    ket = sb("ket", [P, PR * P])
    assert cursor[0] <= operand_at + 2 * DT * NT * 4
    maskf = qk[:, :, :].rearrange("p a n -> p (a n)")[:, 0:6 * C].rearrange("p (v n) -> p v n", v=6)
    xls = xlp[:, XP:XA].rearrange("p (b t) -> p b t", t=XS)

    psU = ctx.enter_context(nc.psum_tensor("psU", [P, 4, 512], F32))
    psM = ctx.enter_context(nc.psum_tensor("psM", [P, 4, 512], F32))

    def sem(name):
        return ctx.enter_context(nc.semaphore(name))

    x_landed = [sem(f"x_landed{m}") for m in range(DT)]
    const_landed = sem("const_landed")
    raw_landed, hi_ready, lo_ready, unit_done, out_taken = (
        [sem(f"{k}{s}") for s in (0, 1)] for k in ("raw_landed", "hi_ready", "lo_ready", "unit_done", "out_taken"))
    small_landed = sem("small_landed")
    gates_landed = sem("gates_landed")
    setup_v, setup_a, setup_p = sem("setup_v"), sem("setup_a"), sem("setup_p")
    x_ready = sem("x_ready")
    xpart = sem("xpart")
    hh_ready, hl_ready = sem("hh_ready"), sem("hl_ready")
    sq_ready, sq_used = sem("sq_ready"), sem("sq_used")
    ssum_zero = sem("ssum_zero")
    cols_ready, std_ready, inv_ready, diag_ready, bcast_ready, rstd_ready = (
        sem(k) for k in ("cols_ready", "std_ready", "inv_ready", "diag_ready", "bcast_ready", "rstd_ready"))
    silu_ready, silur_ready = sem("silu_ready"), sem("silur_ready")
    hidh_ready, hidl_ready = sem("hidh_ready"), sem("hidl_ready")
    gdh_ready, gdl_ready, gdp_ready, logit_ready = (sem(k) for k in ("gdh_ready", "gdl_ready", "gdp_ready", "logit_ready"))
    lru_v, lru_a, lru_p, lru_t = (sem(f"lru_{k}") for k in "vapt")
    gk_v, gk_a = sem("gk_v"), sem("gk_a")
    gla_v, gla_a, gla_t = (sem(f"gla_{k}") for k in "vat")
    eb_ready = sem("eb_ready")
    dec_v, dec_a = sem("dec_v"), sem("dec_a")
    keys_ready, queries_ready = sem("keys_ready"), sem("queries_ready")
    odd_out = sem("odd_out")
    placed = sem("placed")
    s_zero, s0_landed, s_stored = sem("s_zero"), sem("s0_landed"), sem("s_stored")
    head_sq, mix_cols, mix_t, mix_d, mix_v = (sem(k) for k in ("head_sq", "mix_cols", "mix_t", "mix_d", "mix_v"))
    y_stored = sem("y_stored")

    block = ctx.enter_context(nc.Block())

    def tile(t, m):
        return t[:, m, :] if isinstance(m, int) else t[:, bass.ds(m, 1), :].rearrange("p o n -> p (o n)")

    def col(t, k):
        return t[:, bass.ds(k, 1)]

    def dram(t, k):
        return t[bass.ds(k, 1), :, :].rearrange("o p n -> (o p) n")

    @block.sync
    def _(e):
        n = Tally()

        def load(s, width, src):
            e.wait_ge(lo_ready[s], n.now(lo_ready[s]))
            n.up(lo_ready[s])
            e.dma_start(raw[s][:, 0:width], src).then_inc(raw_landed[s], 16)

        def pairs(times, width, src, first):
            with n.loop(e, times, PAIR) as j:
                for s in (0, 1):
                    load(s, width, dram(src, first + j * 2 + s))

        def ffn(l, f):
            for c in range(CH):
                pairs(FC, D, a["w_gu"], (l * 2 + f) * (CH * FC * 2) + c * FC * 2)
                pairs(DT // 2, FC * P, a["w_d"], (l * 2 + f) * (CH * DT) + c * DT)

        for m in range(DT):
            e.dma_start(yT[:, m, :], a["xT"][:, m, :]).then_inc(x_landed[m], 16)
        for t, src in ((par, "par"), (sth, "st_h"), (stc, "st_conv"), (ident, "ident"), (maskf, "masks"), (sign, "sign"),
                       (seqmask, "seqmask"), (cont, "cont")):
            e.dma_start(maskf if t is maskf else t[:], a[src]).then_inc(const_landed, 16)

        with n.loop(e, L, LAYER) as l:
            ffn(l, 0)
            e.wait_ge(logit_ready, n.now(logit_ready))
            n.up(logit_ready)
            e.dma_start(wgd[:, :], dram(a["w_gd"], l)).then_inc(small_landed, 16)
            e.dma_start(wg2[:, :], dram(a["w_g2"], l)).then_inc(small_landed, 16)
            with n.loop(e, LT, LRU_TILE) as i:
                e.wait_ge(lru_t, n.now(lru_t))
                n.up(lru_t)
                e.dma_start(gates[:, :], dram(a["w_ax"], l * LT + i)).then_inc(gates_landed, 16)
                for u in range(4):
                    load(u % 2, D, dram(a["w_in"], l * 20 + i * 4 + u))
            pairs(2, D, a["w_in"], l * 20 + 4 * LT)
            e.wait_ge(lru_v, n.up(lru_v, LT * LRU_TILE["lru_v"]))
            e.wait_ge(lru_p, n.up(lru_p, LT * LRU_TILE["lru_p"]))
            e.wait_ge(sq_used, n.up(sq_used, SQ_BEFORE_S0))
            e.dma_start(S0[:, :, :, :], a["st_gla"][bass.ds(l, 1), :, :, :, :].rearrange("o p b r v -> (o p) b r v")).then_inc(s0_landed, 16)
            for s in (0, 1):
                load(s, D, dram(a["w_out"], l * DT + s))
            e.wait_ge(gla_v, n.up(gla_v, NC_ * CHUNK["gla_v"]))
            e.dma_start(a["gla_p"][bass.ds(l, 1), :, :, :].rearrange("o p r v -> (o p) r v"), S[:, :, :]).then_inc(s_stored, 16)
            e.wait_ge(gla_v, n.up(gla_v, SAMPLE["gla_v"]))
            e.dma_start(a["gla_s"][bass.ds(l, 1), :, :, :, :].rearrange("o p b r v -> (o p) b r v"), S0[:, :, :, :]).then_inc(s_stored, 16)
            n.up(sq_used, LAYER["sq_used"] - SQ_BEFORE_S0)
            pairs(DT // 2 - 1, D, a["w_out"], l * DT + 2)
            ffn(l, 1)
        for m in range(DT):
            e.wait_ge(x_ready, DT * 3 * L + m + 1)
            e.dma_start(a["yT"][:, m, :], xT[:, m, :]).then_inc(y_stored, 16)
        e.dma_start(a["states"], state_out[:, :, :]).then_inc(y_stored, 16)
        e.wait_ge(y_stored, 16 * (DT + 1))
        e.wait_ge(s_stored, 32 * L)

    @block.tensor
    def _(e):
        n = Tally(lambda k: e.matmul(psM[:, 3, 511:512], ones[:, :], means[:, 0:1], start=True, stop=True))

        def product(out, KT, w_h, w_l, M, xh, xl, ready=(), after=None):
            for kt in range(KT):
                for r in ready:
                    e.wait_ge(r, n.up(r))
                for part, (w, x) in enumerate([(w_h, xh), (w_h, xl), (w_l, xh)]):
                    for h in (0, 1):
                        mm = e.matmul(out[h], w[:, kt * M:(kt + 1) * M], x[:, kt, h * H:(h + 1) * H],
                                      start=(kt == 0 and part == 0), stop=(kt == KT - 1 and part == 2))
                if after is not None and kt < KT - 1:
                    after(kt)
            return mm

        def unit(s, KT, xh, xl, ready=(), after=None):
            e.wait_ge(lo_ready[s], n.up(lo_ready[s]))
            e.wait_ge(out_taken[s], n.now(out_taken[s]))
            n.up(out_taken[s]), n.up(unit_done[s])
            product([psU[:, 2 * s + h, 0:H] for h in (0, 1)], KT, wh[s], wl[s], P, xh, xl, ready, after)\
                .then_inc(unit_done[s], 1)
            if after is not None:
                after(KT - 1)

        def pair(KT, xh, xl, ready=()):
            unit(0, KT, xh, xl, ready)
            unit(1, KT, xh, xl)

        def columns(src, k, at, first, last):
            for t in range(NTC):
                mm = e.matmul(psM[0:TC, 0, at + t:at + t + 1], src[:, t * TC:(t + 1) * TC], means[:, k:k + 1],
                              start=(first and t == 0), stop=last, skip_group_check=True)
            return mm

        def spread():
            e.wait_ge(diag_ready, n.up(diag_ready))
            for h in (0, 1):
                mm = e.matmul(psM[:, 1 + h, 0:H], ones[0:TC, :], diag[0][0:TC, 3 * h:3 * h + 3, :], start=True, stop=True)
            mm.then_inc(bcast_ready, 1)

        def pre_columns(kt):
            e.wait_ge(sq_ready, n.up(sq_ready))
            n.up(sq_used)
            columns(sq[kt % 2], 0, 0, kt == 0, kt == DT - 1).then_inc(sq_used, 1)

        def post_norm():
            e.wait_ge(sq_used, n.up(sq_used, DT))
            n.up(sq_ready, DT)
            columns(ssum, 0, 0, True, True).then_inc(cols_ready, 1)
            spread()

        def ffn():
            for c in range(CH):
                if c == 0:
                    unit(0, DT, hh, hl, (hh_ready, hl_ready), pre_columns)
                    unit(1, DT, hh, hl, after=lambda kt: spread() if kt == 5 else None)
                with n.loop(e, FC - (c == 0), PAIR):
                    pair(DT, hh, hl)
                pair(FC, hidh, hidl, (hidl_ready,))
                with n.loop(e, DT // 2 - 1, PAIR):
                    pair(FC, hidh, hidl)
            post_norm()

        def decays_next():
            n.up(dec_a, D_E), n.up(keys_ready), n.up(queries_ready, 2)

        def chunk(T, nl, sample=False):
            up = CHUNK if not sample else SAMPLE
            e.wait_ge(dec_a, n.now(dec_a))
            for h in range(HEADS):
                mm = e.transpose(psU[:, 0, h * DV:(h + 1) * DV], vc[:, h, :], ident[:, :])
            mm.then_inc(gla_t, 1)
            e.wait_ge(keys_ready, n.now(keys_ready))
            for pr in range(PR):
                mm = e.transpose(psU[:, 1, pr * P:(pr + 1) * P], kf[:, pr, nl + 1, :], ident[:, :])
            mm.then_inc(gla_t, 1)
            e.wait_ge(queries_ready, n.now(queries_ready, -1))
            e.wait_ge(gla_a, n.now(gla_a))
            narrow = LEVELS[:min(nl, 4)]
            for odd in (0, 1):
                rows = slice(DK * odd, DK * odd + DK)
                for pr in range(PR):
                    for v, m in enumerate(narrow):
                        q = qf[rows, pr, 1 + v, 0:T].rearrange("p (b m) -> p b m", m=2 * m)[:, :, m:2 * m]
                        mm = e.matmul(psM[:, 2 + odd, pr * 256 + v * (T // 2):pr * 256 + (v + 1) * (T // 2)],
                                      kf[rows, pr, v, :], q, start=(pr == 0 and v == 0), stop=True, skip_group_check=True)
            mm.then_inc(gla_t, 1)
            for odd in (0, 1):
                rows = slice(DK * odd, DK * odd + DK)
                for pr in range(PR):
                    mm = e.matmul(psM[:, odd, pr * 256:pr * 256 + T], kf[rows, pr, nl, :], qf[rows, pr, 0, 0:T],
                                  start=(pr == 0), stop=True, skip_group_check=True)
                    if nl == 5:
                        mm = e.matmul(psM[:, odd, pr * 256 + T:pr * 256 + T + T // 2], kf[rows, pr, 4, :],
                                      qf[rows, pr, 5, T // 2:T], start=False, stop=True, skip_group_check=True)
            mm.then_inc(gla_t, 1)
            e.wait_ge(gla_a, n.now(gla_a, A_KET))
            e.wait_ge(queries_ready, n.now(queries_ready))
            e.wait_ge(gla_v, n.now(gla_v, G_SC))
            if sample:
                e.wait_ge(s0_landed, n.up(s0_landed, 16))
            for odd in (1, 0):
                for pr in range(PR):
                    h = 2 * pr + odd
                    mm = e.matmul(psM[:, 2 + odd, pr * C:pr * C + T], vt[0:T, h * DV:(h + 1) * DV],
                                  (scs if sample else sc)[0:T, 2 * odd + pr, 0:T], start=(pr == 0), stop=False, skip_group_check=True)
                if odd and sample:
                    mm.then_inc(odd_out, 1)
            for odd in (0, 1):
                rows = slice(DK * odd, DK * odd + DK)
                if odd and sample:
                    e.wait_ge(odd_out, n.up(odd_out))
                for pr in range(PR):
                    if not sample:
                        mm = e.matmul(psM[:, 2 + odd, pr * C:pr * C + T], S[rows, pr, :], qe[rows, pr, 0:T],
                                      start=False, stop=True, skip_group_check=True)
                    else:
                        for b in range(NB):
                            mm = e.matmul(psM[:, 2 + odd, pr * C + b * NS:pr * C + (b + 1) * NS], S0[rows, b, pr, :],
                                          qe[rows, pr, b * NS:(b + 1) * NS], start=False, stop=True, skip_group_check=True)
            mm.then_inc(gla_t, 1)
            if not sample:
                for h in range(HEADS):
                    rows = slice(DK * (h % 2), DK * (h % 2) + DK)
                    mm = e.matmul(psU[rows, 2, (h // 2) * DV:(h // 2 + 1) * DV], ket[0:T, h * DK:(h + 1) * DK],
                                  vt[0:T, h * DV:(h + 1) * DV], start=(h < 2), stop=True, skip_group_check=True)
            else:
                e.wait_ge(gla_a, n.now(gla_a, A_O))
                e.wait_ge(gla_v, n.now(gla_v, G_KEM))
                n.pause()
                for b in range(NB):
                    for h in range(HEADS):
                        rows = slice(DK * (h % 2), DK * (h % 2) + DK)
                        at = (b * PR + h // 2) * DV
                        mm = e.matmul(psM[rows, at // 512, at % 512:at % 512 + DV], kem[:, b, h * DK:(h + 1) * DK],
                                      vt[0:T, h * DV:(h + 1) * DV], start=(at % 512 == 0), stop=True, skip_group_check=True)
            mm.then_inc(gla_t, 1)
            for t in (gla_t, gla_v, gla_a):
                n.up(t, up[t.name])
            if not sample:
                decays_next()

        def mixer():
            e.wait_ge(gdl_ready, n.up(gdl_ready))
            e.wait_ge(out_taken[1], n.now(out_taken[1]))
            n.up(out_taken[1])
            product([psU[0:RANK, 2 + h, 0:H] for h in (0, 1)], DT, wgdh, wgdl, RANK, hh, hl, (hh_ready, hl_ready), pre_columns)\
                .then_inc(gdp_ready, 1)
            pre_columns(DT - 1)
            spread()
            with n.loop(e, LT, LRU_TILE):
                pair(DT, hh, hl)
                e.wait_ge(gates_landed, n.up(gates_landed, 16))
                e.wait_ge(lru_v, n.now(lru_v, V_XC))
                e.wait_ge(lru_a, n.now(lru_a))
                n.up(lru_v, LRU_TILE["lru_v"]), n.up(lru_a, LRU_TILE["lru_a"]), n.up(lru_t)
                for g in (0, 1):
                    for h in (0, 1):
                        mm = e.matmul(psM[:, 2 * g + h, 0:H], gates[:, g * P:(g + 1) * P], xc[:, h * H:(h + 1) * H],
                                      start=True, stop=True)
                mm.then_inc(lru_t, 1)
                pair(DT, hh, hl)
            e.wait_ge(lru_a, n.now(lru_a))
            for pr in range(PR):
                for h in (0, 1):
                    mm = e.matmul(psM[:, 2 * pr + h, 0:H], wg2[:, pr * P:(pr + 1) * P], gd[:, h * H:(h + 1) * H],
                                  start=True, stop=True)
            mm.then_inc(logit_ready, 1)
            with n.loop(e, 2, PAIR):
                pair(DT, hh, hl)
            e.wait_ge(gk_v, n.up(gk_v, 4))
            for t in out_taken:
                e.wait_ge(t, n.now(t))
            n.pause()
            decays_next()
            with n.loop(e, NC_, CHUNK):
                chunk(C, 5)
            chunk(NB * NS, 1, sample=True)
            e.wait_ge(gla_v, n.now(gla_v))
            e.wait_ge(sq_used, n.up(sq_used, LT))
            n.up(sq_ready, LT)
            columns(ssum, 1, 0, True, True)
            e.wait_ge(head_sq, n.up(head_sq))
            for h in range(HEADS):
                mm = columns(vT[:, h, :], 2, (1 + h) * NTC, False, True)
            mm.then_inc(mix_cols, 1)
            for g in range(5):
                e.wait_ge(mix_d, n.up(mix_d))
                for h in (0, 1):
                    mm = e.matmul(psM[:, 2 * (g % 2) + h, 0:H], ones[0:TC, :], diag[g % 2][0:TC, 3 * h:3 * h + 3, :],
                                  start=True, stop=True)
                mm.then_inc(mix_t, 1)
            pair(DT, hh, hl, (hh_ready, hl_ready))
            with n.loop(e, DT // 2 - 1, PAIR):
                pair(DT, hh, hl)
            post_norm()

        e.wait_ge(setup_p, 1)
        e.wait_ge(const_landed, 16 * 8)
        with n.loop(e, L, LAYER):
            ffn()
            mixer()
            ffn()

    @block.scalar
    def _(e):
        n = Tally(lambda k: e.activation(spare[0:1, k:k + 1], ones[0:1, 0:1], ACT.Copy))

        def split_hi(s, width):
            if width:
                e.wait_ge(raw_landed[s], n.up(raw_landed[s], 16))
                e.wait_ge(unit_done[s], n.now(unit_done[s]))
                e.activation(wh[s][:, 0:width], raw[s][:, 0:width], ACT.Copy).then_inc(hi_ready[s], 1)

        def output(s):
            n.up(unit_done[s])
            e.wait_ge(out_taken[s], n.up(out_taken[s]))

        def pass_on(s):
            n.up(unit_done[s])
            return n.up(out_taken[s])

        def root(cols):
            e.activation(dcol[0:TC, 0:cols], psM[0:TC, 0, 0:cols], ACT.Sqrt, bias=epsc[0:TC, :]).then_inc(std_ready, 1)

        def pre(l, stage):
            with n.loop(e, DT // 2, TILES) as i:
                for s in (0, 1):
                    m = i * 2 + s
                    e.wait_ge(x_ready, n.up(x_ready))
                    e.activation(tile(hh, m), tile(xT, m), ACT.Copy, scale=col(par, l * NPAR + (PRE + stage * DT) + m))\
                        .then_inc(hh_ready, 1)
                    if s == 0:
                        e.wait_ge(sq_used, n.now(sq_used))
                        n.pause()
                    e.activation(sq[s][:, :], tile(xT, m), ACT.Square).then_inc(sq_ready, 1)
                n.up(sq_used, 2)
            e.wait_ge(sq_used, n.now(sq_used))
            root(NTC)

        def result(width, after):
            def body(i, after):
                split_hi(1, width)
                output(0)
                e.wait_ge(sq_used, n.now(sq_used))
                n.pause()
                e.activation(sq[0][:, :], tile(yT, i * 2), ACT.Square).then_inc(sq_ready, 1)
                split_hi(0, after)
                output(1)
                e.activation(sq[1][:, :], tile(yT, i * 2 + 1), ACT.Square).then_inc(sq_ready, 1)
                n.up(sq_used, 2)
            with n.loop(e, DT // 2 - 1, SQUARED) as i:
                body(i, width)
            body(DT // 2 - 1, after)
            e.wait_ge(cols_ready, n.up(cols_ready))
            root(NTC)

        def passing(width, after):
            split_hi(1, width)
            pass_on(0)
            split_hi(0, after)
            pass_on(1)

        def ffn(l, stage, after):
            pre(l, stage)
            for c in range(CH):
                def body(j, width):
                    split_hi(1, D)
                    output(0)
                    e.activation(act[:, :], gate[:, :], ACT.Silu).then_inc(silu_ready, 1)
                    split_hi(0, width)
                    output(1)
                    e.activation(tile(hidh, j), hid[:, :], ACT.Copy).then_inc(hidh_ready, 1)
                with n.loop(e, FC - 1, HIDDEN) as j:
                    body(j, D)
                body(FC - 1, FC * P)
                if c < CH - 1:
                    with n.loop(e, DT // 2 - 1, PAIR):
                        passing(FC * P, FC * P)
                    passing(FC * P, D)
                else:
                    result(FC * P, after)

        def decays(t0, T, nl):
            e.activation(vc[:, :, 0:T], vT[:, :, bass.ds(t0, T)], ACT.Copy).then_inc(dec_a, 1)
            e.wait_ge(dec_v, n.up(dec_v, 2))
            e.activation(dec[:, :, nl + 1, 0:T], dec[:, :, 0, 0:T], ACT.Exp, scale=-1.0).then_inc(dec_a, 1)
            e.activation(dec[:, :, nl + 2, 0:T], dec[:, :, nl + 2, 0:T], ACT.Exp, scale=-1.0)
            e.wait_ge(dec_a, n.now(dec_a, D_N))
            e.activation(dec[:, :, 0:nl + 1, 0:T], dec[:, :, 0:nl + 1, 0:T], ACT.Exp).then_inc(dec_a, 1)
            n.up(dec_a, D_E)

        def chunk(t0, T, up, following=None):
            at = bass.ds(t0, T)
            e.wait_ge(gla_t, n.now(gla_t, T_VT))
            e.activation(vt[0:T, :], psU[0:T, 0, :], ACT.Copy).then_inc(gla_a, 1)
            e.wait_ge(gla_t, n.now(gla_t, T_KE))
            e.activation(ket[0:T, :], psU[0:T, 1, 0:PR * P], ACT.Copy).then_inc(gla_a, 1)
            if following:
                decays(*following)
            e.wait_ge(gla_t, n.now(gla_t, T_O))
            for odd in (0, 1):
                ins = e.activation(oT[:, :, :].rearrange("p (r o) t -> p r o t", o=2)[:, :, odd, at],
                                   psM[:, 2 + odd, 0:PR * C].rearrange("p (r t) -> p r t", r=PR)[:, :, 0:T], ACT.Copy)
            ins.then_inc(gla_a, 1)
            n.up(gla_t, up["gla_t"]), n.up(gla_a, up["gla_a"])

        def mixer(l):
            e.wait_ge(small_landed, n.up(small_landed, 32))
            e.activation(wgdh[:, :], wgd[:, :], ACT.Copy).then_inc(gdh_ready, 1)
            pre(l, 1)
            n.up(out_taken[1])
            with n.loop(e, LT, LRU_TILE) as i:
                k = l * LT + i
                pk = l * NPAR + i
                split_hi(1, D)
                pass_on(0)
                split_hi(0, D)
                yl_taken = pass_on(1)
                split_hi(1, D)
                pass_on(0)
                e.wait_ge(lru_t, n.up(lru_t))
                e.activation(halves(rg[:, :]), psM[:, 0:2, 0:H], ACT.Sigmoid, bias=col(par, pk + BA)).then_inc(lru_a, 1)
                e.activation(halves(ig[:, :]), psM[:, 2:4, 0:H], ACT.Sigmoid, bias=col(par, pk + BX)).then_inc(lru_a, 1)
                e.wait_ge(lru_a, n.now(lru_a, A_R))
                e.activation(tau[:, :], rg[:, :], ACT.Tanh, scale=col(sp8, k)).then_inc(lru_a, 1)
                e.activation(aa[:, :], rg[:, :], ACT.Exp, scale=col(nsp8, k)).then_inc(lru_a, 1)
                e.wait_ge(lru_a, n.now(lru_a, A_TAU))
                e.activation(l1[:, :], tau[:, :], ACT.Ln, scale=2.0, bias=tinyc[:, :]).then_inc(lru_a, 1)
                e.activation(l2[:, :], tau[:, :], ACT.Ln, bias=1.0).then_inc(lru_a, 1)
                split_hi(0, D)
                pass_on(1)
                e.wait_ge(lru_v, n.now(lru_v, V_D))
                e.activation(l1[:, :], l1[:, :], ACT.Exp, scale=0.5).then_inc(lru_a, 1)
                e.wait_ge(out_taken[1], yl_taken)
                n.pause()
                e.activation(tile(lruo, i), tile(lruo, i), ACT.Gelu_apprx_tanh).then_inc(lru_a, 1)
                n.up(lru_v, LRU_TILE["lru_v"]), n.up(lru_a, LRU_TILE["lru_a"])
                n.up(sq_used)
            split_hi(1, D)
            pass_on(0)
            e.wait_ge(logit_ready, n.up(logit_ready))
            for pr in range(PR):
                ins = e.activation(halves(oT[:, pr, :]), psM[:, 2 * pr:2 * pr + 2, 0:H], ACT.Abs, bias=col(par, l * NPAR + (GB + pr)))
            ins.then_inc(gk_a, 1)
            split_hi(0, D)
            pass_on(1)
            e.wait_ge(gk_a, n.up(gk_a))
            e.activation(oT[:, 0:PR, :], oT[:, 0:PR, :], ACT.Exp, scale=-1.0).then_inc(gk_a, 1)
            e.wait_ge(gk_a, n.up(gk_a))
            e.activation(oT[:, 0:PR, :], oT[:, 0:PR, :], ACT.Ln, bias=1.0).then_inc(gk_a, 1)
            n.up(gk_a)
            split_hi(1, D)
            pass_on(0)
            split_hi(0, D)
            output(1)
            e.wait_ge(gk_v, n.up(gk_v, 4))
            e.activation(eb[:, :, :], bc[:, :, :], ACT.Exp).then_inc(eb_ready, 1)
            n.up(eb_ready)
            decays(0, C, 5)
            e.activation(gT[:, :, :], gT[:, :, :], ACT.Silu)
            with n.loop(e, NC_ - 1, CHUNK) as c:
                chunk(c * C, C, CHUNK, ((c + 1) * C, C, 5))
            chunk(SEQ - C, C, CHUNK, (SEQ, NB * NS, 1))
            chunk(SEQ, NB * NS, SAMPLE)
            e.wait_ge(gla_a, n.now(gla_a))
            e.activation(vT[:, :, :], oT[:, :, :], ACT.Square).then_inc(head_sq, 1)
            e.wait_ge(mix_cols, n.up(mix_cols))
            root(5 * NTC)
            for k in range(DT):
                e.wait_ge(mix_v, n.up(mix_v, 2))
                e.activation(hh[:, k, :], (l1, l2)[k % 2][:, :], ACT.Copy).then_inc(hh_ready, 1)
            result(D, D)

        e.wait_ge(const_landed, 16 * 8)
        e.wait_ge(setup_p, 1)
        lam = par[:, :].rearrange("p (l k) -> p l k", l=L)[:, :, LAM:LAM + LT]
        t = [spt[:, k, :].rearrange("p (l k) -> p l k", l=L) for k in range(6)]
        e.activation(t[0], lam, ACT.Abs).then_inc(setup_a, 1)
        e.wait_ge(setup_a, 1)
        e.activation(t[1], t[0], ACT.Exp, scale=-1.0).then_inc(setup_a, 1)
        e.wait_ge(setup_v, 2)
        e.activation(t[3], t[2], ACT.Ln).then_inc(setup_a, 1)
        e.wait_ge(setup_v, 9)
        with n.loop(e, L, LAYER) as l:
            split_hi(0, D)
            ffn(l, 0, D)
            mixer(l)
            ffn(l, 2, 0)

    @block.vector
    def _(e):
        n = Tally(lambda k: e.tensor_copy(spare[32:33, k:k + 1], ones[32:33, 0:1]))

        def split_lo(s, width):
            if width:
                e.wait_ge(hi_ready[s], n.up(hi_ready[s]))
                e.tensor_tensor(wl[s][:, 0:width], raw[s][:, 0:width], wh[s][:, 0:width].bitcast(F32), ALU.subtract)\
                    .then_inc(lo_ready[s], 1)

        def psum(s):
            return psU[:, 2 * s:2 * s + 2, 0:H]

        def product_done(s):
            e.wait_ge(unit_done[s], n.up(unit_done[s]))
            n.up(out_taken[s])

        def inverse(cols):
            e.wait_ge(std_ready, n.up(std_ready))
            e.reciprocal(dinv[0:TC, 0:cols], dcol[0:TC, 0:cols]).then_inc(inv_ready, 1)
            e.wait_ge(inv_ready, n.up(inv_ready))

        def diagonals(out, at):
            return e.tensor_tensor(out[0:TC, :, :], ident[0:TC, 0:TC].unsqueeze(1).broadcast_to([TC, NTC, TC]),
                                   dinv[0:TC, at:at + NTC].unsqueeze(2).broadcast_to([TC, NTC, TC]), ALU.mult)

        def pre_lo(l, stage):
            with n.loop(e, DT // 2, TILES) as i:
                for s in (0, 1):
                    m = i * 2 + s
                    e.wait_ge(hh_ready, n.up(hh_ready))
                    e.scalar_tensor_tensor(tile(hl, m), tile(xT, m), col(par, l * NPAR + (PRE + stage * DT) + m),
                                           tile(hh, m).bitcast(F32), ALU.mult, ALU.subtract).then_inc(hl_ready, 1)
                n.up(hl_ready, 2)

        def pre_rms():
            inverse(NTC)
            diagonals(diag[0], 0).then_inc(diag_ready, 1)
            e.wait_ge(bcast_ready, n.up(bcast_ready))
            e.tensor_copy(halves(rstd[:, :]), psM[:, 1:3, 0:H]).then_inc(rstd_ready, 1)
            e.wait_ge(rstd_ready, n.up(rstd_ready))

        def residual(l, stage):
            inverse(NTC)
            diagonals(diag[0], 0).then_inc(diag_ready, 1)
            e.wait_ge(bcast_ready, n.up(bcast_ready))
            n.pause()
            with n.loop(e, DT // 2, TILES) as i:
                e.wait_ge(x_ready, n.now(x_ready))
                n.up(x_ready, 2)
                for s in (0, 1):
                    e.tensor_tensor(halves(tmp[s][:, :]), halves(tile(yT, i * 2 + s)), psM[:, 1:3, 0:H], ALU.mult).then_inc(xpart, 1)
                for s in (0, 1):
                    e.wait_ge(xpart, n.up(xpart))
                    e.scalar_tensor_tensor(tile(xT, i * 2 + s), tmp[s][:, :], col(ph, l * 24 + stage * DT + i * 2 + s),
                                           tile(xT, i * 2 + s), ALU.mult, ALU.add).then_inc(x_ready, 1)

        def take(s, out, scale=None):
            product_done(s)
            if scale is None:
                e.tensor_tensor(halves(out), psum(s), halves(rstd[:, :]), ALU.mult).then_inc(out_taken[s], 1)
            else:
                e.scalar_tensor_tensor(halves(out), psum(s), scale, halves(rstd[:, :]), ALU.mult, ALU.mult).then_inc(out_taken[s], 1)

        def ffn(l, stage, after):
            pre_lo(l, stage)
            for c in range(CH):
                def body(j, width, first=False):
                    split_lo(1, D)
                    if first:
                        pre_rms()
                    take(0, gate[:, :])
                    split_lo(0, width)
                    e.wait_ge(silur_ready, n.up(silur_ready))
                    product_done(1)
                    e.tensor_tensor(halves(hid[:, :]), psum(1), halves(actr[:, :]), ALU.mult).then_inc(out_taken[1], 1)
                if c == 0:
                    body(0, D, first=True)
                with n.loop(e, FC - 1 - (c == 0), HIDDEN) as j:
                    body(j, D)
                body(0, FC * P)

                def down(i, after):
                    for s, width in ((0, FC * P), (1, after)):
                        split_lo(1 - s, width)
                        product_done(s)
                        y = halves(tile(yT, i * 2 + s))
                        if c == 0:
                            e.tensor_copy(y, psum(s)).then_inc(out_taken[s], 1)
                        else:
                            e.tensor_tensor(y, psum(s), y, ALU.add).then_inc(out_taken[s], 1)
                with n.loop(e, DT // 2 - 1, PAIR) as i:
                    down(i, FC * P)
                down(DT // 2 - 1, D if c < CH - 1 else after)
            residual(l, stage)

        def lru_tile(l, i):
            k = l * LT + i
            pk = l * NPAR + i

            def step(ins, more=0):
                ins.then_inc(lru_v, 1)

            split_lo(1, D)
            product_done(0)
            e.wait_ge(lru_p, n.now(lru_p))
            e.tensor_tensor(xlp[:, CW - 1:CW - 1 + H], psU[:, 0, 0:H], rstd[:, 0:H], ALU.mult)
            e.tensor_tensor(xlp[:, CW - 1 + H:XP], psU[:, 1, 0:SEQ - H], rstd[:, H:SEQ], ALU.mult)
            e.tensor_tensor(xls[:, :, CW - 1:XS], psU[:, 1, SEQ - H:H].rearrange("p (b t) -> p b t", t=NS),
                            rstd[:, SEQ:NT].rearrange("p (b t) -> p b t", t=NS), ALU.mult).then_inc(out_taken[0], 1)
            e.wait_ge(out_taken[0], n.now(out_taken[0]))
            e.wait_ge(lru_p, n.now(lru_p, P_HEAD))
            W = XA - CW + 1
            e.tensor_scalar(cv[0][:, :], xlp[:, 0:W], col(par, pk + CONVW), col(par, pk + CONVB), ALU.mult, ALU.add).then_inc(lru_v, 1)
            e.wait_ge(lru_v, n.now(lru_v, 1))
            e.scalar_tensor_tensor(cv[1][:, :], xlp[:, 1:1 + W], col(par, pk + (CONVW + LT)), cv[0][:, :], ALU.mult, ALU.add).then_inc(lru_v, 1)
            e.wait_ge(lru_v, n.now(lru_v, 2))
            e.scalar_tensor_tensor(cv[0][:, :], xlp[:, 2:2 + W], col(par, pk + (CONVW + 2 * LT)), cv[1][:, :], ALU.mult, ALU.add).then_inc(lru_v, 1)
            e.wait_ge(lru_v, n.now(lru_v, 3))
            w3 = col(par, pk + (CONVW + 3 * LT))
            e.scalar_tensor_tensor(xc[:, 0:SEQ], xlp[:, 3:3 + SEQ], w3, cv[0][:, 0:SEQ], ALU.mult, ALU.add)
            e.scalar_tensor_tensor(xc[:, SEQ:NT].rearrange("p (b t) -> p b t", t=NS), xls[:, :, CW - 1:XS], w3,
                                   starts_of(cv[0], XP, XS, NS), ALU.mult, ALU.add).then_inc(lru_v, 1)
            split_lo(0, D)
            take(1, tile(lruo, i))
            split_lo(1, D)
            take(0, tile(qkv, i * 2), col(qkvs, i * 2))
            e.wait_ge(lru_a, n.now(lru_a, A_L2))
            e.tensor_tensor(l1[:, :], l1[:, :], l2[:, :], ALU.subtract).then_inc(lru_v, 1)
            split_lo(0, D)
            e.wait_ge(lru_a, n.now(lru_a, A_M))
            e.memset(l1[:, 0:1], 1.0).then_inc(lru_v, 1)
            e.wait_ge(lru_v, n.now(lru_v, V_ONE))
            e.wait_ge(lru_p, n.now(lru_p, P_IX))
            e.tensor_tensor(l2[:, :], l1[:, :], ig[:, :], ALU.mult).then_inc(lru_v, 1)
            first = [t[:, SEQ:NT].rearrange("p (b t) -> p b t", t=NS)[:, :, 0] for t in (aa, l2)]
            e.tensor_tensor(cv[1][:, 0:NB], first[0], tile(sth, k), ALU.mult).then_inc(lru_v, 1)
            e.wait_ge(lru_v, n.now(lru_v, V_AH))
            e.tensor_tensor(first[1], first[1], cv[1][:, 0:NB], ALU.add).then_inc(lru_v, 1)
            e.memset(first[0], 0.0).then_inc(lru_v, 1)
            e.wait_ge(lru_v, n.now(lru_v, V_A0))
            e.tensor_tensor_scan(tau[:, :], aa[:, :], l2[:, :], 0.0, ALU.mult, ALU.add).then_inc(lru_v, 1)
            e.wait_ge(lru_v, n.now(lru_v, V_H))
            e.wait_ge(lru_a, n.now(lru_a, A_GE))
            e.tensor_tensor(tile(lruo, i), tau[:, :], tile(lruo, i), ALU.mult).then_inc(lru_v, 1)
            take(1, tile(qkv, i * 2 + 1), col(qkvs, i * 2 + 1))
            n.up(lru_v, LRU_TILE["lru_v"]), n.up(lru_a, LRU_TILE["lru_a"]), n.up(lru_p, LRU_TILE["lru_p"])

        def starts_of(t, at, period, width):
            whole = t[:, at:at + (NB - 1) * period + width]
            return bass.AP(whole.tensor, whole.offset, [list(whole.ap[0]), [period, NB], [1, width]])

        def exponents(t0, T, nl):
            def about(slot, width, ref):
                b = bc[:, :, bass.ds(t0, T)].rearrange("p r (b m) -> p r b m", m=width)
                return e.tensor_tensor(dec[:, :, slot, 0:T].rearrange("p r (b m) -> p r b m", m=width), b,
                                       b[:, :, :, ref:ref + 1].broadcast_to([P, PR, T // width, width]), ALU.subtract)
            span = NS if nl == 1 else T
            about(0, 4, 1)
            about(nl + 2, span, span - 1)
            for v, m in enumerate(LEVELS[:nl]):
                ins = about(1 + v, 2 * m, m - 1)
            ins.then_inc(dec_v, 1)
            e.wait_ge(dec_v, n.up(dec_v))
            lv = dec[:, :, 1:1 + nl, 0:T]
            e.tensor_tensor(lv, lv, sign[:, 0:nl, 0:T].unsqueeze(1).broadcast_to([P, PR, nl, T]), ALU.mult).then_inc(dec_v, 1)
            n.up(dec_v)

        def keys(t0, T, nl):
            e.wait_ge(dec_a, n.up(dec_a, D_E))
            e.tensor_tensor(kf[:, :, 0:nl + 2, 0:T], dec[:, :, 1:nl + 3, 0:T],
                            qk[:, PR:2 * PR, bass.ds(t0, T)].unsqueeze(2).broadcast_to([P, PR, nl + 2, T]), ALU.mult)\
                .then_inc(keys_ready, 1)
            n.up(keys_ready), n.up(queries_ready, 2)

        def chunk(t0, T, nl, up, following=None):
            sample = up is SAMPLE
            if following:
                e.wait_ge(queries_ready, n.now(queries_ready, -1))
                e.wait_ge(keys_ready, n.now(keys_ready))
                exponents(*following)
            out = scs if sample else sc

            def place(m, data, mask):
                def blocks(t):
                    return t.rearrange("p h (b m) -> p h b m", m=m)
                o = out[0:T, :, 0:T].rearrange("p h (b m) -> p h b m", m=2 * m)[:, :, :, m:2 * m]
                e.copy_predicated(o, blocks(mask.unsqueeze(1).broadcast_to([T, HEADS, T // 2])), blocks(data)).then_inc(placed, 1)
                e.wait_ge(placed, n.up(placed))
                n.pause()
            e.wait_ge(gla_t, n.now(gla_t, T_SA))
            n.pause()
            banks = [psM[0:T, 2 * g:2 * g + 2, :].rearrange("p o (r x) -> p (o r) x", r=PR) for g in (0, 1)]
            for v, m in enumerate(LEVELS[:min(nl, 4)]):
                place(m, banks[1][:, :, v * (T // 2):(v + 1) * (T // 2)], masks[0:T, v, 0:T // 2])
            e.wait_ge(gla_t, n.now(gla_t, T_SB))
            n.pause()
            if nl == 5:
                place(LEVELS[4], banks[0][:, :, T:T + T // 2], masks[0:T, 4, 0:T // 2])
            e.copy_predicated(out[0:T, :, 0:T], masks[0:T, 5, 0:T].unsqueeze(1).broadcast_to([T, HEADS, T]),
                              banks[0][:, :, 0:T]).then_inc(gla_v, 1)
            if following:
                keys(*following)
            if not sample:
                e.wait_ge(gla_t, n.now(gla_t, T_SU))
                for pr in range(PR):
                    ins = e.scalar_tensor_tensor(S[:, pr, :], S[:, pr, :], eb[:, pr, bass.ds(t0 + T - 1, 1)], psU[:, 2, pr * DV:(pr + 1) * DV],
                                                 ALU.mult, ALU.add)
                ins.then_inc(gla_v, 1)
            else:
                e.wait_ge(gla_a, n.now(gla_a, A_KET))
                e.tensor_tensor(kem[:, :, :], ket[0:T, :].unsqueeze(1).broadcast_to([T, NB, PR * P]),
                                seqmask[:, :].unsqueeze(2).broadcast_to([T, NB, PR * P]), ALU.mult).then_inc(gla_v, 1)
                e.wait_ge(gla_t, n.now(gla_t, T_O))
                last = eb[:, :, SEQ:NT].rearrange("p r (b t) -> p b r t", t=NS)[:, :, :, NS - 1:NS]
                e.tensor_tensor(S0[:, :, :, :], S0[:, :, :, :], last.broadcast_to([P, NB, PR, DV]), ALU.mult).then_inc(gla_v, 1)
                e.wait_ge(gla_v, n.now(gla_v, G_S1))
                e.wait_ge(gla_t, n.now(gla_t, T_SU))
                s0 = S0[:, :, :, :].rearrange("p b r v -> p (b r v)")
                e.tensor_tensor(s0, s0, psM[:, :, :].rearrange("p o n -> p (o n)"), ALU.add).then_inc(gla_v, 1)
            for t in (gla_v, gla_a, gla_t):
                n.up(t, up[t.name])

        def mixer(l):
            e.wait_ge(gdh_ready, n.up(gdh_ready))
            e.tensor_tensor(wgdl[:, :], wgd[:, :], wgdh[:, :].bitcast(F32), ALU.subtract).then_inc(gdl_ready, 1)
            pre_lo(l, 1)
            pre_rms()
            e.wait_ge(gdp_ready, n.up(gdp_ready))
            n.up(out_taken[1])
            e.tensor_tensor(halves(gd[:, :]), psU[0:RANK, 2:4, 0:H], halves(rstd[0:RANK, :]), ALU.mult).then_inc(out_taken[1], 1)
            with n.loop(e, LT, LRU_TILE) as i:
                lru_tile(l, i)
            split_lo(1, D)
            e.wait_ge(logit_ready, n.up(logit_ready))
            e.wait_ge(gk_a, n.up(gk_a))
            for pr in range(PR):
                ins = e.tensor_scalar(halves(oT[:, PR + pr, :]), psM[:, 2 * pr:2 * pr + 2, 0:H],
                                      col(par, l * NPAR + (GB + pr)), 0.0, ALU.add, ALU.min)
            ins.then_inc(gk_v, 1)
            take(0, gT[:, 0, :])
            split_lo(0, D)
            take(1, gT[:, 1, :])
            e.wait_ge(gk_v, n.up(gk_v))
            e.wait_ge(gk_a, n.up(gk_a, 2))
            g = oT[:, PR:2 * PR, :]
            e.tensor_tensor(g, g, oT[:, 0:PR, :], ALU.subtract).then_inc(gk_v, 1)
            split_lo(1, D)
            e.wait_ge(gk_v, n.up(gk_v))
            e.tensor_scalar(g, g, 1.0 / NORMALIZER, GK_MIN, ALU.mult, ALU.max).then_inc(gk_v, 1)
            e.wait_ge(gk_v, n.up(gk_v))
            for pr in range(PR):
                ins = e.tensor_tensor_scan(bc[:, pr, :], cont[:, :], oT[:, PR + pr, :], 0.0, ALU.mult, ALU.add)
            ins.then_inc(gk_v, 1)
            n.up(gk_v)
            take(0, gT[:, 2, :])
            split_lo(0, D)
            take(1, gT[:, 3, :])
            e.wait_ge(gk_v, n.now(gk_v))
            e.wait_ge(s_zero, n.up(s_zero))
            exponents(0, C, 5)
            keys(0, C, 5)
            with n.loop(e, NC_ - 1, CHUNK) as c:
                chunk(c * C, C, 5, CHUNK, ((c + 1) * C, C, 5))
            chunk(SEQ - C, C, 5, CHUNK, (SEQ, NB * NS, 1))
            chunk(SEQ, NB * NS, 1, SAMPLE)
            inverse(5 * NTC)
            diagonals(diag[0], 0).then_inc(mix_d, 1)
            diagonals(diag[1], NTC).then_inc(mix_d, 1)
            k = 0
            for g in range(5):
                e.wait_ge(mix_t, n.up(mix_t))
                for src in ([lruo[:, i, :] for i in range(LT)] if g == 0 else [oT[:, g - 1, :]]):
                    val = (l1, l2)[k % 2]
                    e.tensor_tensor(halves(tmp[k % 2][:, :]), halves(src), psM[:, 2 * (g % 2):2 * (g % 2) + 2, 0:H], ALU.mult)\
                        .then_inc(mix_v, 1)
                    e.wait_ge(mix_v, n.up(mix_v))
                    if k >= 2:
                        e.wait_ge(hl_ready, n.now(hl_ready, k - 1))
                    if g == 0:
                        ins = e.tensor_scalar(val[:, :], tmp[k % 2][:, :], col(par, l * NPAR + (LNORM + k)), None, ALU.mult)
                    else:
                        ins = e.scalar_tensor_tensor(val[:, :], tmp[k % 2][:, :], col(par, l * NPAR + GNORM), gT[:, g - 1, :],
                                                     ALU.mult, ALU.mult)
                    ins.then_inc(mix_v, 1)
                    n.up(mix_v)
                    k += 1
                if g < 3:
                    diagonals(diag[g % 2], (g + 2) * NTC).then_inc(mix_d, 1)
            n.up(hh_ready, DT), n.up(hl_ready, DT)
            e.wait_ge(s_stored, n.up(s_stored, 32))

            def out(i, after):
                for s, width in ((0, D), (1, after)):
                    split_lo(1 - s, width)
                    product_done(s)
                    e.tensor_copy(halves(tile(yT, i * 2 + s)), psum(s)).then_inc(out_taken[s], 1)
            n.pause()
            with n.loop(e, DT // 2 - 1, PAIR) as i:
                out(i, D)
            out(DT // 2 - 1, D)
            residual(l, 1)

        e.wait_ge(const_landed, 16 * 8)
        e.wait_ge(setup_p, 1)
        e.tensor_copy(masks[:, :, :], maskf)
        for l in range(L):
            for s, f in enumerate((0.5, 1.0, 0.5)):
                at = l * NPAR + POST + s * DT
                ins = e.tensor_scalar(ph[:, l * 24 + s * DT:l * 24 + (s + 1) * DT], par[:, at:at + DT], f, None, ALU.mult)
        ins.then_inc(setup_v, 1)
        lam = par[:, :].rearrange("p (l k) -> p l k", l=L)[:, :, LAM:LAM + LT]
        t = [spt[:, k, :].rearrange("p (l k) -> p l k", l=L) for k in range(6)]
        made = 1

        def then(ins):
            nonlocal made
            made += 1
            ins.then_inc(setup_v, 1)
            e.wait_ge(setup_v, made)
        e.wait_ge(setup_a, 2)
        then(e.tensor_scalar(t[2], t[1], 1.0, None, ALU.add))
        then(e.scalar_tensor_tensor(t[1], t[2], -1.0, t[1], ALU.add, ALU.subtract))
        then(e.reciprocal(t[4], t[2]))
        then(e.tensor_tensor(t[1], t[1], t[4], ALU.mult))
        then(e.tensor_scalar(t[5], lam, -1.0, 0.0, ALU.mult, ALU.max))
        e.wait_ge(setup_a, 3)
        then(e.tensor_tensor(t[3], t[3], t[1], ALU.subtract))
        then(e.tensor_tensor(t[3], t[3], t[5], ALU.add))
        e.tensor_scalar(sp8[:, :], spt[:, 3, :], LRU_C, None, ALU.mult)
        then(e.tensor_scalar(nsp8[:, :], spt[:, 3, :], -LRU_C, None, ALU.mult))
        for m in range(DT):
            e.wait_ge(x_landed[m], 16)
            e.tensor_copy(xT[:, m, :], yT[:, m, :]).then_inc(x_ready, 1)
            n.up(x_ready)
        with n.loop(e, L, LAYER) as l:
            split_lo(0, D)
            ffn(l, 0, D)
            mixer(l)
            ffn(l, 2, 0)

    @block.gpsimd
    def _(e):
        n = Tally(lambda k: e.tensor_tensor(spare[:, 32 + k:33 + k], ones[:, 0:1], ones[:, 1:2], ALU.mult))

        def add_squares(s):
            e.wait_ge(sq_ready, n.up(sq_ready))
            e.wait_ge(sq_used, n.now(sq_used))
            n.up(sq_used)
            e.tensor_tensor(ssum[:, :], ssum[:, :], sq[s][:, :], ALU.add).then_inc(sq_used, 1)

        def clear(ready):
            e.wait_ge(ready, n.up(ready))
            n.pause()
            e.memset(ssum[:, :], 0.0).then_inc(ssum_zero, 1)

        def pre():
            n.up(hh_ready, DT), n.up(sq_ready, DT), n.up(sq_used, DT)

        def result():
            e.wait_ge(ssum_zero, n.up(ssum_zero))
            n.pause()
            with n.loop(e, DT // 2, SQUARED):
                add_squares(0)
                add_squares(1)
            clear(cols_ready)

        def ffn():
            pre()
            for c in range(CH):
                with n.loop(e, FC, HIDDEN) as j:
                    e.wait_ge(silu_ready, n.up(silu_ready))
                    e.tensor_tensor(actr[:, :], act[:, :], rstd[:, :], ALU.mult).then_inc(silur_ready, 1)
                    e.wait_ge(hidh_ready, n.up(hidh_ready))
                    e.tensor_tensor(tile(hidl, j), hid[:, :], tile(hidh, j).bitcast(F32), ALU.subtract).then_inc(hidl_ready, 1)
            result()

        def queries(t0, T, nl, before=0):
            if before:
                e.wait_ge(gla_t, n.now(gla_t, T_SB))
            e.wait_ge(dec_a, n.up(dec_a, D_E))
            q = qk[:, 0:PR, bass.ds(t0, T)]
            e.tensor_tensor(qf[:, :, 0:nl + 1, 0:T], dec[:, :, 0:nl + 1, 0:T],
                            q.unsqueeze(2).broadcast_to([P, PR, nl + 1, T]), ALU.mult).then_inc(queries_ready, 1)
            if before:
                e.wait_ge(gla_t, n.now(gla_t, T_O))
            e.tensor_tensor(qe[:, :, 0:T], q, eb[:, :, bass.ds(t0, T)], ALU.mult).then_inc(queries_ready, 1)
            n.up(queries_ready, 2), n.up(gla_t, before)

        def mixer(l):
            pre()
            e.wait_ge(s_stored, n.now(s_stored))
            n.up(s_stored, 32)
            n.pause()
            e.memset(xlp[:, 0:CW - 1], 0.0)
            e.memset(S[:, :, :], 0.0).then_inc(s_zero, 1)
            e.wait_ge(ssum_zero, n.up(ssum_zero))
            n.pause()
            with n.loop(e, LT, LRU_TILE) as i:
                k = l * LT + i
                e.wait_ge(lru_v, n.now(lru_v))
                e.tensor_copy(xls[:, :, 0:CW - 1], stc[:, bass.ds(k, 1), :, :].rearrange("p o b t -> p (o b) t")).then_inc(lru_p, 1)
                e.wait_ge(lru_a, n.now(lru_a, A_I))
                e.tensor_tensor(ig[:, :], ig[:, :], xc[:, :], ALU.mult).then_inc(lru_p, 1)
                e.wait_ge(lru_v, n.now(lru_v, V_H))
                out = tile(state_out, k)
                e.tensor_copy(out[:, O_CP:O_CS], xlp[:, SEQ:XP])
                e.tensor_copy(out[:, O_CS:O_HP].rearrange("p (b t) -> p b t", t=CW - 1), xls[:, :, NS:XS])
                e.tensor_copy(out[:, O_HP:O_HS], tau[:, SEQ - 1:SEQ])
                e.tensor_copy(out[:, O_HS:NST], tau[:, SEQ:NT].rearrange("p (b t) -> p b t", t=NS)[:, :, NS - 1])\
                    .then_inc(lru_p, 1)
                e.wait_ge(lru_v, n.now(lru_v, V_O))
                e.tensor_tensor(sq[0][:, :], tile(lruo, i), tile(lruo, i), ALU.mult).then_inc(sq_ready, 1)
                add_squares(0)
                n.up(lru_v, LRU_TILE["lru_v"]), n.up(lru_a, LRU_TILE["lru_a"]), n.up(lru_p, LRU_TILE["lru_p"])
            e.wait_ge(eb_ready, n.up(eb_ready))
            queries(0, C, 5)
            with n.loop(e, NC_ - 1, CHUNK) as c:
                queries((c + 1) * C, C, 5, CHUNK["gla_t"])
            queries(SEQ, NB * NS, 1, CHUNK["gla_t"])
            n.up(gla_t, SAMPLE["gla_t"])
            clear(mix_cols)
            for k in range(DT):
                e.wait_ge(hh_ready, n.up(hh_ready))
                e.tensor_tensor(hl[:, k, :], (l1, l2)[k % 2][:, :], hh[:, k, :].bitcast(F32), ALU.subtract).then_inc(hl_ready, 1)
            result()

        e.memset(ones[:, :], 1.0)
        for k, width in enumerate((D, DL, DV)):
            e.memset(means[:, k:k + 1], 1.0 / width)
        e.memset(qkvs[:, 0:PR], DK ** -0.5)
        e.memset(qkvs[:, PR:], 1.0)
        e.memset(epsc[:, :], EPS)
        e.memset(tinyc[:, :], TINY)
        e.memset(sc[:, :, :], 0.0)
        e.memset(scs[:, :, :], 0.0)
        e.memset(ssum[:, :], 0.0).then_inc(ssum_zero, 1)
        e.memset(dcol[:, :], 1.0).then_inc(setup_p, 1)
        e.wait_ge(setup_p, 1)
        with n.loop(e, L, LAYER) as l:
            ffn()
            mixer(l)
            ffn()



def layouts(x_prompt, x_sample, state_lru_h, state_lru_conv, state_gla, norm_pre, norm_post, w_ffn_gate, w_ffn_up,
            w_ffn_down, w_in, conv_w, conv_b, lru_wa, lru_ba, lru_wx, lru_bx, lru_lambda, lru_norm, gla_w_gate,
            gla_b_gate, gla_norm, w_out):
    import numpy as np
    f = np.float32

    def units(w):
        *lead, K, N = w.shape
        w = w.reshape(*lead, K // P, P, N // P, P)
        k = len(lead)
        return w.transpose(*range(k), k + 2, k + 1, k, k + 3).reshape(*lead, N // P, P, K)

    def vec(v):
        return v.reshape(L, -1, P).transpose(2, 0, 1)

    x = np.concatenate([x_prompt.reshape(SEQ, D), x_sample.reshape(NB * NS, D)])
    gu = np.stack([units(w_ffn_gate), units(w_ffn_up)], axis=3)
    down = units(w_ffn_down.reshape(L, 2, CH, FC * P, D))
    wi = units(w_in[:, :, :20 * P])
    order = [t for i in range(LT) for t in (i, LT + i, 2 * LT + 2 * i, 2 * LT + 2 * i + 1)] + list(range(4 * LT, 20))
    gates = np.zeros((L, LT, P, 2, P), f)
    for g, w in enumerate((lru_wa, lru_wx)):
        for b in range(8):
            r = slice(64 * (b % 2), 64 * (b % 2) + 64)
            gates[:, b // 2, r, g, r] = w[:, b]
    par = np.concatenate([vec(norm_pre.reshape(L, -1)), vec(norm_post.reshape(L, -1)), vec(conv_w.reshape(L, -1)),
                          vec(conv_b), vec(lru_ba), vec(lru_bx), vec(lru_lambda), vec(lru_norm), vec(gla_b_gate),
                          vec(gla_norm)], axis=2)
    s, t = np.arange(C)[:, None], np.arange(C)[None, :]
    masks = np.zeros((P, 6, C), f)
    sign = np.zeros((P, len(LEVELS), C), f)
    for v, m in enumerate(LEVELS):
        ok = (s // (2 * m) == t // (2 * m)) & (s % (2 * m) < m) & (t % (2 * m) >= m)
        masks[:, v, :C // 2] = ok[:, (np.arange(C) % (2 * m)) >= m]
        sign[:, v, :] = np.where(t % (2 * m) >= m, 1.0, -1.0)
    masks[:, 5, :] = (s // 4 == t // 4) & (s <= t)
    cont = np.ones((P, NT), f)
    cont[:, 0:SEQ:C] = 0
    cont[:, SEQ:NT:NS] = 0
    return {
        "xT": x.reshape(NT, DT, P).transpose(2, 1, 0),
        "w_gu": gu.reshape(-1, P, D),
        "w_d": down.reshape(-1, P, FC * P),
        "w_in": wi[:, order].reshape(-1, P, D),
        "w_gd": w_in[:, :, 20 * P:].reshape(L, DT, P, RANK).transpose(0, 2, 1, 3).reshape(L, P, DT * RANK),
        "w_g2": gla_w_gate,
        "w_ax": gates.reshape(L * LT, P, 2 * P),
        "w_out": units(w_out).reshape(-1, P, D),
        "par": par.reshape(P, L * NPAR),
        "st_h": state_lru_h.reshape(L, NB, LT, P).transpose(3, 0, 2, 1).reshape(P, L * LT, NB),
        "st_conv": state_lru_conv.reshape(L, NB, CW - 1, LT, P).transpose(4, 0, 3, 1, 2).reshape(P, L * LT, NB, CW - 1),
        "st_gla": state_gla.reshape(L, NB, PR, P, DV).transpose(0, 3, 1, 2, 4),
        "ident": np.eye(P, dtype=f), "masks": masks, "sign": sign,
        "seqmask": np.repeat(np.eye(NB, dtype=f), NS, axis=0), "cont": cont,
    }


OUTPUTS = {"yT": (P, DT, NT), "states": (P, L * LT, NST), "gla_p": (L, P, PR, DV), "gla_s": (L, P, NB, PR, DV)}


def kernel(**inputs):
    import numpy as np
    import concourse.bacc as bacc
    from concourse.bass_utils import run_bass_kernel_spmd

    arrays = {f"in_{k}": np.ascontiguousarray(v) for k, v in layouts(**{k: np.asarray(v) for k, v in inputs.items()}).items()}
    nc = bacc.Bacc("TRN2", target_bir_lowering=False, num_devices=1)
    a = {k[3:]: nc.dram_tensor(k, v.shape, mybir.dt.from_np(v.dtype), kind="ExternalInput").ap() for k, v in arrays.items()}
    a["yT_in"] = a["xT"]
    for k, shape in OUTPUTS.items():
        a[k] = nc.dram_tensor(f"out_{k}", shape, F32, kind="ExternalOutput").ap()
    build(nc, a)
    r = run_bass_kernel_spmd(nc, [arrays], core_ids=[0]).results[0]
    y = r["out_yT"].transpose(2, 1, 0).reshape(NT, D)
    st = r["out_states"].reshape(P, L, LT, NST).transpose(1, 3, 2, 0).reshape(L, NST, DL)
    return (y[:SEQ].reshape(1, SEQ, D), y[SEQ:].reshape(NB, NS, D),
            st[:, O_HP:O_HS], st[:, O_CP:O_CS].reshape(L, 1, CW - 1, DL),
            r["out_gla_p"].transpose(0, 2, 1, 3).reshape(L, 1, HEADS, DK, DV),
            st[:, O_HS:], st[:, O_CS:O_HP].reshape(L, NB, CW - 1, DL),
            r["out_gla_s"].transpose(0, 2, 3, 1, 4).reshape(L, NB, HEADS, DK, DV))
```

```python
from contextlib import ExitStack, contextmanager

import concourse.bass as bass
from concourse import mybir

F32 = mybir.dt.float32
F32R = mybir.dt.float32r
U8 = mybir.dt.uint8
ALU = mybir.AluOpType
ACT = mybir.ActivationFunctionType

P = 128
D = 1024
DT = D // P
L = 2
SEQ = 512
NB, NS = 8, 8
NT = SEQ + NB * NS
H = NT // 2
FF = 2816
FT = FF // P
LAG = 3
CH = 2
FC = FT // CH
DL = 512
LT = DL // P
CW = 4
XP = SEQ + CW - 1
XS = NS + CW - 1
XA = XP + NB * XS
HEADS = 4
DK, DV = 64, 128
PR = 2
RANK = 16
C = 128
NC_ = SEQ // C
LEVELS = [4, 8, 16, 32, 64]
EPS = 1e-6
TC = 96
NTC = NT // TC
NSL = 3 + len(LEVELS)
LRU_C, NORMALIZER = 8.0, 16.0
GK_MIN = -40.0
TINY = 1e-18

PRE, POST, CONVW, CONVB, BA, BX, LAM, LNORM, GB, GNORM, NPAR = 0, 24, 48, 64, 68, 72, 76, 80, 84, 86, 87
O_CP, O_CS, O_HP, O_HS, NST = 0, 3, 27, 28, 36
V_XC, V_D, V_ONE, V_B, V_AH, V_BS, V_A0, V_H, V_O = 4, 5, 6, 7, 8, 9, 10, 11, 12
A_R, A_I, A_TAU, A_AA, A_L1, A_L2, A_M, A_GE = range(1, 9)
P_HEAD, P_IX, P_ST = 1, 2, 3
G_SC, G_S, G_KEM, G_S1, G_S2 = 1, 2, 2, 3, 4
D_N, D_E, D_VC = 1, 2, 3
A_VT, A_KET, A_O = 1, 2, 3
T_VT, T_KE, T_SA, T_SB, T_O, T_SU = range(1, 7)


class Tally:

    def __init__(self, small_step=None):
        self.small_step, self.count, self.open, self.pauses = small_step, {}, [], 0

    def pause(self):
        if self.small_step:
            self.small_step(self.pauses)
            self.pauses += 1

    def now(self, sem, more=0):
        v = self.count.get(sem.name, 0) + more
        for reg, rises in self.open:
            if rises.get(sem.name, 0):
                v = reg * rises[sem.name] + v
        return v

    def up(self, sem, k=1):
        self.count[sem.name] = self.count.get(sem.name, 0) + k
        return self.now(sem)

    @contextmanager
    def loop(self, eng, times, rises):
        before = dict(self.count)
        with eng.Fori(0, times) as i:
            self.open.append((i, rises))
            yield i
            self.open.pop()
        rise = {k: v - before.get(k, 0) for k, v in self.count.items() if v != before.get(k, 0)}
        assert all(rises.get(k) == v for k, v in rise.items()), f"a loop raises {rise}, said {rises}"
        for k, v in rise.items():
            self.count[k] = before.get(k, 0) + v * times


PAIR = {f"{k}{s}": 1 for k in ("lo_ready", "hi_ready", "unit_done", "out_taken") for s in (0, 1)}
PAIR |= {"raw_landed0": 16, "raw_landed1": 16}
HIDDEN = PAIR | {"silu_ready": 1, "silur_ready": 1, "hidh_ready": 1, "hidl_ready": 1}
SQUARED = PAIR | {"sq_ready": 2, "sq_used": 2}
TILES = {"x_ready": 2, "xpart": 2, "hh_ready": 2, "hl_ready": 2, "sq_ready": 2, "sq_used": 2}
LRU_TILE = {k: 2 * v for k, v in PAIR.items()} | {"gates_landed": 16, "lru_v": 12, "lru_a": 8, "lru_p": 3, "lru_t": 1, "sq_ready": 1, "sq_used": 1}
CHUNK = {"gla_v": 2, "gla_a": 3, "gla_t": 6, "placed": 5, "dec_v": 2, "dec_a": 3, "keys_ready": 1, "queries_ready": 2}
SAMPLE = {"gla_v": 4, "gla_a": 3, "gla_t": 6, "placed": 1, "dec_v": 2, "dec_a": 3, "keys_ready": 1, "queries_ready": 2}
UNITS = 2 * (FT * 2 + CH * DT) + 20 + DT
LAYER = {f"{k}{s}": UNITS // 2 for k in ("lo_ready", "hi_ready", "unit_done") for s in (0, 1)}
LAYER |= {"out_taken0": UNITS // 2, "out_taken1": UNITS // 2 + 1, "raw_landed0": 8 * UNITS, "raw_landed1": 8 * UNITS}
LAYER |= {k: LT * LRU_TILE[k] for k in ("gates_landed", "lru_v", "lru_a", "lru_p", "lru_t")}
LAYER |= {k: NC_ * CHUNK[k] + SAMPLE[k] for k in CHUNK}
LAYER |= {"eb_ready": 1}
LAYER |= {"x_ready": 3 * DT, "xpart": 3 * DT, "hh_ready": 4 * DT, "hl_ready": 4 * DT}
LAYER |= {"sq_ready": 6 * DT + LT, "sq_used": 6 * DT + LT, "ssum_zero": 7, "small_landed": 32}
LAYER |= {"cols_ready": 6, "gate_ready": 2, "std_ready": 7, "inv_ready": 7, "diag_ready": 6, "bcast_ready": 6, "rstd_ready": 3}
LAYER |= {"silu_ready": 2 * FT, "silur_ready": 2 * FT, "hidh_ready": 2 * FT, "hidl_ready": 2 * FT}
LAYER |= {"gdh_ready": 1, "gdl_ready": 1, "gdp_ready": 1, "logit_ready": 1, "gk_v": 4, "gk_a": 3}
LAYER |= {"s_zero": 1, "odd_out": 1, "s0_landed": 16, "s_stored": 32, "head_sq": 1, "mix_cols": 1, "mix_t": 5, "mix_d": 5, "mix_v": 16}
SQ_BEFORE_S0 = 3 * DT + LT


def halves(ap):
    return ap.rearrange("p (a n) -> p a n", a=2)


def build(nc, a):
    ctx = ExitStack()
    with ctx:
        program(nc, a, ctx)


def program(nc, a, ctx):
    cursor = [(nc.sbuf_base + 31) // 32 * 32]

    def sb(name, shape, dt=F32):
        size = 1 if dt == U8 else 4
        for n in shape[1:]:
            size *= n
        t = nc.alloc_sbuf_tensor_at(name, shape, dt, offset=cursor[0])
        cursor[0] += (size + 31) // 32 * 32
        assert cursor[0] <= nc.sbuf_usable_end, (name, cursor[0])
        return t

    xT = sb("xT", [P, DT, NT])
    operand_at = cursor[0]
    hh = sb("hh", [P, DT, NT], F32R)
    hl = sb("hl", [P, DT, NT], F32R)
    raw = [sb(f"raw{s}", [P, FC * P]) for s in (0, 1)]
    wh = [sb(f"wh{s}", [P, FC * P], F32R) for s in (0, 1)]
    wl = [sb(f"wl{s}", [P, FC * P], F32R) for s in (0, 1)]
    par = sb("par", [P, L * NPAR])
    ph = sb("ph", [P, L * 24])
    sp8 = sb("sp8", [P, L * LT])
    nsp8 = sb("nsp8", [P, L * LT])
    spt = sb("spt", [P, 6, L * LT])
    ones = sb("ones", [P, P])
    means = sb("means", [P, 3])
    spare = sb("spare", [P, 64])
    qkvs = sb("qkvs", [P, 2 * PR + HEADS])
    epsc = sb("epsc", [P, 1])
    tinyc = sb("tinyc", [P, 1])
    rstd = sb("rstd", [P, NT])
    ident = sb("ident", [P, P])
    dcol = sb("dcol", [P, 5 * NTC])
    dinv = sb("dinv", [P, 5 * NTC])
    diag = [sb(f"diag{s}", [P, NTC, TC]) for s in (0, 1)]
    ssum = sb("ssum", [P, NT])
    sq = [sb(f"sq{s}", [P, NT]) for s in (0, 1)]
    tmp = [sb(f"tmp{s}", [P, NT]) for s in (0, 1)]
    state_out = sb("state_out", [P, L * LT, NST])
    sth = sb("sth", [P, L * LT, NB])
    stc = sb("stc", [P, L * LT, NB, CW - 1])
    wgd = sb("wgd", [P, DT * RANK])
    wgdh = sb("wgdh", [P, DT * RANK], F32R)
    wgdl = sb("wgdl", [P, DT * RANK], F32R)
    wg2 = sb("wg2", [RANK, PR * P])
    gates = sb("gates", [P, 2 * P])
    masks = sb("masks", [P, 6, C], U8)
    sign = sb("sign", [P, len(LEVELS), C])
    seqmask = sb("seqmask", [NB * NS, NB])
    cont = sb("cont", [P, NT])
    sc = sb("sc", [P, HEADS, C])
    scs = sb("scs", [NB * NS, HEADS, NB * NS])
    S = sb("S", [P, PR, DV])
    result_at = cursor[0]
    yT = sb("yT", [P, DT, NT])
    shared_at = cursor[0]
    hidh = sb("hidh", [P, FC, NT], F32R)
    hidl = sb("hidl", [P, FC, NT], F32R)
    gate = sb("gate", [P, NT])
    act = sb("act", [P, NT])
    actr = sb("actr", [P, NT])
    hid = sb("hid", [P, NT])
    cursor[0] = shared_at
    qkv = sb("qkv", [P, 2 * PR + HEADS, NT])
    qk, vT = qkv[:, 0:2 * PR, :], qkv[:, 2 * PR:, :]
    bc = sb("bc", [P, PR, NT])
    gT = sb("gT", [P, HEADS, NT])
    oT = sb("oT", [P, HEADS, NT])
    lruo = sb("lruo", [P, LT, NT])
    gd = sb("gd", [RANK, NT])
    xlp = sb("xlp", [P, XA])
    l1 = sb("l1", [P, NT])
    l2 = sb("l2", [P, NT])
    cursor[0] = result_at
    cv = [sb(f"cv{s}", [P, XA - CW + 1]) for s in (0, 1)]
    xc = sb("xc", [P, NT])
    rg = sb("rg", [P, NT])
    ig = sb("ig", [P, NT])
    tau = sb("tau", [P, NT])
    aa = sb("aa", [P, NT])
    assert cursor[0] <= shared_at
    cursor[0] = result_at
    S0 = sb("S0", [P, NB, PR, DV])
    dec_at = cursor[0]
    dec = sb("dec", [P, PR, NSL, C])
    cursor[0] = dec_at
    kem = sb("kem", [NB * NS, NB, PR * P])
    assert cursor[0] <= shared_at
    cursor[0] = operand_at
    eb = sb("eb", [P, PR, NT])
    qe = sb("qe", [P, PR, C])
    qf = sb("qf", [P, PR, NSL - 2, C])
    kf = sb("kf", [P, PR, NSL - 1, C])
    vc = sb("vc", [P, HEADS, C])
    vt = sb("vt", [P, HEADS * DV])
    ket = sb("ket", [P, PR * P])
    assert cursor[0] <= operand_at + 2 * DT * NT * 4
    maskf = qk[:, :, :].rearrange("p a n -> p (a n)")[:, 0:6 * C].rearrange("p (v n) -> p v n", v=6)
    xls = xlp[:, XP:XA].rearrange("p (b t) -> p b t", t=XS)

    psU = ctx.enter_context(nc.psum_tensor("psU", [P, 4, 512], F32))
    psM = ctx.enter_context(nc.psum_tensor("psM", [P, 4, 512], F32))

    def sem(name):
        return ctx.enter_context(nc.semaphore(name))

    x_landed = [sem(f"x_landed{m}") for m in range(DT)]
    par_landed = sem("par_landed")
    const_landed = sem("const_landed")
    raw_landed, hi_ready, lo_ready, unit_done, out_taken = (
        [sem(f"{k}{s}") for s in (0, 1)] for k in ("raw_landed", "hi_ready", "lo_ready", "unit_done", "out_taken"))
    small_landed = sem("small_landed")
    gates_landed = sem("gates_landed")
    setup_v, setup_a, setup_p = sem("setup_v"), sem("setup_a"), sem("setup_p")
    x_ready = sem("x_ready")
    xpart = sem("xpart")
    hh_ready, hl_ready = sem("hh_ready"), sem("hl_ready")
    sq_ready, sq_used = sem("sq_ready"), sem("sq_used")
    ssum_zero = sem("ssum_zero")
    cols_ready, std_ready, inv_ready, diag_ready, bcast_ready, rstd_ready = (
        sem(k) for k in ("cols_ready", "std_ready", "inv_ready", "diag_ready", "bcast_ready", "rstd_ready"))
    gate_ready = sem("gate_ready")
    silu_ready, silur_ready = sem("silu_ready"), sem("silur_ready")
    hidh_ready, hidl_ready = sem("hidh_ready"), sem("hidl_ready")
    gdh_ready, gdl_ready, gdp_ready, logit_ready = (sem(k) for k in ("gdh_ready", "gdl_ready", "gdp_ready", "logit_ready"))
    lru_v, lru_a, lru_p, lru_t = (sem(f"lru_{k}") for k in "vapt")
    gk_v, gk_a = sem("gk_v"), sem("gk_a")
    gla_v, gla_a, gla_t = (sem(f"gla_{k}") for k in "vat")
    eb_ready = sem("eb_ready")
    dec_v, dec_a = sem("dec_v"), sem("dec_a")
    keys_ready, queries_ready = sem("keys_ready"), sem("queries_ready")
    odd_out = sem("odd_out")
    placed = sem("placed")
    s_zero, s0_landed, s_stored = sem("s_zero"), sem("s0_landed"), sem("s_stored")
    head_sq, mix_cols, mix_t, mix_d, mix_v = (sem(k) for k in ("head_sq", "mix_cols", "mix_t", "mix_d", "mix_v"))
    y_stored = sem("y_stored")

    block = ctx.enter_context(nc.Block())

    def tile(t, m):
        return t[:, m, :] if isinstance(m, int) else t[:, bass.ds(m, 1), :].rearrange("p o n -> p (o n)")

    def col(t, k):
        return t[:, bass.ds(k, 1)]

    def dram(t, k):
        return t[bass.ds(k, 1), :, :].rearrange("o p n -> (o p) n")

    @block.sync
    def _(e):
        n = Tally()

        def load(s, width, src):
            e.wait_ge(lo_ready[s], n.now(lo_ready[s]))
            n.up(lo_ready[s])
            e.dma_start(raw[s][:, 0:width], src).then_inc(raw_landed[s], 16)

        def pairs(times, width, src, first):
            with n.loop(e, times, PAIR) as j:
                for s in (0, 1):
                    load(s, width, dram(src, first + j * 2 + s))

        def ffn(l, f):
            for c in range(CH):
                pairs(FC, D, a["w_gu"], (l * 2 + f) * (CH * FC * 2) + c * FC * 2)
                pairs(DT // 2, FC * P, a["w_d"], (l * 2 + f) * (CH * DT) + c * DT)

        e.dma_start(par[:], a["par"]).then_inc(par_landed, 16)
        for m in range(DT):
            e.dma_start(yT[:, m, :], a["xT"][:, m, :]).then_inc(x_landed[m], 16)
        for t, src in ((sth, "st_h"), (stc, "st_conv"), (ident, "ident"), (maskf, "masks"), (sign, "sign"),
                       (seqmask, "seqmask"), (cont, "cont")):
            e.dma_start(maskf if t is maskf else t[:], a[src]).then_inc(const_landed, 16)

        with n.loop(e, L, LAYER) as l:
            e.wait_ge(logit_ready, n.now(logit_ready))
            n.up(logit_ready)
            e.dma_start(wgd[:, :], dram(a["w_gd"], l)).then_inc(small_landed, 16)
            e.dma_start(wg2[:, :], dram(a["w_g2"], l)).then_inc(small_landed, 16)
            ffn(l, 0)
            with n.loop(e, LT, LRU_TILE) as i:
                e.wait_ge(lru_t, n.now(lru_t))
                n.up(lru_t)
                e.dma_start(gates[:, :], dram(a["w_ax"], l * LT + i)).then_inc(gates_landed, 16)
                for u in range(4):
                    load(u % 2, D, dram(a["w_in"], l * 20 + i * 4 + u))
            pairs(2, D, a["w_in"], l * 20 + 4 * LT)
            e.wait_ge(lru_v, n.up(lru_v, LT * LRU_TILE["lru_v"]))
            e.wait_ge(lru_p, n.up(lru_p, LT * LRU_TILE["lru_p"]))
            e.wait_ge(sq_used, n.up(sq_used, SQ_BEFORE_S0))
            e.dma_start(S0[:, :, :, :], a["st_gla"][bass.ds(l, 1), :, :, :, :].rearrange("o p b r v -> (o p) b r v")).then_inc(s0_landed, 16)
            for s in (0, 1):
                load(s, D, dram(a["w_out"], l * DT + s))
            e.wait_ge(gla_v, n.up(gla_v, NC_ * CHUNK["gla_v"]))
            e.dma_start(a["gla_p"][bass.ds(l, 1), :, :, :].rearrange("o p r v -> (o p) r v"), S[:, :, :]).then_inc(s_stored, 16)
            e.wait_ge(gla_v, n.up(gla_v, SAMPLE["gla_v"]))
            e.dma_start(a["gla_s"][bass.ds(l, 1), :, :, :, :].rearrange("o p b r v -> (o p) b r v"), S0[:, :, :, :]).then_inc(s_stored, 16)
            n.up(sq_used, LAYER["sq_used"] - SQ_BEFORE_S0)
            pairs(DT // 2 - 1, D, a["w_out"], l * DT + 2)
            ffn(l, 1)
        for m in range(DT):
            e.wait_ge(x_ready, DT * 3 * L + m + 1)
            e.dma_start(a["yT"][:, m, :], xT[:, m, :]).then_inc(y_stored, 16)
        e.dma_start(a["states"], state_out[:, :, :]).then_inc(y_stored, 16)
        e.wait_ge(y_stored, 16 * (DT + 1))
        e.wait_ge(s_stored, 32 * L)

    @block.tensor
    def _(e):
        n = Tally(lambda k: e.matmul(psM[:, 3, 511:512], ones[:, :], means[:, 0:1], start=True, stop=True))

        def step(out, kt, KT, w_h, w_l, M, xh, xl):
            for part, (w, x) in enumerate([(w_h, xh), (w_h, xl), (w_l, xh)]):
                for h in (0, 1):
                    mm = e.matmul(out[h], w[:, kt * M:(kt + 1) * M], x[:, kt, h * H:(h + 1) * H],
                                  start=(kt == 0 and part == 0), stop=(kt == KT - 1 and part == 2))
            return mm

        def slot(s):
            return [psU[:, 2 * s + h, 0:H] for h in (0, 1)]

        def open_unit(s):
            e.wait_ge(lo_ready[s], n.up(lo_ready[s]))
            e.wait_ge(out_taken[s], n.now(out_taken[s]))
            n.up(out_taken[s]), n.up(unit_done[s])

        def unit(s, KT, xh, xl, ready=(), then=None):
            open_unit(s)
            for kt in range(KT):
                for r in ready:
                    e.wait_ge(r, n.up(r))
                mm = step(slot(s), kt, KT, wh[s], wl[s], P, xh, xl)
                if kt == KT - 1:
                    mm.then_inc(unit_done[s], 1)
                if then is not None and kt == 3:
                    then()

        def first_pair(gate_rank=False, before=None):
            open_unit(0)
            if gate_rank:
                e.wait_ge(gdl_ready, n.up(gdl_ready))
                e.wait_ge(out_taken[1], n.now(out_taken[1]))
                n.up(out_taken[1])
            else:
                open_unit(1)
            for kt in range(DT + (0 if gate_rank else LAG)):
                if before is not None:
                    before(kt)
                if kt < DT:
                    e.wait_ge(hh_ready, n.up(hh_ready))
                    e.wait_ge(hl_ready, n.up(hl_ready))
                    if gate_rank:
                        mm = step([psU[0:RANK, 2 + h, 0:H] for h in (0, 1)], kt, DT, wgdh, wgdl, RANK, hh, hl)
                        if kt == DT - 1:
                            mm.then_inc(gdp_ready, 1)
                    mm = step(slot(0), kt, DT, wh[0], wl[0], P, hh, hl)
                    if kt == DT - 1:
                        mm.then_inc(unit_done[0], 1)
                if kt >= LAG and not gate_rank:
                    mm = step(slot(1), kt - LAG, DT, wh[1], wl[1], P, hh, hl)
            if not gate_rank:
                mm.then_inc(unit_done[1], 1)

        def pair(KT, xh, xl, ready=()):
            unit(0, KT, xh, xl, ready)
            unit(1, KT, xh, xl)

        def columns(src, k, at, first, last, bank=psM[:, 0, :]):
            for t in range(NTC):
                mm = e.matmul(bank[0:TC, at + t:at + t + 1], src[:, t * TC:(t + 1) * TC], means[:, k:k + 1],
                              start=(first and t == 0), stop=last, skip_group_check=True)
            return mm

        def spread():
            e.wait_ge(diag_ready, n.up(diag_ready))
            for h in (0, 1):
                mm = e.matmul(psM[:, 1 + h, 0:H], ones[0:TC, :], diag[0][0:TC, 3 * h:3 * h + 3, :], start=True, stop=True)
            mm.then_inc(bcast_ready, 1)

        def statistics():
            e.wait_ge(sq_used, n.up(sq_used, DT - 1))
            columns(ssum, 0, 0, True, False).then_inc(sq_used, 1)
            n.up(sq_used)
            e.wait_ge(sq_ready, n.up(sq_ready, DT))
            columns(sq[1], 0, 0, False, True).then_inc(cols_ready, 1)

        def post_norm():
            statistics()
            spread()

        def ffn():
            first_pair(before=lambda kt: statistics() if kt == DT else None)
            spread()
            pair(DT, hh, hl)
            for c in range(CH):
                with n.loop(e, FC - 2 * (c == 0), PAIR):
                    pair(DT, hh, hl)
                pair(FC, hidh, hidl, (hidl_ready,))
                with n.loop(e, DT // 2 - 1, PAIR):
                    pair(FC, hidh, hidl)
            post_norm()

        def decays_next():
            n.up(dec_a, D_VC), n.up(keys_ready), n.up(queries_ready, 2)

        def chunk(T, nl, sample=False):
            up = CHUNK if not sample else SAMPLE
            e.wait_ge(dec_a, n.now(dec_a))
            for h in range(HEADS):
                mm = e.transpose(psU[:, 0, h * DV:(h + 1) * DV], vc[:, h, :], ident[:, :])
            mm.then_inc(gla_t, 1)
            e.wait_ge(keys_ready, n.now(keys_ready))
            for pr in range(PR):
                mm = e.transpose(psU[:, 1, pr * P:(pr + 1) * P], kf[:, pr, nl + 1, :], ident[:, :])
            mm.then_inc(gla_t, 1)
            e.wait_ge(queries_ready, n.now(queries_ready, -1))
            e.wait_ge(gla_a, n.now(gla_a))
            narrow = LEVELS[:min(nl, 4)]
            for pr in range(PR):
                for v, m in enumerate(narrow):
                    for odd in (0, 1):
                        rows = slice(DK * odd, DK * odd + DK)
                        q = qf[rows, pr, 1 + v, 0:T].rearrange("p (b m) -> p b m", m=2 * m)[:, :, m:2 * m]
                        mm = e.matmul(psM[:, 2 + odd, pr * 256 + v * (T // 2):pr * 256 + (v + 1) * (T // 2)],
                                      kf[rows, pr, v, :], q, start=(pr == 0 and v == 0), stop=True, skip_group_check=True)
            mm.then_inc(gla_t, 1)
            for pr in range(PR):
                for odd in (0, 1):
                    rows = slice(DK * odd, DK * odd + DK)
                    mm = e.matmul(psM[:, odd, pr * 256:pr * 256 + T], kf[rows, pr, nl, :], qf[rows, pr, 0, 0:T],
                                  start=(pr == 0), stop=True, skip_group_check=True)
                    if nl == 5:
                        mm = e.matmul(psM[:, odd, pr * 256 + T:pr * 256 + T + T // 2], kf[rows, pr, 4, :],
                                      qf[rows, pr, 5, T // 2:T], start=False, stop=True, skip_group_check=True)
            mm.then_inc(gla_t, 1)
            e.wait_ge(gla_a, n.now(gla_a, A_KET))
            e.wait_ge(queries_ready, n.now(queries_ready))
            e.wait_ge(gla_v, n.now(gla_v, G_SC))
            if sample:
                e.wait_ge(s0_landed, n.up(s0_landed, 16))
            for odd in (1, 0):
                for pr in range(PR):
                    h = 2 * pr + odd
                    mm = e.matmul(psM[:, 2 + odd, pr * C:pr * C + T], vt[0:T, h * DV:(h + 1) * DV],
                                  (scs if sample else sc)[0:T, 2 * odd + pr, 0:T], start=(pr == 0), stop=False, skip_group_check=True)
                if odd and sample:
                    mm.then_inc(odd_out, 1)
            if sample:
                e.wait_ge(odd_out, n.up(odd_out))
            for pr in range(PR):
                for b in range(NB if sample else 1):
                    for odd in (0, 1):
                        rows = slice(DK * odd, DK * odd + DK)
                        state, at, width = (S0[rows, b, pr, :], b * NS, NS) if sample else (S[rows, pr, :], 0, T)
                        mm = e.matmul(psM[:, 2 + odd, pr * C + at:pr * C + at + width], state, qe[rows, pr, at:at + width],
                                      start=False, stop=True, skip_group_check=True)
            mm.then_inc(gla_t, 1)
            if not sample:
                for h in range(HEADS):
                    rows = slice(DK * (h % 2), DK * (h % 2) + DK)
                    mm = e.matmul(psU[rows, 2, (h // 2) * DV:(h // 2 + 1) * DV], ket[0:T, h * DK:(h + 1) * DK],
                                  vt[0:T, h * DV:(h + 1) * DV], start=(h < 2), stop=True, skip_group_check=True)
            else:
                e.wait_ge(gla_a, n.now(gla_a, A_O))
                e.wait_ge(gla_v, n.now(gla_v, G_KEM))
                n.pause()
                for b in range(NB):
                    for h in range(HEADS):
                        rows = slice(DK * (h % 2), DK * (h % 2) + DK)
                        at = (b * PR + h // 2) * DV
                        mm = e.matmul(psM[rows, at // 512, at % 512:at % 512 + DV], kem[:, b, h * DK:(h + 1) * DK],
                                      vt[0:T, h * DV:(h + 1) * DV], start=(at % 512 == 0), stop=True, skip_group_check=True)
            mm.then_inc(gla_t, 1)
            for t in (gla_t, gla_v, gla_a):
                n.up(t, up[t.name])
            if not sample:
                decays_next()

        def mixer():
            first_pair(gate_rank=True)
            statistics()

            def lru_tile(first):
                if first:
                    unit(1, DT, hh, hl, then=spread)
                else:
                    pair(DT, hh, hl)
                e.wait_ge(gates_landed, n.up(gates_landed, 16))
                e.wait_ge(lru_v, n.now(lru_v, V_XC))
                e.wait_ge(lru_a, n.now(lru_a))
                n.up(lru_v, LRU_TILE["lru_v"]), n.up(lru_a, LRU_TILE["lru_a"]), n.up(lru_t)
                for g in (0, 1):
                    for h in (0, 1):
                        mm = e.matmul(psM[:, 2 * g + h, 0:H], gates[:, g * P:(g + 1) * P], xc[:, h * H:(h + 1) * H],
                                      start=True, stop=True)
                mm.then_inc(lru_t, 1)
                pair(DT, hh, hl)
            lru_tile(True)
            with n.loop(e, LT - 1, LRU_TILE):
                lru_tile(False)
            e.wait_ge(lru_a, n.now(lru_a))
            for pr in range(PR):
                for h in (0, 1):
                    mm = e.matmul(psM[:, 2 * pr + h, 0:H], wg2[:, pr * P:(pr + 1) * P], gd[:, h * H:(h + 1) * H],
                                  start=True, stop=True)
            mm.then_inc(logit_ready, 1)
            with n.loop(e, 2, PAIR):
                pair(DT, hh, hl)
            e.wait_ge(gk_v, n.up(gk_v, 4))
            for t in out_taken:
                e.wait_ge(t, n.now(t))
            e.wait_ge(sq_used, n.up(sq_used, LT))
            n.up(sq_ready, LT)
            columns(ssum, 1, 0, True, True, psU[:, 3, :])
            n.pause()
            decays_next()
            with n.loop(e, NC_, CHUNK):
                chunk(C, 5)
            chunk(NB * NS, 1, sample=True)
            e.wait_ge(gla_v, n.now(gla_v))
            e.wait_ge(head_sq, n.up(head_sq))
            for h in range(HEADS):
                mm = columns(vT[:, h, :], 2, (1 + h) * NTC, False, True, psU[:, 3, :])
            mm.then_inc(mix_cols, 1)

            def spread_group(g):
                e.wait_ge(mix_d, n.up(mix_d))
                for h in (0, 1):
                    mm = e.matmul(psM[:, 2 * (g % 2) + h, 0:H], ones[0:TC, :], diag[g % 2][0:TC, 3 * h:3 * h + 3, :],
                                  start=True, stop=True)
                mm.then_inc(mix_t, 1)
            spread_group(0)
            spread_group(1)
            first_pair(before=lambda kt: spread_group(kt - LT + 2) if LT <= kt < LT + 3 else None)
            with n.loop(e, DT // 2 - 1, PAIR):
                pair(DT, hh, hl)
            post_norm()

        e.wait_ge(setup_p, 1)
        e.wait_ge(const_landed, 16 * 7)
        with n.loop(e, L, LAYER):
            ffn()
            mixer()
            ffn()

    @block.scalar
    def _(e):
        n = Tally(lambda k: e.activation(spare[0:1, k:k + 1], ones[0:1, 0:1], ACT.Copy))

        def split_hi(s, width):
            if width:
                e.wait_ge(raw_landed[s], n.up(raw_landed[s], 16))
                e.wait_ge(unit_done[s], n.now(unit_done[s]))
                e.activation(wh[s][:, 0:width], raw[s][:, 0:width], ACT.Copy).then_inc(hi_ready[s], 1)

        def done(s, width, pause=False):
            n.up(unit_done[s])
            split_hi(s, width)
            return n.up(out_taken[s])

        def root(cols, bank=psM[:, 0, :]):
            e.activation(dcol[0:TC, 0:cols], bank[0:TC, 0:cols], ACT.Sqrt, bias=epsc[0:TC, :]).then_inc(std_ready, 1)

        def pre(l, stage, after_first=None):
            with n.loop(e, DT // 2, TILES) as i:
                for s in (0, 1):
                    m = i * 2 + s
                    e.wait_ge(x_ready, n.up(x_ready))
                    e.activation(tile(hh, m), tile(xT, m), ACT.Copy, scale=col(par, l * NPAR + (PRE + stage * DT) + m))\
                        .then_inc(hh_ready, 1)
                    if s == 0:
                        e.wait_ge(sq_used, n.now(sq_used))
                        n.pause()
                    e.activation(sq[s][:, :], tile(xT, m), ACT.Square).then_inc(sq_ready, 1)
                n.up(sq_used, 2)
            if after_first is not None:
                done(0, after_first)
            e.wait_ge(cols_ready, n.up(cols_ready))
            root(NTC)

        def result(width, after):
            def body(i, after, last=False):
                e.wait_ge(out_taken[0], done(0, after))
                e.wait_ge(sq_used, n.now(sq_used))
                n.pause()
                e.activation(sq[0][:, :], tile(yT, i * 2), ACT.Square).then_inc(sq_ready, 1)
                n.up(unit_done[1])
                e.wait_ge(out_taken[1], n.up(out_taken[1]))
                n.pause()
                e.activation(sq[1][:, :], tile(yT, i * 2 + 1), ACT.Square).then_inc(sq_ready, 1)
                if not last:
                    split_hi(1, after)
                n.up(sq_used, 2)
            with n.loop(e, DT // 2 - 1, SQUARED) as i:
                body(i, width)
            body(DT // 2 - 1, after, last=True)
            e.wait_ge(cols_ready, n.up(cols_ready))
            root(NTC)
            split_hi(1, after)

        def passing(width):
            done(0, width)
            done(1, width)

        def ffn(l, stage, after):
            if stage == 0:
                e.wait_ge(small_landed, n.up(small_landed, 32))
                e.activation(wgdh[:, :], wgd[:, :], ACT.Copy).then_inc(gdh_ready, 1)
            pre(l, stage, D)
            done(1, D)
            e.wait_ge(gate_ready, n.up(gate_ready))
            e.activation(act[:, :], gate[:, :], ACT.Silu).then_inc(silu_ready, 1)
            e.wait_ge(out_taken[1], n.now(out_taken[1]))
            e.activation(hidh[:, 0, :], hid[:, :], ACT.Copy).then_inc(hidh_ready, 1)
            for c in range(CH):
                def body(j, width):
                    e.wait_ge(out_taken[0], done(0, width))
                    e.activation(act[:, :], gate[:, :], ACT.Silu).then_inc(silu_ready, 1)
                    e.wait_ge(out_taken[1], done(1, width))
                    e.activation(tile(hidh, j), hid[:, :], ACT.Copy).then_inc(hidh_ready, 1)
                first = int(c == 0)
                with n.loop(e, FC - 1 - first, HIDDEN) as j:
                    body(j + first, D)
                body(FC - 1, FC * P)
                if c < CH - 1:
                    with n.loop(e, DT // 2 - 1, PAIR):
                        passing(FC * P)
                    passing(D)
                else:
                    result(FC * P, after)

        def factors(t0, T, nl):
            e.wait_ge(dec_v, n.up(dec_v, 2))
            e.activation(dec[:, :, nl + 1, 0:T], dec[:, :, 0, 0:T], ACT.Exp, scale=-1.0).then_inc(dec_a, 1)
            e.activation(dec[:, :, nl + 2, 0:T], dec[:, :, nl + 2, 0:T], ACT.Exp, scale=-1.0)
            e.wait_ge(dec_a, n.now(dec_a, D_N))
            e.activation(dec[:, :, 0:nl + 1, 0:T], dec[:, :, 0:nl + 1, 0:T], ACT.Exp).then_inc(dec_a, 1)
            n.up(dec_a, D_E)

        def copy_v(t0, T, nl):
            e.activation(vc[:, :, 0:T], vT[:, :, bass.ds(t0, T)], ACT.Copy).then_inc(dec_a, 1)
            n.up(dec_a)

        def chunk(t0, T, up, following=None):
            at = bass.ds(t0, T)
            e.wait_ge(gla_t, n.now(gla_t, T_VT))
            e.activation(vt[0:T, :], psU[0:T, 0, :], ACT.Copy).then_inc(gla_a, 1)
            e.wait_ge(gla_t, n.now(gla_t, T_KE))
            e.activation(ket[0:T, :], psU[0:T, 1, 0:PR * P], ACT.Copy).then_inc(gla_a, 1)
            if following:
                factors(*following)
                copy_v(*following)
            e.wait_ge(gla_t, n.now(gla_t, T_O))
            for odd in (0, 1):
                ins = e.activation(oT[:, :, :].rearrange("p (r o) t -> p r o t", o=2)[:, :, odd, at],
                                   psM[:, 2 + odd, 0:PR * C].rearrange("p (r t) -> p r t", r=PR)[:, :, 0:T], ACT.Copy)
            ins.then_inc(gla_a, 1)
            n.up(gla_t, up["gla_t"]), n.up(gla_a, up["gla_a"])

        def mixer(l):
            pre(l, 1)
            n.up(out_taken[1])
            with n.loop(e, LT, LRU_TILE) as i:
                k = l * LT + i
                pk = l * NPAR + i
                done(0, D)
                yl_taken = done(1, D)
                n.up(unit_done[0]), n.up(out_taken[0])
                e.wait_ge(lru_t, n.up(lru_t))
                e.activation(halves(rg[:, :]), psM[:, 0:2, 0:H], ACT.Sigmoid, bias=col(par, pk + BA)).then_inc(lru_a, 1)
                e.activation(halves(ig[:, :]), psM[:, 2:4, 0:H], ACT.Sigmoid, bias=col(par, pk + BX)).then_inc(lru_a, 1)
                e.wait_ge(lru_a, n.now(lru_a, A_R))
                e.activation(tau[:, :], rg[:, :], ACT.Tanh, scale=col(sp8, k)).then_inc(lru_a, 1)
                e.activation(aa[:, :], rg[:, :], ACT.Exp, scale=col(nsp8, k)).then_inc(lru_a, 1)
                e.wait_ge(lru_a, n.now(lru_a, A_TAU))
                e.activation(l1[:, :], tau[:, :], ACT.Ln, scale=2.0, bias=tinyc[:, :]).then_inc(lru_a, 1)
                e.activation(l2[:, :], tau[:, :], ACT.Ln, bias=1.0).then_inc(lru_a, 1)
                split_hi(0, D)
                e.wait_ge(lru_v, n.now(lru_v, V_D))
                e.activation(l1[:, :], l1[:, :], ACT.Exp, scale=0.5).then_inc(lru_a, 1)
                e.wait_ge(out_taken[1], yl_taken)
                n.pause()
                e.activation(tile(lruo, i), tile(lruo, i), ACT.Gelu_apprx_tanh).then_inc(lru_a, 1)
                n.up(lru_v, LRU_TILE["lru_v"]), n.up(lru_a, LRU_TILE["lru_a"])
                n.up(sq_used)
                done(1, D)
            done(0, D)
            e.wait_ge(logit_ready, n.up(logit_ready))
            for pr in range(PR):
                ins = e.activation(halves(oT[:, pr, :]), psM[:, 2 * pr:2 * pr + 2, 0:H], ACT.Abs, bias=col(par, l * NPAR + (GB + pr)))
            ins.then_inc(gk_a, 1)
            done(1, D)
            e.wait_ge(gk_a, n.up(gk_a))
            e.activation(oT[:, 0:PR, :], oT[:, 0:PR, :], ACT.Exp, scale=-1.0).then_inc(gk_a, 1)
            e.wait_ge(gk_a, n.up(gk_a))
            e.activation(oT[:, 0:PR, :], oT[:, 0:PR, :], ACT.Ln, bias=1.0).then_inc(gk_a, 1)
            n.up(gk_a)
            done(0, D)
            factors(0, C, 5)
            n.up(gk_v, 4), n.up(unit_done[1])
            e.wait_ge(out_taken[1], n.up(out_taken[1]))
            e.activation(eb[:, :, :], bc[:, :, :], ACT.Exp).then_inc(eb_ready, 1)
            n.up(eb_ready)
            copy_v(0, C, 5)
            split_hi(1, D)
            e.activation(gT[:, :, :], gT[:, :, :], ACT.Silu)
            with n.loop(e, NC_ - 1, CHUNK) as c:
                chunk(c * C, C, CHUNK, ((c + 1) * C, C, 5))
            chunk(SEQ - C, C, CHUNK, (SEQ, NB * NS, 1))
            chunk(SEQ, NB * NS, SAMPLE)
            e.wait_ge(gla_a, n.now(gla_a))
            e.activation(vT[:, :, :], oT[:, :, :], ACT.Square).then_inc(head_sq, 1)
            e.wait_ge(mix_cols, n.up(mix_cols))
            root(5 * NTC, psU[:, 3, :])
            for k in range(DT):
                e.wait_ge(mix_v, n.up(mix_v, 2))
                e.activation(hh[:, k, :], (l1, l2)[k % 2][:, :], ACT.Copy).then_inc(hh_ready, 1)
            result(D, D)

        e.wait_ge(par_landed, 16)
        e.wait_ge(setup_p, 1)
        lam = par[:, :].rearrange("p (l k) -> p l k", l=L)[:, :, LAM:LAM + LT]
        t = [spt[:, k, :].rearrange("p (l k) -> p l k", l=L) for k in range(6)]
        e.activation(t[0], lam, ACT.Abs).then_inc(setup_a, 1)
        e.wait_ge(setup_a, 1)
        e.activation(t[1], t[0], ACT.Exp, scale=-1.0).then_inc(setup_a, 1)
        e.wait_ge(setup_v, 2)
        e.activation(t[3], t[2], ACT.Ln).then_inc(setup_a, 1)
        e.wait_ge(setup_v, 9)
        with n.loop(e, L, LAYER) as l:
            split_hi(0, D)
            split_hi(1, D)
            ffn(l, 0, D)
            mixer(l)
            ffn(l, 2, 0)

    @block.vector
    def _(e):
        n = Tally(lambda k: e.tensor_copy(spare[32:33, k:k + 1], ones[32:33, 0:1]))

        def split_lo(s, width):
            if width:
                e.wait_ge(hi_ready[s], n.up(hi_ready[s]))
                e.tensor_tensor(wl[s][:, 0:width], raw[s][:, 0:width], wh[s][:, 0:width].bitcast(F32), ALU.subtract)\
                    .then_inc(lo_ready[s], 1)

        def psum(s):
            return psU[:, 2 * s:2 * s + 2, 0:H]

        def product_done(s):
            e.wait_ge(unit_done[s], n.up(unit_done[s]))
            n.up(out_taken[s])

        def inverse(cols):
            e.wait_ge(std_ready, n.up(std_ready))
            e.reciprocal(dinv[0:TC, 0:cols], dcol[0:TC, 0:cols]).then_inc(inv_ready, 1)
            e.wait_ge(inv_ready, n.up(inv_ready))

        def diagonals(out, at):
            return e.tensor_tensor(out[0:TC, :, :], ident[0:TC, 0:TC].unsqueeze(1).broadcast_to([TC, NTC, TC]),
                                   dinv[0:TC, at:at + NTC].unsqueeze(2).broadcast_to([TC, NTC, TC]), ALU.mult)

        def lo_part(l, stage, m):
            e.wait_ge(hh_ready, n.up(hh_ready))
            e.scalar_tensor_tensor(tile(hl, m), tile(xT, m), col(par, l * NPAR + (PRE + stage * DT) + m),
                                   tile(hh, m).bitcast(F32), ALU.mult, ALU.subtract).then_inc(hl_ready, 1)
            n.up(hl_ready)

        def rms(width=0, gate_rank=False):
            inverse(NTC)
            diagonals(diag[0], 0).then_inc(diag_ready, 1)
            split_lo(1, width)
            if gate_rank:
                e.wait_ge(gdh_ready, n.up(gdh_ready))
                e.tensor_tensor(wgdl[:, :], wgd[:, :], wgdh[:, :].bitcast(F32), ALU.subtract).then_inc(gdl_ready, 1)
            e.wait_ge(bcast_ready, n.up(bcast_ready))

        def keep_rms():
            e.tensor_copy(halves(rstd[:, :]), psM[:, 1:3, 0:H]).then_inc(rstd_ready, 1)
            e.wait_ge(rstd_ready, n.up(rstd_ready))

        def residual(l, stage, following):
            rms(D if following else 0, gate_rank=(stage == 0))
            n.pause()

            def scale(i):
                e.wait_ge(x_ready, n.now(x_ready))
                n.up(x_ready, 2)
                for s in (0, 1):
                    e.tensor_tensor(halves(tmp[s][:, :]), halves(tile(yT, i * 2 + s)), psM[:, 1:3, 0:H], ALU.mult).then_inc(xpart, 1)

            def add(i):
                for s in (0, 1):
                    e.wait_ge(xpart, n.up(xpart))
                    e.scalar_tensor_tensor(tile(xT, i * 2 + s), tmp[s][:, :], col(ph, l * 24 + stage * DT + i * 2 + s),
                                           tile(xT, i * 2 + s), ALU.mult, ALU.add).then_inc(x_ready, 1)
            scale(0)
            add(0)
            with n.loop(e, DT // 2 - 1, TILES) as i:
                scale(i + 1)
                if following:
                    lo_part(l, stage + 1, i * 2)
                    lo_part(l, stage + 1, i * 2 + 1)
                add(i + 1)
            if following:
                lo_part(l, stage + 1, DT - 2)
                lo_part(l, stage + 1, DT - 1)

        def take(s, out, scale=None):
            product_done(s)
            if scale is None:
                e.tensor_tensor(halves(out), psum(s), halves(rstd[:, :]), ALU.mult).then_inc(out_taken[s], 1)
            else:
                e.scalar_tensor_tensor(halves(out), psum(s), scale, halves(rstd[:, :]), ALU.mult, ALU.mult).then_inc(out_taken[s], 1)

        def ffn(l, stage, after):
            def hidden_tile(j, width):
                e.wait_ge(silur_ready, n.up(silur_ready))
                product_done(1)
                e.tensor_tensor(halves(hid[:, :]), psum(1), halves(actr[:, :]), ALU.mult).then_inc(out_taken[1], 1)
                split_lo(1, width)
            product_done(0)
            e.tensor_copy(halves(tmp[0][:, :]), psum(0)).then_inc(out_taken[0], 1)
            split_lo(0, D)
            inverse(NTC)
            diagonals(diag[0], 0).then_inc(diag_ready, 1)
            e.wait_ge(bcast_ready, n.up(bcast_ready))
            keep_rms()
            e.tensor_tensor(gate[:, :], tmp[0][:, :], rstd[:, :], ALU.mult).then_inc(gate_ready, 1)
            hidden_tile(0, D)
            for c in range(CH):
                def body(j, width):
                    take(0, gate[:, :])
                    split_lo(0, width)
                    hidden_tile(j, width)
                with n.loop(e, FC - 1 - (c == 0), HIDDEN) as j:
                    body(j, D)
                body(0, FC * P)

                def down(i, after, last=False):
                    for s in (0, 1):
                        product_done(s)
                        y = halves(tile(yT, i * 2 + s))
                        if c == 0:
                            e.tensor_copy(y, psum(s)).then_inc(out_taken[s], 1)
                        else:
                            e.tensor_tensor(y, psum(s), y, ALU.add).then_inc(out_taken[s], 1)
                        if s == 0 or not (c == CH - 1 and last):
                            split_lo(s, after)
                with n.loop(e, DT // 2 - 1, PAIR) as i:
                    down(i, FC * P)
                down(DT // 2 - 1, D if c < CH - 1 else after, True)

        def lru_tile(l, i):
            k = l * LT + i
            pk = l * NPAR + i

            product_done(0)
            e.wait_ge(lru_p, n.now(lru_p))
            e.tensor_tensor(xlp[:, CW - 1:CW - 1 + H], psU[:, 0, 0:H], rstd[:, 0:H], ALU.mult)
            e.tensor_tensor(xlp[:, CW - 1 + H:XP], psU[:, 1, 0:SEQ - H], rstd[:, H:SEQ], ALU.mult)
            e.tensor_tensor(xls[:, :, CW - 1:XS], psU[:, 1, SEQ - H:H].rearrange("p (b t) -> p b t", t=NS),
                            rstd[:, SEQ:NT].rearrange("p (b t) -> p b t", t=NS), ALU.mult).then_inc(out_taken[0], 1)
            e.wait_ge(out_taken[0], n.now(out_taken[0]))
            e.wait_ge(lru_p, n.now(lru_p, P_HEAD))
            W = XA - CW + 1
            e.tensor_scalar(cv[0][:, :], xlp[:, 0:W], col(par, pk + CONVW), col(par, pk + CONVB), ALU.mult, ALU.add).then_inc(lru_v, 1)
            e.wait_ge(lru_v, n.now(lru_v, 1))
            e.scalar_tensor_tensor(cv[1][:, :], xlp[:, 1:1 + W], col(par, pk + (CONVW + LT)), cv[0][:, :], ALU.mult, ALU.add).then_inc(lru_v, 1)
            e.wait_ge(lru_v, n.now(lru_v, 2))
            e.scalar_tensor_tensor(cv[0][:, :], xlp[:, 2:2 + W], col(par, pk + (CONVW + 2 * LT)), cv[1][:, :], ALU.mult, ALU.add).then_inc(lru_v, 1)
            e.wait_ge(lru_v, n.now(lru_v, 3))
            w3 = col(par, pk + (CONVW + 3 * LT))
            e.scalar_tensor_tensor(xc[:, 0:SEQ], xlp[:, 3:3 + SEQ], w3, cv[0][:, 0:SEQ], ALU.mult, ALU.add)
            e.scalar_tensor_tensor(xc[:, SEQ:NT].rearrange("p (b t) -> p b t", t=NS), xls[:, :, CW - 1:XS], w3,
                                   starts_of(cv[0], XP, XS, NS), ALU.mult, ALU.add).then_inc(lru_v, 1)
            split_lo(0, D)
            take(1, tile(lruo, i))
            split_lo(1, D)
            take(0, tile(qkv, i * 2), col(qkvs, i * 2))
            e.wait_ge(lru_a, n.now(lru_a, A_L2))
            e.tensor_tensor(l1[:, :], l1[:, :], l2[:, :], ALU.subtract).then_inc(lru_v, 1)
            split_lo(0, D)
            e.wait_ge(lru_a, n.now(lru_a, A_M))
            e.memset(l1[:, 0:1], 1.0).then_inc(lru_v, 1)
            e.wait_ge(lru_v, n.now(lru_v, V_ONE))
            e.wait_ge(lru_p, n.now(lru_p, P_IX))
            e.tensor_tensor(l2[:, :], l1[:, :], ig[:, :], ALU.mult).then_inc(lru_v, 1)
            first = [t[:, SEQ:NT].rearrange("p (b t) -> p b t", t=NS)[:, :, 0] for t in (aa, l2)]
            e.tensor_tensor(cv[1][:, 0:NB], first[0], tile(sth, k), ALU.mult).then_inc(lru_v, 1)
            e.wait_ge(lru_v, n.now(lru_v, V_AH))
            e.tensor_tensor(first[1], first[1], cv[1][:, 0:NB], ALU.add).then_inc(lru_v, 1)
            e.memset(first[0], 0.0).then_inc(lru_v, 1)
            e.wait_ge(lru_v, n.now(lru_v, V_A0))
            e.tensor_tensor_scan(tau[:, :], aa[:, :], l2[:, :], 0.0, ALU.mult, ALU.add).then_inc(lru_v, 1)
            e.wait_ge(lru_v, n.now(lru_v, V_H))
            e.wait_ge(lru_a, n.now(lru_a, A_GE))
            e.tensor_tensor(tile(lruo, i), tau[:, :], tile(lruo, i), ALU.mult).then_inc(lru_v, 1)
            take(1, tile(qkv, i * 2 + 1), col(qkvs, i * 2 + 1))
            split_lo(1, D)
            n.up(lru_v, LRU_TILE["lru_v"]), n.up(lru_a, LRU_TILE["lru_a"]), n.up(lru_p, LRU_TILE["lru_p"])

        def starts_of(t, at, period, width):
            whole = t[:, at:at + (NB - 1) * period + width]
            return bass.AP(whole.tensor, whole.offset, [list(whole.ap[0]), [period, NB], [1, width]])

        def exponents(t0, T, nl):
            def about(slot, width, ref):
                b = bc[:, :, bass.ds(t0, T)].rearrange("p r (b m) -> p r b m", m=width)
                return e.tensor_tensor(dec[:, :, slot, 0:T].rearrange("p r (b m) -> p r b m", m=width), b,
                                       b[:, :, :, ref:ref + 1].broadcast_to([P, PR, T // width, width]), ALU.subtract)
            span = NS if nl == 1 else T
            about(0, 4, 1)
            about(nl + 2, span, span - 1)
            for v, m in enumerate(LEVELS[:nl]):
                ins = about(1 + v, 2 * m, m - 1)
            ins.then_inc(dec_v, 1)
            e.wait_ge(dec_v, n.up(dec_v))
            lv = dec[:, :, 1:1 + nl, 0:T]
            e.tensor_tensor(lv, lv, sign[:, 0:nl, 0:T].unsqueeze(1).broadcast_to([P, PR, nl, T]), ALU.mult).then_inc(dec_v, 1)
            n.up(dec_v)

        def keys(t0, T, nl):
            e.wait_ge(dec_a, n.now(dec_a, D_E))
            n.up(dec_a, D_VC)
            e.tensor_tensor(kf[:, :, 0:nl + 2, 0:T], dec[:, :, 1:nl + 3, 0:T],
                            qk[:, PR:2 * PR, bass.ds(t0, T)].unsqueeze(2).broadcast_to([P, PR, nl + 2, T]), ALU.mult)\
                .then_inc(keys_ready, 1)
            n.up(keys_ready), n.up(queries_ready, 2)

        def chunk(t0, T, nl, up, following=None):
            sample = up is SAMPLE
            if following:
                e.wait_ge(queries_ready, n.now(queries_ready, -1))
                e.wait_ge(keys_ready, n.now(keys_ready))
                exponents(*following)
            out = scs if sample else sc

            def place(m, data, mask):
                def blocks(t):
                    return t.rearrange("p h (b m) -> p h b m", m=m)
                o = out[0:T, :, 0:T].rearrange("p h (b m) -> p h b m", m=2 * m)[:, :, :, m:2 * m]
                e.copy_predicated(o, blocks(mask.unsqueeze(1).broadcast_to([T, HEADS, T // 2])), blocks(data)).then_inc(placed, 1)
                e.wait_ge(placed, n.up(placed))
                n.pause()
            e.wait_ge(gla_t, n.now(gla_t, T_SA))
            n.pause()
            banks = [psM[0:T, 2 * g:2 * g + 2, :].rearrange("p o (r x) -> p (o r) x", r=PR) for g in (0, 1)]
            for v, m in enumerate(LEVELS[:min(nl, 4)]):
                place(m, banks[1][:, :, v * (T // 2):(v + 1) * (T // 2)], masks[0:T, v, 0:T // 2])
            e.wait_ge(gla_t, n.now(gla_t, T_SB))
            n.pause()
            if nl == 5:
                place(LEVELS[4], banks[0][:, :, T:T + T // 2], masks[0:T, 4, 0:T // 2])
            e.copy_predicated(out[0:T, :, 0:T], masks[0:T, 5, 0:T].unsqueeze(1).broadcast_to([T, HEADS, T]),
                              banks[0][:, :, 0:T]).then_inc(gla_v, 1)
            if following:
                keys(*following)
            if not sample:
                e.wait_ge(gla_t, n.now(gla_t, T_SU))
                for pr in range(PR):
                    ins = e.scalar_tensor_tensor(S[:, pr, :], S[:, pr, :], eb[:, pr, bass.ds(t0 + T - 1, 1)], psU[:, 2, pr * DV:(pr + 1) * DV],
                                                 ALU.mult, ALU.add)
                ins.then_inc(gla_v, 1)
            else:
                e.wait_ge(gla_a, n.now(gla_a, A_KET))
                e.wait_ge(queries_ready, n.now(queries_ready))
                e.tensor_tensor(kem[:, :, :], ket[0:T, :].unsqueeze(1).broadcast_to([T, NB, PR * P]),
                                seqmask[:, :].unsqueeze(2).broadcast_to([T, NB, PR * P]), ALU.mult).then_inc(gla_v, 1)
                e.wait_ge(gla_t, n.now(gla_t, T_O))
                last = eb[:, :, SEQ:NT].rearrange("p r (b t) -> p b r t", t=NS)[:, :, :, NS - 1:NS]
                e.tensor_tensor(S0[:, :, :, :], S0[:, :, :, :], last.broadcast_to([P, NB, PR, DV]), ALU.mult).then_inc(gla_v, 1)
                e.wait_ge(gla_v, n.now(gla_v, G_S1))
                e.wait_ge(gla_t, n.now(gla_t, T_SU))
                s0 = S0[:, :, :, :].rearrange("p b r v -> p (b r v)")
                e.tensor_tensor(s0, s0, psM[:, :, :].rearrange("p o n -> p (o n)"), ALU.add).then_inc(gla_v, 1)
            for t in (gla_v, gla_a, gla_t):
                n.up(t, up[t.name])

        def mixer(l):
            e.wait_ge(gdp_ready, n.up(gdp_ready))
            n.up(out_taken[1])
            e.tensor_copy(halves(tmp[0][0:RANK, :]), psU[0:RANK, 2:4, 0:H]).then_inc(out_taken[1], 1)
            rms()
            keep_rms()
            e.tensor_tensor(gd[:, :], tmp[0][0:RANK, :], rstd[0:RANK, :], ALU.mult)
            with n.loop(e, LT, LRU_TILE) as i:
                lru_tile(l, i)
            e.wait_ge(logit_ready, n.up(logit_ready))
            e.wait_ge(gk_a, n.up(gk_a))
            for pr in range(PR):
                ins = e.tensor_scalar(halves(oT[:, PR + pr, :]), psM[:, 2 * pr:2 * pr + 2, 0:H],
                                      col(par, l * NPAR + (GB + pr)), 0.0, ALU.add, ALU.min)
            ins.then_inc(gk_v, 1)
            take(0, gT[:, 0, :])
            split_lo(0, D)
            take(1, gT[:, 1, :])
            split_lo(1, D)
            e.wait_ge(gk_v, n.up(gk_v))
            e.wait_ge(gk_a, n.up(gk_a, 2))
            g = oT[:, PR:2 * PR, :]
            e.tensor_tensor(g, g, oT[:, 0:PR, :], ALU.subtract).then_inc(gk_v, 1)
            e.wait_ge(gk_v, n.up(gk_v))
            e.tensor_scalar(g, g, 1.0 / NORMALIZER, GK_MIN, ALU.mult, ALU.max).then_inc(gk_v, 1)
            e.wait_ge(gk_v, n.up(gk_v))
            for pr in range(PR):
                ins = e.tensor_tensor_scan(bc[:, pr, :], cont[:, :], oT[:, PR + pr, :], 0.0, ALU.mult, ALU.add)
            ins.then_inc(gk_v, 1)
            e.wait_ge(gk_v, n.up(gk_v))
            e.wait_ge(lru_p, n.now(lru_p))
            e.wait_ge(lru_a, n.now(lru_a))
            exponents(0, C, 5)
            take(0, gT[:, 2, :])
            split_lo(0, D)
            take(1, gT[:, 3, :])
            e.wait_ge(gk_v, n.now(gk_v))
            e.wait_ge(s_zero, n.up(s_zero))
            keys(0, C, 5)
            split_lo(1, D)
            with n.loop(e, NC_ - 1, CHUNK) as c:
                chunk(c * C, C, 5, CHUNK, ((c + 1) * C, C, 5))
            chunk(SEQ - C, C, 5, CHUNK, (SEQ, NB * NS, 1))
            chunk(SEQ, NB * NS, 1, SAMPLE)
            inverse(5 * NTC)
            diagonals(diag[0], 0).then_inc(mix_d, 1)
            diagonals(diag[1], NTC).then_inc(mix_d, 1)
            k = 0
            for g in range(5):
                e.wait_ge(mix_t, n.up(mix_t))
                for src in ([lruo[:, i, :] for i in range(LT)] if g == 0 else [oT[:, g - 1, :]]):
                    val = (l1, l2)[k % 2]
                    e.tensor_tensor(halves(tmp[k % 2][:, :]), halves(src), psM[:, 2 * (g % 2):2 * (g % 2) + 2, 0:H], ALU.mult)\
                        .then_inc(mix_v, 1)
                    e.wait_ge(mix_v, n.up(mix_v))
                    if k >= 2:
                        e.wait_ge(hl_ready, n.now(hl_ready, k - 1))
                    if g == 0:
                        ins = e.tensor_scalar(val[:, :], tmp[k % 2][:, :], col(par, l * NPAR + (LNORM + k)), None, ALU.mult)
                    else:
                        ins = e.scalar_tensor_tensor(val[:, :], tmp[k % 2][:, :], col(par, l * NPAR + GNORM), gT[:, g - 1, :],
                                                     ALU.mult, ALU.mult)
                    ins.then_inc(mix_v, 1)
                    n.up(mix_v)
                    k += 1
                if g < 3:
                    diagonals(diag[g % 2], (g + 2) * NTC).then_inc(mix_d, 1)
            n.up(hh_ready, DT), n.up(hl_ready, DT)
            e.wait_ge(s_stored, n.up(s_stored, 32))

            def out(i, after, last=False):
                for s in (0, 1):
                    product_done(s)
                    e.tensor_copy(halves(tile(yT, i * 2 + s)), psum(s)).then_inc(out_taken[s], 1)
                    if not (last and s == 1):
                        split_lo(s, after)
            n.pause()
            with n.loop(e, DT // 2 - 1, PAIR) as i:
                out(i, D)
            out(DT // 2 - 1, D, True)

        e.wait_ge(par_landed, 16)
        e.wait_ge(setup_p, 1)
        for l in range(L):
            for s, f in enumerate((0.5, 1.0, 0.5)):
                at = l * NPAR + POST + s * DT
                ins = e.tensor_scalar(ph[:, l * 24 + s * DT:l * 24 + (s + 1) * DT], par[:, at:at + DT], f, None, ALU.mult)
        ins.then_inc(setup_v, 1)
        lam = par[:, :].rearrange("p (l k) -> p l k", l=L)[:, :, LAM:LAM + LT]
        t = [spt[:, k, :].rearrange("p (l k) -> p l k", l=L) for k in range(6)]
        made = 1

        def then(ins):
            nonlocal made
            made += 1
            ins.then_inc(setup_v, 1)
            e.wait_ge(setup_v, made)
        e.wait_ge(setup_a, 2)
        then(e.tensor_scalar(t[2], t[1], 1.0, None, ALU.add))
        then(e.scalar_tensor_tensor(t[1], t[2], -1.0, t[1], ALU.add, ALU.subtract))
        then(e.reciprocal(t[4], t[2]))
        then(e.tensor_tensor(t[1], t[1], t[4], ALU.mult))
        then(e.tensor_scalar(t[5], lam, -1.0, 0.0, ALU.mult, ALU.max))
        e.wait_ge(setup_a, 3)
        then(e.tensor_tensor(t[3], t[3], t[1], ALU.subtract))
        then(e.tensor_tensor(t[3], t[3], t[5], ALU.add))
        e.tensor_scalar(sp8[:, :], spt[:, 3, :], LRU_C, None, ALU.mult)
        then(e.tensor_scalar(nsp8[:, :], spt[:, 3, :], -LRU_C, None, ALU.mult))
        for m in range(DT):
            e.wait_ge(x_landed[m], 16)
            e.tensor_copy(xT[:, m, :], yT[:, m, :]).then_inc(x_ready, 1)
            n.up(x_ready)
        e.wait_ge(const_landed, 16 * 7)
        e.tensor_copy(masks[:, :, :], maskf)
        with n.loop(e, L, LAYER) as l:
            split_lo(0, D)
            split_lo(1, D)
            with n.loop(e, DT, {k: v // 2 for k, v in TILES.items()}) as m:
                lo_part(l, 0, m)
            ffn(l, 0, D)
            residual(l, 0, True)
            mixer(l)
            residual(l, 1, True)
            ffn(l, 2, 0)
            residual(l, 2, False)

    @block.gpsimd
    def _(e):
        n = Tally(lambda k: e.tensor_tensor(spare[:, 32 + k:33 + k], ones[:, 0:1], ones[:, 1:2], ALU.mult))

        def add_squares(s):
            e.wait_ge(sq_ready, n.up(sq_ready))
            e.wait_ge(sq_used, n.now(sq_used))
            n.up(sq_used)
            e.tensor_tensor(ssum[:, :], ssum[:, :], sq[s][:, :], ALU.add).then_inc(sq_used, 1)

        def clear(ready):
            e.wait_ge(ready, n.up(ready))
            n.pause()
            e.memset(ssum[:, :], 0.0).then_inc(ssum_zero, 1)

        def statistics():
            e.wait_ge(ssum_zero, n.up(ssum_zero))
            n.pause()
            with n.loop(e, DT // 2 - 1, SQUARED):
                add_squares(0)
                add_squares(1)
            add_squares(0)
            n.up(sq_ready), n.up(sq_used)
            clear(cols_ready)

        def ffn():
            statistics()
            n.up(hh_ready, DT)
            for c in range(CH):
                with n.loop(e, FC, HIDDEN) as j:
                    e.wait_ge(silu_ready, n.up(silu_ready))
                    e.tensor_tensor(actr[:, :], act[:, :], rstd[:, :], ALU.mult).then_inc(silur_ready, 1)
                    e.wait_ge(hidh_ready, n.up(hidh_ready))
                    e.tensor_tensor(tile(hidl, j), hid[:, :], tile(hidh, j).bitcast(F32), ALU.subtract).then_inc(hidl_ready, 1)
            statistics()

        def queries(t0, T, nl, before=0):
            if before:
                e.wait_ge(gla_t, n.now(gla_t, T_SB))
            e.wait_ge(dec_a, n.now(dec_a, D_E))
            n.up(dec_a, D_VC)
            q = qk[:, 0:PR, bass.ds(t0, T)]
            e.tensor_tensor(qf[:, :, 0:nl + 1, 0:T], dec[:, :, 0:nl + 1, 0:T],
                            q.unsqueeze(2).broadcast_to([P, PR, nl + 1, T]), ALU.mult).then_inc(queries_ready, 1)
            if before:
                e.wait_ge(gla_t, n.now(gla_t, T_O))
            e.tensor_tensor(qe[:, :, 0:T], q, eb[:, :, bass.ds(t0, T)], ALU.mult).then_inc(queries_ready, 1)
            n.up(queries_ready, 2), n.up(gla_t, before)

        def mixer(l):
            statistics()
            n.up(hh_ready, DT)
            e.wait_ge(s_stored, n.now(s_stored))
            n.up(s_stored, 32)
            n.pause()
            e.memset(xlp[:, 0:CW - 1], 0.0)
            e.memset(S[:, :, :], 0.0).then_inc(s_zero, 1)
            e.wait_ge(ssum_zero, n.up(ssum_zero))
            n.pause()
            with n.loop(e, LT, LRU_TILE) as i:
                k = l * LT + i
                e.wait_ge(lru_v, n.now(lru_v))
                e.tensor_copy(xls[:, :, 0:CW - 1], stc[:, bass.ds(k, 1), :, :].rearrange("p o b t -> p (o b) t")).then_inc(lru_p, 1)
                e.wait_ge(lru_a, n.now(lru_a, A_I))
                e.tensor_tensor(ig[:, :], ig[:, :], xc[:, :], ALU.mult).then_inc(lru_p, 1)
                e.wait_ge(lru_v, n.now(lru_v, V_H))
                out = tile(state_out, k)
                e.tensor_copy(out[:, O_CP:O_CS], xlp[:, SEQ:XP])
                e.tensor_copy(out[:, O_CS:O_HP].rearrange("p (b t) -> p b t", t=CW - 1), xls[:, :, NS:XS])
                e.tensor_copy(out[:, O_HP:O_HS], tau[:, SEQ - 1:SEQ])
                e.tensor_copy(out[:, O_HS:NST], tau[:, SEQ:NT].rearrange("p (b t) -> p b t", t=NS)[:, :, NS - 1])\
                    .then_inc(lru_p, 1)
                e.wait_ge(lru_v, n.now(lru_v, V_O))
                e.tensor_tensor(sq[0][:, :], tile(lruo, i), tile(lruo, i), ALU.mult).then_inc(sq_ready, 1)
                add_squares(0)
                n.up(lru_v, LRU_TILE["lru_v"]), n.up(lru_a, LRU_TILE["lru_a"]), n.up(lru_p, LRU_TILE["lru_p"])
            e.wait_ge(eb_ready, n.up(eb_ready))
            queries(0, C, 5)
            with n.loop(e, NC_ - 1, CHUNK) as c:
                queries((c + 1) * C, C, 5, CHUNK["gla_t"])
            queries(SEQ, NB * NS, 1, CHUNK["gla_t"])
            n.up(gla_t, SAMPLE["gla_t"])
            clear(mix_cols)
            for k in range(DT):
                e.wait_ge(hh_ready, n.up(hh_ready))
                e.tensor_tensor(hl[:, k, :], (l1, l2)[k % 2][:, :], hh[:, k, :].bitcast(F32), ALU.subtract).then_inc(hl_ready, 1)
            statistics()

        e.memset(ones[:, :], 1.0)
        for k, width in enumerate((D, DL, DV)):
            e.memset(means[:, k:k + 1], 1.0 / width)
        e.memset(qkvs[:, 0:PR], DK ** -0.5)
        e.memset(qkvs[:, PR:], 1.0)
        e.memset(epsc[:, :], EPS)
        e.memset(tinyc[:, :], TINY)
        e.memset(sc[:, :, :], 0.0)
        e.memset(scs[:, :, :], 0.0)
        e.memset(ssum[:, :], 0.0).then_inc(ssum_zero, 1)
        e.memset(dcol[:, :], 1.0).then_inc(setup_p, 1)
        e.wait_ge(setup_p, 1)
        with n.loop(e, L, LAYER) as l:
            ffn()
            mixer(l)
            ffn()



def layouts(x_prompt, x_sample, state_lru_h, state_lru_conv, state_gla, norm_pre, norm_post, w_ffn_gate, w_ffn_up,
            w_ffn_down, w_in, conv_w, conv_b, lru_wa, lru_ba, lru_wx, lru_bx, lru_lambda, lru_norm, gla_w_gate,
            gla_b_gate, gla_norm, w_out):
    import numpy as np
    f = np.float32

    def units(w):
        *lead, K, N = w.shape
        w = w.reshape(*lead, K // P, P, N // P, P)
        k = len(lead)
        return w.transpose(*range(k), k + 2, k + 1, k, k + 3).reshape(*lead, N // P, P, K)

    def vec(v):
        return v.reshape(L, -1, P).transpose(2, 0, 1)

    x = np.concatenate([x_prompt.reshape(SEQ, D), x_sample.reshape(NB * NS, D)])
    gu = np.stack([units(w_ffn_gate), units(w_ffn_up)], axis=3)
    down = units(w_ffn_down.reshape(L, 2, CH, FC * P, D))
    wi = units(w_in[:, :, :20 * P])
    order = [t for i in range(LT) for t in (i, LT + i, 2 * LT + 2 * i, 2 * LT + 2 * i + 1)] + list(range(4 * LT, 20))
    gates = np.zeros((L, LT, P, 2, P), f)
    for g, w in enumerate((lru_wa, lru_wx)):
        for b in range(8):
            r = slice(64 * (b % 2), 64 * (b % 2) + 64)
            gates[:, b // 2, r, g, r] = w[:, b]
    par = np.concatenate([vec(norm_pre.reshape(L, -1)), vec(norm_post.reshape(L, -1)), vec(conv_w.reshape(L, -1)),
                          vec(conv_b), vec(lru_ba), vec(lru_bx), vec(lru_lambda), vec(lru_norm), vec(gla_b_gate),
                          vec(gla_norm)], axis=2)
    s, t = np.arange(C)[:, None], np.arange(C)[None, :]
    masks = np.zeros((P, 6, C), f)
    sign = np.zeros((P, len(LEVELS), C), f)
    for v, m in enumerate(LEVELS):
        ok = (s // (2 * m) == t // (2 * m)) & (s % (2 * m) < m) & (t % (2 * m) >= m)
        masks[:, v, :C // 2] = ok[:, (np.arange(C) % (2 * m)) >= m]
        sign[:, v, :] = np.where(t % (2 * m) >= m, 1.0, -1.0)
    masks[:, 5, :] = (s // 4 == t // 4) & (s <= t)
    cont = np.ones((P, NT), f)
    cont[:, 0:SEQ:C] = 0
    cont[:, SEQ:NT:NS] = 0
    return {
        "xT": x.reshape(NT, DT, P).transpose(2, 1, 0),
        "w_gu": gu.reshape(-1, P, D),
        "w_d": down.reshape(-1, P, FC * P),
        "w_in": wi[:, order].reshape(-1, P, D),
        "w_gd": w_in[:, :, 20 * P:].reshape(L, DT, P, RANK).transpose(0, 2, 1, 3).reshape(L, P, DT * RANK),
        "w_g2": gla_w_gate,
        "w_ax": gates.reshape(L * LT, P, 2 * P),
        "w_out": units(w_out).reshape(-1, P, D),
        "par": par.reshape(P, L * NPAR),
        "st_h": state_lru_h.reshape(L, NB, LT, P).transpose(3, 0, 2, 1).reshape(P, L * LT, NB),
        "st_conv": state_lru_conv.reshape(L, NB, CW - 1, LT, P).transpose(4, 0, 3, 1, 2).reshape(P, L * LT, NB, CW - 1),
        "st_gla": state_gla.reshape(L, NB, PR, P, DV).transpose(0, 3, 1, 2, 4),
        "ident": np.eye(P, dtype=f), "masks": masks, "sign": sign,
        "seqmask": np.repeat(np.eye(NB, dtype=f), NS, axis=0), "cont": cont,
    }


OUTPUTS = {"yT": (P, DT, NT), "states": (P, L * LT, NST), "gla_p": (L, P, PR, DV), "gla_s": (L, P, NB, PR, DV)}


def kernel(**inputs):
    import numpy as np
    import concourse.bacc as bacc
    from concourse.bass_utils import run_bass_kernel_spmd

    arrays = {f"in_{k}": np.ascontiguousarray(v) for k, v in layouts(**{k: np.asarray(v) for k, v in inputs.items()}).items()}
    nc = bacc.Bacc("TRN2", target_bir_lowering=False, num_devices=1)
    a = {k[3:]: nc.dram_tensor(k, v.shape, mybir.dt.from_np(v.dtype), kind="ExternalInput").ap() for k, v in arrays.items()}
    for k, shape in OUTPUTS.items():
        a[k] = nc.dram_tensor(f"out_{k}", shape, F32, kind="ExternalOutput").ap()
    build(nc, a)
    r = run_bass_kernel_spmd(nc, [arrays], core_ids=[0]).results[0]
    y = r["out_yT"].transpose(2, 1, 0).reshape(NT, D)
    st = r["out_states"].reshape(P, L, LT, NST).transpose(1, 3, 2, 0).reshape(L, NST, DL)
    return (y[:SEQ].reshape(1, SEQ, D), y[SEQ:].reshape(NB, NS, D),
            st[:, O_HP:O_HS], st[:, O_CP:O_CS].reshape(L, 1, CW - 1, DL),
            r["out_gla_p"].transpose(0, 2, 1, 3).reshape(L, 1, HEADS, DK, DV),
            st[:, O_HS:], st[:, O_CS:O_HP].reshape(L, NB, CW - 1, DL),
            r["out_gla_s"].transpose(0, 2, 3, 1, 4).reshape(L, NB, HEADS, DK, DV))
```
